# Optimizing a Trainium2 kernel written in Bass

```python
import jax, jax.numpy as jnp
from jax import lax
import numpy as np
import math

D_MODEL = 1024
BATCH = 1
SEQ = 1024
DEPTH = 2

GRID_W = 64
CTX_LEN = 256
CHUNK = 128
A_HEADS = 4
A_HEAD_DIM = 128
A_W = A_HEADS * A_HEAD_DIM
B_GROUPS = 4
B_GROUP_DIM = 128
B_W = B_GROUPS * B_GROUP_DIM
AB_IN = 3 * A_W + 2 * B_W
AB_OUT = A_W + B_W
C_HEADS = 16
C_KV_HEADS = 4
C_GROUP = C_HEADS // C_KV_HEADS
C_HEAD_DIM = 64
C_Q_W = C_HEADS * C_HEAD_DIM
C_KV_W = C_KV_HEADS * C_HEAD_DIM
C_IN = 2 * C_Q_W + 2 * C_KV_W
WINDOW = 128
Q_BLOCK = 128
ROPE_BASE = 10000.0
NORM_EPS = 1e-6
NEG_INF = -1e30
N_EVEN = (DEPTH + 1) // 2
N_ODD = DEPTH // 2


def rms_norm(x, g):
    xf = x.astype(jnp.float32)
    y = xf * lax.rsqrt(jnp.mean(xf * xf, axis=-1, keepdims=True) + NORM_EPS)
    return (y * g.astype(jnp.float32)).astype(x.dtype)

def layer_norm(x, g):
    xf = x.astype(jnp.float32)
    mu = jnp.mean(xf, axis=-1, keepdims=True)
    xc = xf - mu
    y = xc * lax.rsqrt(jnp.mean(xc * xc, axis=-1, keepdims=True) + NORM_EPS)
    return (y * g.astype(jnp.float32)).astype(x.dtype)

def adaln(cond, w, b):
    m = jax.nn.silu(cond) @ w + b
    return jnp.split(m, 3, axis=-1)

def rope_1d(x, pos):
    nf = x.shape[-1] // 2
    inv = ROPE_BASE ** (-jnp.arange(nf, dtype=jnp.float32) / nf)
    ang = pos.astype(jnp.float32)[:, None] * inv[None, :]
    cos = jnp.cos(ang)[None, :, None, :].astype(x.dtype)
    sin = jnp.sin(ang)[None, :, None, :].astype(x.dtype)
    x1, x2 = x[..., :nf], x[..., nf:]
    return jnp.concatenate([x1 * cos - x2 * sin, x2 * cos + x1 * sin], axis=-1)

def rope_2d(x, row, col):
    half = x.shape[-1] // 2
    return jnp.concatenate([rope_1d(x[..., :half], row), rope_1d(x[..., half:], col)], axis=-1)

def sink_softmax(scores, sink):
    s = jnp.broadcast_to(sink, scores.shape[:-1] + (1,))
    p = jax.nn.softmax(jnp.concatenate([s, scores], axis=-1), axis=-1)
    return p[..., 1:]

def mixer_ab(h, w_in, v_g, s_w, s_b, w_out):
    bsz, L, _ = h.shape
    z = h @ w_in
    u, v, g_a, x_b, g_b = jnp.split(z, [A_W, 2 * A_W, 3 * A_W, 3 * A_W + B_W], axis=-1)
    v = layer_norm(v, v_g).reshape(bsz, L // CHUNK, CHUNK, A_HEADS, A_HEAD_DIM)
    sv = jnp.einsum('bnphc,hqp->bnqhc', v, s_w) + s_b.T[:, :, None]
    y_a = u * sv.reshape(bsz, L, A_W) * jax.nn.silu(g_a)
    xb = x_b.reshape(bsz, L, B_GROUPS, B_GROUP_DIM).astype(jnp.float32)
    f = jnp.real(jnp.fft.fft2(xb, axes=(1, 3), norm='ortho')).astype(h.dtype).reshape(bsz, L, B_W)
    y_b = f * jax.nn.silu(g_b)
    return jnp.concatenate([y_a, y_b], axis=-1) @ w_out

def split_c(z):
    return jnp.split(z, [C_Q_W, C_Q_W + C_KV_W, C_Q_W + 2 * C_KV_W], axis=-1)

def window_attention(q, k, v, k_ctx, v_ctx, sink):
    bsz, S, _, hd = q.shape
    qg = q.reshape(bsz, S, C_KV_HEADS, C_GROUP, hd)
    pad = ((0, 0), (WINDOW, WINDOW), (0, 0), (0, 0))
    kp, vp = jnp.pad(k, pad), jnp.pad(v, pad)
    kb_len = Q_BLOCK + 2 * WINDOW
    scale = hd ** -0.5
    sink_b = sink.reshape(C_KV_HEADS, C_GROUP).astype(jnp.float32)[None, :, :, None, None]

    def one_block(n):
        start = n * Q_BLOCK
        qb = lax.dynamic_slice_in_dim(qg, start, Q_BLOCK, axis=1)
        kb = lax.dynamic_slice_in_dim(kp, start, kb_len, axis=1)
        vb = lax.dynamic_slice_in_dim(vp, start, kb_len, axis=1)
        qpos = start + jnp.arange(Q_BLOCK)
        kpos = start - WINDOW + jnp.arange(kb_len)
        valid = (jnp.abs(qpos[:, None] - kpos[None, :]) <= WINDOW) & (kpos[None, :] >= 0) & (kpos[None, :] < S)
        s_win = jnp.einsum('bqkgd,bjkd->bkgqj', qb, kb).astype(jnp.float32) * scale
        s_win = jnp.where(valid, s_win, NEG_INF)
        s_ctx = jnp.einsum('bqkgd,bjkd->bkgqj', qb, k_ctx).astype(jnp.float32) * scale
        p = sink_softmax(jnp.concatenate([s_ctx, s_win], axis=-1), sink_b)
        vals = jnp.concatenate([v_ctx, vb], axis=1)
        return jnp.einsum('bkgqj,bjkd->bqkgd', p.astype(v.dtype), vals)

    out = lax.map(one_block, jnp.arange(S // Q_BLOCK))
    return jnp.moveaxis(out, 0, 1).reshape(bsz, S, C_Q_W)

def context_attention(q, k, v, sink):
    bsz, L, _, hd = q.shape
    qg = q.reshape(bsz, L, C_KV_HEADS, C_GROUP, hd)
    s = jnp.einsum('bqkgd,bjkd->bkgqj', qg, k).astype(jnp.float32) * hd ** -0.5
    sink_b = sink.reshape(C_KV_HEADS, C_GROUP).astype(jnp.float32)[None, :, :, None, None]
    p = sink_softmax(s, sink_b)
    o = jnp.einsum('bkgqj,bjkd->bqkgd', p.astype(v.dtype), v)
    return o.reshape(bsz, L, C_Q_W)

def first_inputs(seed: int = 0) -> dict:
    key = jax.random.key(seed)
    ks = jax.random.split(key, 16)

    def nrm(k, shape, s):
        return jax.random.normal(k, shape, jnp.float32) * s

    return {
        'x': nrm(ks[0], (BATCH, SEQ, D_MODEL), 1.0),
        'c': nrm(ks[1], (BATCH, D_MODEL), 1.0),
        'ctx': nrm(ks[2], (BATCH, CTX_LEN, D_MODEL), 1.0),
        'c_ctx': nrm(ks[3], (D_MODEL,), 1.0),
        'norm_g': 1.0 + nrm(ks[4], (DEPTH, D_MODEL), 0.02),
        'ada_w': nrm(ks[5], (DEPTH, D_MODEL, 3 * D_MODEL), 0.5 * D_MODEL ** -0.5),
        'ada_b': nrm(ks[6], (DEPTH, 3 * D_MODEL), 0.02),
        'w_in_ab': nrm(ks[7], (N_EVEN, D_MODEL, AB_IN), D_MODEL ** -0.5),
        'v_norm_g': 1.0 + nrm(ks[8], (N_EVEN, A_W), 0.02),
        'spatial_w': nrm(ks[9], (N_EVEN, A_HEADS, CHUNK, CHUNK), CHUNK ** -0.5),
        'spatial_b': 1.0 + nrm(ks[10], (N_EVEN, A_HEADS, CHUNK), 0.02),
        'w_out_ab': nrm(ks[11], (N_EVEN, AB_OUT, D_MODEL), AB_OUT ** -0.5),
        'w_in_c': nrm(ks[12], (N_ODD, D_MODEL, C_IN), D_MODEL ** -0.5),
        'sink_logit': nrm(ks[13], (N_ODD, C_HEADS), 0.5),
        'w_out_c': nrm(ks[14], (N_ODD, C_Q_W, D_MODEL), C_Q_W ** -0.5),
        'final_g': 1.0 + nrm(ks[15], (D_MODEL,), 0.02),
    }

def first_block(x, c, ctx, c_ctx, norm_g, ada_w, ada_b, w_in_ab, v_norm_g, spatial_w, spatial_b,
              w_out_ab, w_in_c, sink_logit, w_out_c, final_g):
    bsz, S, _ = x.shape
    rows = S // GRID_W
    row = jnp.repeat(jnp.arange(rows), GRID_W)
    col = jnp.tile(jnp.arange(GRID_W), rows)

    for layer in range(DEPTH):
        need_ctx_out = layer < DEPTH - 1
        shift, scale, gate = adaln(c[:, None, :], ada_w[layer], ada_b[layer])
        shift_c, scale_c, gate_c = adaln(c_ctx, ada_w[layer], ada_b[layer])
        h = rms_norm(x, norm_g[layer]) * (1.0 + scale) + shift
        if layer % 2 == 0:
            i = layer // 2
            y = mixer_ab(h, w_in_ab[i], v_norm_g[i], spatial_w[i], spatial_b[i], w_out_ab[i])
            if need_ctx_out:
                hc = rms_norm(ctx, norm_g[layer]) * (1.0 + scale_c) + shift_c
                yc = mixer_ab(hc, w_in_ab[i], v_norm_g[i], spatial_w[i], spatial_b[i], w_out_ab[i])
                ctx = ctx + gate_c * yc
            x = x + gate * y
        else:
            i = layer // 2
            w_in = w_in_c[i]
            hc = rms_norm(ctx, norm_g[layer]) * (1.0 + scale_c) + shift_c
            q, k, v, g = split_c(h @ w_in)
            q = rope_2d(q.reshape(bsz, S, C_HEADS, C_HEAD_DIM), row, col)
            k = rope_2d(k.reshape(bsz, S, C_KV_HEADS, C_HEAD_DIM), row, col)
            v = v.reshape(bsz, S, C_KV_HEADS, C_HEAD_DIM)
            Lc = ctx.shape[1]
            if need_ctx_out:
                q_c, k_c, v_c, g_c = split_c(hc @ w_in)
            else:
                k_c, v_c = jnp.split(hc @ w_in[:, C_Q_W:C_Q_W + 2 * C_KV_W], 2, axis=-1)
            k_c = k_c.reshape(bsz, Lc, C_KV_HEADS, C_HEAD_DIM)
            v_c = v_c.reshape(bsz, Lc, C_KV_HEADS, C_HEAD_DIM)
            o = window_attention(q, k, v, k_c, v_c, sink_logit[i])
            y = (o * jax.nn.silu(g)) @ w_out_c[i]
            if need_ctx_out:
                o_c = context_attention(q_c.reshape(bsz, Lc, C_HEADS, C_HEAD_DIM), k_c, v_c, sink_logit[i])
                ctx = ctx + gate_c * ((o_c * jax.nn.silu(g_c)) @ w_out_c[i])
            x = x + gate * y

    return rms_norm(x, final_g)


DEPTH_2 = 1

D_MIX = D_MODEL
ATTN_WIDTH = D_MIX // 2
HEAD_DIM = 64
N_HEADS = ATTN_WIDTH // HEAD_DIM
CONV_WIDTH = D_MIX - ATTN_WIDTH
CONV_GROUPS = CONV_WIDTH // HEAD_DIM
CONV_K = 31
D_IN = 3 * ATTN_WIDTH + N_HEADS + 2 * CONV_WIDTH
D_FF = int(math.ceil((8 * D_MODEL / 3) / 256) * 256)
N_MOD = 6
EPS = 1e-6


def rms_norm_2(x, g):
    xf = x.astype(jnp.float32)
    y = xf * lax.rsqrt(jnp.mean(xf * xf, axis=-1, keepdims=True) + EPS)
    return (y * g.astype(jnp.float32)).astype(x.dtype)

def layer_norm_2(x, g, b):
    xf = x.astype(jnp.float32)
    mu = jnp.mean(xf, axis=-1, keepdims=True)
    var = jnp.mean(jnp.square(xf - mu), axis=-1, keepdims=True)
    y = (xf - mu) * lax.rsqrt(var + EPS)
    return (y * g.astype(jnp.float32) + b.astype(jnp.float32)).astype(x.dtype)

def fox_attention(q, k, v, log_f):
    B, S, H, Dh = q.shape
    nb = S // Q_BLOCK
    scale = Dh ** -0.5
    cum = jnp.cumsum(log_f, axis=1)
    cum_k = jnp.transpose(cum, (0, 2, 1))[:, :, None, :]
    q_blocks = jnp.transpose(q.reshape(B, nb, Q_BLOCK, H, Dh), (1, 0, 2, 3, 4))
    c_blocks = jnp.transpose(cum.reshape(B, nb, Q_BLOCK, H), (1, 0, 3, 2))
    k_pos = jnp.arange(S, dtype=jnp.int32)

    def one_block(args):
        i, q_blk, c_blk = args
        s = jnp.einsum('bqhd,bkhd->bhqk', q_blk, k).astype(jnp.float32) * scale
        s = s + c_blk[..., None] - cum_k
        q_pos = i * Q_BLOCK + jnp.arange(Q_BLOCK, dtype=jnp.int32)
        mask = k_pos[None, :] <= q_pos[:, None]
        s = jnp.where(mask[None, None], s, -jnp.inf)
        p = jax.nn.softmax(s, axis=-1)
        return jnp.einsum('bhqk,bkhd->bqhd', p.astype(v.dtype), v)

    outs = lax.map(one_block, (jnp.arange(nb, dtype=jnp.int32), q_blocks, c_blocks))
    return jnp.transpose(outs, (1, 0, 2, 3, 4)).reshape(B, S, H * Dh)

def causal_depthwise_conv(u, w, b):
    C = u.shape[-1]
    out = lax.conv_general_dilated(
        u, w[:, None, :].astype(u.dtype), window_strides=(1,), padding=((CONV_K - 1, 0),),
        dimension_numbers=('NWC', 'WIO', 'NWC'), feature_group_count=C)
    return out + b.astype(u.dtype)

def hybrid_mixer(h, w_in, b_f, conv_w, conv_b, conv_ln_g, conv_ln_b, w_o):
    B, S, _ = h.shape
    proj = h @ w_in
    splits = [ATTN_WIDTH, 2 * ATTN_WIDTH, 3 * ATTN_WIDTH, 3 * ATTN_WIDTH + N_HEADS,
              3 * ATTN_WIDTH + N_HEADS + CONV_WIDTH]
    q, k, v, f_logit, conv_val, conv_gate = jnp.split(proj, splits, axis=-1)
    q = q.reshape(B, S, N_HEADS, HEAD_DIM)
    k = k.reshape(B, S, N_HEADS, HEAD_DIM)
    v = v.reshape(B, S, N_HEADS, HEAD_DIM)
    log_f = jax.nn.log_sigmoid((f_logit + b_f).astype(jnp.float32))
    attn = fox_attention(q, k, v, log_f)
    u = conv_val * jax.nn.sigmoid(conv_gate)
    u = causal_depthwise_conv(u, conv_w, conv_b)
    u = jax.nn.silu(layer_norm_2(u, conv_ln_g, conv_ln_b))
    return jnp.concatenate([attn, u], axis=-1) @ w_o

def swiglu_ffn(h, w_ffn_in, w_ffn_out):
    g, u = jnp.split(h @ w_ffn_in, 2, axis=-1)
    return (jax.nn.silu(g) * u) @ w_ffn_out

def second_inputs(seed: int = 0) -> dict:
    key = jax.random.key(seed)
    ks = jax.random.split(key, 24)
    f32 = jnp.float32
    L, D = DEPTH_2, D_MODEL

    def nrm(k, shape, s):
        return jax.random.normal(k, shape, f32) * s

    x = jax.random.normal(ks[0], (BATCH, SEQ, D), f32)
    c = jax.random.normal(ks[1], (BATCH, D), f32)
    w_in = jnp.concatenate([
        nrm(ks[2], (L, D, 3 * ATTN_WIDTH), D ** -0.5),
        nrm(ks[3], (L, D, N_HEADS), 0.5 * D ** -0.5),
        nrm(ks[4], (L, D, 2 * CONV_WIDTH), D ** -0.5),
    ], axis=-1)
    b_f = 2.5 + 0.5 * jax.random.normal(ks[5], (L, N_HEADS), f32)
    conv_w = nrm(ks[6], (L, CONV_K, CONV_WIDTH), CONV_K ** -0.5)
    conv_b = nrm(ks[7], (L, CONV_WIDTH), 0.01)
    conv_ln_g = 1.0 + nrm(ks[8], (L, CONV_WIDTH), 0.05)
    conv_ln_b = nrm(ks[9], (L, CONV_WIDTH), 0.01)
    w_o = nrm(ks[10], (L, D_MIX, D), D_MIX ** -0.5)
    w_ffn_in = nrm(ks[11], (L, D, 2 * D_FF), D ** -0.5)
    w_ffn_out = nrm(ks[12], (L, D_FF, D), D_FF ** -0.5)
    mix_pre_g = 1.0 + nrm(ks[13], (L, D), 0.05)
    mix_post_g = 1.0 + nrm(ks[14], (L, D), 0.05)
    ffn_pre_g = 1.0 + nrm(ks[15], (L, D), 0.05)
    ffn_post_g = 1.0 + nrm(ks[16], (L, D), 0.05)
    ada_w = nrm(ks[17], (L, D, N_MOD * D), 0.5 * D ** -0.5)
    ada_b = nrm(ks[18], (L, N_MOD * D), 0.01)
    return {"x": x, "c": c, "w_in": w_in, "b_f": b_f, "conv_w": conv_w, "conv_b": conv_b,
            "conv_ln_g": conv_ln_g, "conv_ln_b": conv_ln_b, "w_o": w_o,
            "w_ffn_in": w_ffn_in, "w_ffn_out": w_ffn_out,
            "mix_pre_g": mix_pre_g, "mix_post_g": mix_post_g,
            "ffn_pre_g": ffn_pre_g, "ffn_post_g": ffn_post_g,
            "ada_w": ada_w, "ada_b": ada_b}

def second_block(x, c, w_in, b_f, conv_w, conv_b, conv_ln_g, conv_ln_b, w_o,
              w_ffn_in, w_ffn_out, mix_pre_g, mix_post_g, ffn_pre_g, ffn_post_g,
              ada_w, ada_b):
    c_act = jax.nn.silu(c)
    for i in range(DEPTH_2):
        mod = c_act @ ada_w[i] + ada_b[i]
        sh1, sc1, g1, sh2, sc2, g2 = [m[:, None, :] for m in jnp.split(mod, N_MOD, axis=-1)]
        h = rms_norm_2(x, mix_pre_g[i]) * (1.0 + sc1) + sh1
        y = hybrid_mixer(h, w_in[i], b_f[i], conv_w[i], conv_b[i], conv_ln_g[i], conv_ln_b[i], w_o[i])
        x = x + g1 * rms_norm_2(y, mix_post_g[i])
        h = rms_norm_2(x, ffn_pre_g[i]) * (1.0 + sc2) + sh2
        y = swiglu_ffn(h, w_ffn_in[i], w_ffn_out[i])
        x = x + g2 * rms_norm_2(y, ffn_post_g[i])
    return x


def setup_inputs(seed=0):
    out = dict(first_inputs(seed))
    for name, value in second_inputs(seed + 1).items():
        if name != "x":
            out[name + "_2"] = value
    return out


def reference(
    x, c, ctx, c_ctx, norm_g, ada_w, ada_b, w_in_ab, v_norm_g, spatial_w, spatial_b, w_out_ab,
    w_in_c, sink_logit, w_out_c, final_g, c_2, w_in_2, b_f_2, conv_w_2, conv_b_2, conv_ln_g_2,
    conv_ln_b_2, w_o_2, w_ffn_in_2, w_ffn_out_2, mix_pre_g_2, mix_post_g_2, ffn_pre_g_2,
    ffn_post_g_2, ada_w_2, ada_b_2,
):
    x = first_block(
        x, c, ctx, c_ctx, norm_g, ada_w, ada_b, w_in_ab, v_norm_g, spatial_w, spatial_b,
        w_out_ab, w_in_c, sink_logit, w_out_c, final_g,
    )
    return second_block(
        x, c_2, w_in_2, b_f_2, conv_w_2, conv_b_2, conv_ln_g_2, conv_ln_b_2, w_o_2, w_ffn_in_2,
        w_ffn_out_2, mix_pre_g_2, mix_post_g_2, ffn_pre_g_2, ffn_post_g_2, ada_w_2, ada_b_2,
    )


_drawn_inputs = setup_inputs


def setup_inputs(seed=0):
    import zlib

    import numpy as np

    out = dict(_drawn_inputs(seed))
    spreads = {}
    factors = {'ctx': 4.029,
     'norm_g': 7.674,
     'ada_b': 2.875,
     'v_norm_g': 8.0,
     'spatial_b': 8.0,
     'sink_logit': 8.0,
     'final_g': 2.745,
     'conv_b_2': 40.727,
     'conv_ln_g_2': 16.024,
     'conv_ln_b_2': 64.0,
     'mix_pre_g_2': 3.199,
     'mix_post_g_2': 10.475,
     'ffn_pre_g_2': 3.107,
     'ffn_post_g_2': 12.303,
     'ada_b_2': 3.614}
    for name, (base, spread) in spreads.items():
        noise = np.random.default_rng([zlib.crc32(name.encode()), seed]).standard_normal(out[name].shape)
        drawn = base * np.exp(spread * noise) if base else spread * noise
        out[name] = __import__('jax').numpy.asarray(drawn.astype(out[name].dtype))
    for name, factor in factors.items():
        out[name] = (out[name] * factor).astype(out[name].dtype)
    return out
```

```python
import math
from contextlib import ExitStack

import numpy as np

import concourse.bass as bass
from concourse import mybir

F32 = mybir.dt.float32
F32R = mybir.dt.float32r
ALU = mybir.AluOpType
ACT = mybir.ActivationFunctionType
AX = mybir.AxisListType

P = 128
D = 1024
KT = D // P
T = 1024
C = 256
HALF = 512
NB_T = T // P
EPS = 1e-6
NEG = -1e30
SCALE = 0.125
HID = 2816
TAPS = 31
WSLOTS, RSLOTS = 8, 4
PARTS = {"h0": (0, 512), "h1": (512, 512), "c": (0, 256)}

ROWS = {}
_at = 0
for _name, _n in (("norm_g", 16), ("ada_b", 48), ("c", 8), ("c_ctx", 8), ("c_2", 8), ("v_norm_g", 4),
                  ("final_g", 8), ("conv_b_2", 4), ("conv_ln_g_2", 4), ("conv_ln_b_2", 4),
                  ("mix_pre_g_2", 8), ("mix_post_g_2", 8),
                  ("ffn_pre_g_2", 8), ("ffn_post_g_2", 8), ("ada_b_2", 48)):
    ROWS[_name] = (_at, _n)
    _at += _n
ROWS["conv_w_2"] = (256, TAPS * 4)


def shape_tables():
    k = np.arange(512)
    l = np.arange(512)
    s = 1.0 / math.sqrt(T * P)
    slots = []
    for odd in (0, 1):
        ang = 2 * np.pi * ((l[:, None] * (2 * k[None, :] + odd)) % T) / T
        cs, sn = np.cos(ang) * s, -np.sin(ang) * s
        for kt in range(4):
            slots += [cs[kt * P:(kt + 1) * P], sn[kt * P:(kt + 1) * P]]
    n = np.arange(C)
    ang = 2 * np.pi * ((n[:, None] * n[None, :]) % C) / C
    s = 1.0 / math.sqrt(C * P)
    both = np.concatenate([np.cos(ang) * s, -np.sin(ang) * s], axis=1)
    slots += [both[:P], both[P:]]
    n = np.arange(P)
    ang = 2 * np.pi * ((n[:, None] * n[None, :]) % P) / P
    chan = np.concatenate([np.cos(ang), np.sin(ang)], axis=1)
    inv = 10000.0 ** (-np.arange(16, dtype=np.float32) / 16)
    t = np.arange(T)
    pos = np.where((np.arange(P) % 64 < 32)[:, None], (t // 64)[None, :], (t % 64)[None, :]).astype(np.float32)
    ang = (pos * inv.astype(np.float32)[np.arange(P) % 16][:, None]).astype(np.float32).astype(np.float64)
    sign = np.where(np.arange(P) % 32 < 16, -1.0, 1.0)[:, None]
    q, m = np.arange(P)[:, None], np.arange(P)[None, :]
    left = np.where(m >= q, 0.0, -NEG)
    right = np.where(m <= q, 0.0, -NEG)
    f = np.float32
    return {
        "t_ident": np.eye(P, dtype=f),
        "t_dft": np.stack(slots).astype(f),
        "t_chan": chan.astype(f),
        "t_rope": np.stack([np.cos(ang), np.sin(ang) * sign], axis=1).astype(f),
        "t_mask": np.stack([left, right], axis=1).astype(f),
    }


def plan():
    tl, slots = [], []

    def slot(kind, src, job):
        slots.append((kind, src, job))
        return len(slots) - 1

    def lin(name, layer, group, part, ws, kts=KT, kind="lin", mid=None, last=False, h="H", **kw):
        tl.append(dict(kind=kind, name=name, layer=layer, group=group, part=part, ws=ws, kts=kts,
                       mid=mid, last=last, h=h, **kw))

    def weights(layer, group, kts=KT):
        return [slot("split", (layer, group, k), None) for k in range(kts)]

    def ada(v):
        ws = [slot("raw", ("ada", v, k, n), None) for k in range(KT) for n in range(2)]
        tl.append(dict(kind="ada", name=("ada", v), v=v, ws=ws))
        tl.append(dict(kind="adac", name=("adac", v), v=v))

    def ev(kind, name, **kw):
        tl.append(dict(kind=kind, name=name, **kw))

    def adav(v, n=None):
        halves = (n,) if n is not None else (0, 1)
        ws = [slot("raw", ("ada", v, k, x), None) for k in range(KT) for x in halves]
        ev("adav", ("adav", v, n), v=v, n=n, ws=ws)

    ev("params", "params")
    for k in range(KT):
        ev("tx", ("tx", k), k=k)
    ev("sum", ("sum", 0, "h0"), n=0, part="h0")
    ada(0)
    ev("stat", ("stat", 0, "h0"), n=0, part="h0")
    ev("sum", ("sum", 0, "h1"), n=0, part="h1")
    ada(1)
    ev("stat", ("stat", 0, "h1"), n=0, part="h1")
    ev("sum", ("sum", 0, "c"), n=0, part="c")
    ev("small", "small")
    ev("stat", ("stat", 0, "c"), n=0, part="c")
    for p in ("h0", "h1", "c"):
        ev("apply", ("apply", 0, p), n=0, part=p)
    ev("spill", ("spill", 0), n=0)
    x3 = ("h0", "h1", "c")

    def group(name, v, kind="lin", after=None):
        w = weights("ab", name)
        for p in x3:
            mid = {("h0", True): ("adac", v - 1, 1), ("h1", v < 6): ("adac", v, 0),
                   ("c", v == 6): ("adac", v, None)}.get((p, v > 2 if p == "h0" else True))
            lin((name, p), "ab", name, p, w, last=p == "c", kind=kind, mid=mid)
            if mid:
                ev("adapost", ("adapost",) + mid[1:], v=mid[1], n=mid[2])
            if after:
                after(p)
            if p == "h0":
                adav(v, 0 if v < 6 else None)
            if p == "h1" and v < 6:
                adav(v, 1)

    def chans(p):
        for half in range(2 if p != "c" else 1):
            ev("chan", ("chan", p, half), part=p, half=half)

    group("xb", 2, after=chans)
    group("u", 3)
    group("ga", 4)
    group("v", 5, kind="tok", after=lambda p: ev("spat", ("spat", p), part=p))
    group("gb", 6)
    for a in range(4):
        ev("abload", ("abload", a), a=a)
    ev("abload", ("abload", "c"), a="c")
    for odd in (0, 1):
        w = [slot("split", ("dft", odd * 8 + i, 0), None) for i in range(8)]
        ev("dft", ("dft", odd), odd=odd, ws=w)
    w = [slot("split", ("dft", 16 + i, 0), None) for i in range(2)]
    ev("dftc", ("dft", "c"), ws=w)
    for p in x3:
        ev("ysplit", ("ysplit", p), part=p)
    ev("reload", ("reload", 0), n=0)
    outs = [(g, p) for g in (0, 1) for p in x3]
    w = [weights("abo", 0), None]
    for g, p in outs:
        if g == 1 and p == "h0":
            w[1] = weights("abo", 1)
        lin(("abo", g, p), "abo", g, p, w[g], last=p == "c",
            mid=("stat", 1, "h0") if (g, p) == (1, "h1") else ("stat", 1, "h1") if (g, p) == (1, "c") else None)
        if g == 1:
            ev("sum", ("sum", 1, p), n=1, part=p)
            if p != "c":
                ev("statpost", ("statpost", 1, p), n=1, part=p)
                ev("apply", ("apply", 1, p), n=1, part=p)
    ev("spill", ("spill", 1), n=1)
    ev("statpost", ("statpost", 1, "c"), n=1, part="c")
    ev("apply", ("apply", 1, "c"), n=1, part="c")
    w = weights("c", "kv")
    for p in x3:
        lin(("kv", p), "c", "kv", p, w, last=p == "c", kind="kv",
            mid=("stat", 1, "c") if p == "h0" else None)
    x2 = ("h0", "h1")
    for g in range(2):
        w = weights("c", ("q", g))
        for p in x2:
            lin(("q", g, p), "c", ("q", g), p, w, last=p == "h1")
    last_v = None
    for g in range(2):
        w = weights("c", ("g", g))
        for p in x2:
            lin(("g", g, p), "c", ("g", g), p, w, last=p == "h1", mid=("adac", last_v, None) if last_v else None)
            if last_v:
                ev("adapost", ("adapost", last_v, None), v=last_v, n=None)
            last_v = 7 + 2 * g + x2.index(p)
            adav(last_v)
    ev("attc", "attc")
    ev("reload", ("reload", 1), n=1)
    for p in x2:
        ev("hload", ("hload", 1, p), n=1, part=p)
    for g in (0, 1):
        w = weights("co", g)
        for p in x2:
            lin(("co", g, p), "co", g, p, w, last=p == "h1",
                mid={(0, "h0"): ("adac", 10, None), (1, "h0"): ("adac", 11, None),
                     (1, "h1"): ("stat", 2, "h0")}.get((g, p)))
            if (g, p) == (0, "h0"):
                ev("adapost", ("adapost", 10, None), v=10, n=None)
                adav(11)
            if (g, p) == (1, "h0"):
                ev("adapost", ("adapost", 11, None), v=11, n=None)
            if g == 1:
                ev("sum", ("sum", 2, p), n=2, part=p)
                ev("statpost", ("statpost", 2, p), n=2, part=p)
                ev("apply", ("apply", 2, p), n=2, part=p)
    ev("spill", ("spill", 2), n=2)
    for name in ("cv", "cg", "q2", "k2", "v2"):
        w = weights("b2", name)
        for p in x2:
            first = name == "cv" and p == "h0"
            lin((name, p), "b2", name, p, w, last=p == "h1", kind="tok" if name == "v2" else "lin",
                mid=("stat", 2, "h1") if first else None)
            if name in ("q2", "k2", "v2"):
                ev("conv", ("conv", name, p), i=2 * ("q2", "k2", "v2").index(name) + x2.index(p))
    w = weights("b2", "f")
    ev("flog", "flog", ws=w)
    for p in x2:
        ev("cmean", ("cmean", p), part=p)
        ev("cvar", ("cvar", p), part=p)
    ev("attf", "attf")
    ev("reload", ("reload", 2), n=2)
    for p in x2:
        ev("hload", ("hload", 2, p), n=2, part=p)
    def stats(n, p, mid=False):
        ev("statpost" if mid else "stat", ("statpost" if mid else "stat", n, p), n=n, part=p)

    for g in (0, 1):
        w = weights("wo", g)
        for p in x2:
            lin(("wo", g, p), "wo", g, p, w, last=p == "h1", mid=("stat", 3, "h0") if (g, p) == (1, "h1") else None)
            if (g, p) == (1, "h0"):
                ev("sum", ("sum", 3, p), n=3, part=p)
                stats(3, p, mid=True)
                ev("resid", ("resid", 3, p), n=3, part=p)
                ev("sum", ("sum", 4, p), n=4, part=p)
    stats(4, "h0")
    ev("apply", ("apply", 4, "h0"), n=4, part="h0")
    ev("sum", ("sum", 3, "h1"), n=3, part="h1")
    stats(3, "h1", mid=True)
    ev("resid", ("resid", 3, "h1"), n=3, part="h1")
    ev("sum", ("sum", 4, "h1"), n=4, part="h1")
    nch = HID // 256
    for ch in range(nch):
        w = weights("fi", ch)
        for p in x2:
            lin(("fi", ch, p), "fi", ch, p, w, last=p == "h1", mid=("stat", 3, "h1") if (ch, p) == (0, "h0") else None)
            if (ch, p) == (0, "h0"):
                stats(4, "h1")
                ev("apply", ("apply", 4, "h1"), n=4, part="h1")
        w = [[slot("split", ("fo", (ch, g), k), None) for k in range(2)] for g in range(2)]
        for p in x2:
            for g in (0, 1):
                lin(("fo", ch, g, p), "fo", g, p, w[g], kts=2, last=p == "h1", h="A", ch=ch)
            if ch == nch - 1 and p == "h0":
                ev("sum", ("sum", 5, p), n=5, part=p)
    stats(5, "h0")
    ev("resid", ("resid", 5, "h0"), n=5, part="h0")
    ev("sum", ("sum", 5, "h1"), n=5, part="h1")
    stats(5, "h1")
    for p in x2:
        if p == "h1":
            ev("resid", ("resid", 5, "h1"), n=5, part="h1")
        for half in range(2):
            ev("out", ("out", p, half), part=p, half=half)
    return tl, slots


def program(nc, a, marks, old):
    TL, SLOTS = plan()
    ctx = ExitStack()
    with ctx:
        slab = ctx.enter_context(nc.sbuf_tensor("slab", [P, 212000 // 4], F32))
        base = [None]

        def at(name, shape, dt, off):
            return nc.alloc_sbuf_tensor_at(name, [P] + shape, dt, offset=BASE + off)

        BASE = 16512
        HREG, WREG, XREG = 0, 81920, 122880
        MREG = 163840
        HXH, HXL = at("HXH", [KT, T], F32R, HREG), at("HXL", [KT, T], F32R, HREG + 32768)
        HCH, HCL = at("HCH", [KT, C], F32R, HREG + 65536), at("HCL", [KT, C], F32R, HREG + 73728)
        AHH, AHL = at("AHH", [2, T], F32R, HREG + 65536), at("AHL", [2, T], F32R, HREG + 73728)
        XRAW = at("XRAW", [10, D], F32, HREG)
        WH, WL = at("WH", [WSLOTS, HALF], F32R, WREG), at("WL", [WSLOTS, HALF], F32R, WREG + 16384)
        RAW = at("RAW", [RSLOTS, HALF], F32, WREG + 32768)
        XX, XC = at("XX", [KT, T], F32, XREG), at("XC", [KT, C], F32, XREG + 32768)
        o = [MREG + 32768]

        def small(name, shape, dt=F32):
            n = 4 * int(np.prod(shape))
            t = at(name, shape, dt, o[0])
            o[0] += -(-n // 32) * 32
            return t

        TM = [small(f"TM{i}", [HALF]) for i in range(3)]
        SUM, RST = small("SUM", [HALF]), small("RST", [HALF])
        RST0 = {p: at(f"RST0{p}", [HALF], F32, MREG + 8192 + 2048 * i) for i, p in enumerate(PARTS)}
        PC = small("PC", [384])
        IDF, IDR, ONF = small("IDF", [P]), small("IDR", [P], F32R), small("ONF", [P])
        MOD = small("MOD", [12, 2, KT])
        MX, SU, RC = ([small(f"{n}{b}", [4]) for b in range(2)] for n in ("MX", "SU", "RC"))
        NSK = small("NSK", [16])
        CO = small("CO", [10, KT])
        CS = small("CS", [KT, 4])
        EPT = small("EPT", [1])
        BST, MV = small("BST", [4, 6]), small("MV", [4, 2])
        SM = small("SM", [64])
        assert BASE + o[0] <= 229368, BASE + o[0]
        M = MREG
        PROW = at("PROW", [3, P], F32, M)
        VBH, VBL = at("VBH", [4, HALF], F32R, M), at("VBL", [4, HALF], F32R, M + 8192)
        STG = at("STG", [2048], F32, M + 16384)
        SWH, SWL = at("SWH", [4, P], F32R, M + 24576), at("SWL", [4, P], F32R, M + 26624)
        SBB = at("SBB", [4, P], F32, M + 28672)
        CHH, CHL = at("CHH", [256], F32R, M + 30720), at("CHL", [256], F32R, M + 31744)
        SWRAW = at("SWRAW", [4, P], F32, M + 16384)
        CHRAW = at("CHRAW", [256], F32, M + 18432)
        ARAW = at("ARAW", [2, D], F32, M + 16384)
        ASD = at("ASD", [2, D], F32, M)
        KS, VS = at("KS", [4, T + C], F32R, XREG), at("VS", [10, 4, P], F32R, XREG + 20480)
        ROPE = at("ROPE", [2, T], F32, M)
        QS = [[at(f"QS{b}{x}", [4, HALF], F32R, HREG + 16384 * b + 8192 * x) for x in range(2)] for b in range(2)]
        RQ = [at(f"RQ{b}", [2, HALF], F32, (HREG + 53312, M + 28160)[b]) for b in range(2)]
        PB = [at(f"PB{b}", [4, 641], F32, HREG + 32768 + 10272 * b) for b in range(2)]
        PTH, PTL = at("PTH", [5, HALF], F32R, HREG + 61440), at("PTL", [5, HALF], F32R, HREG + 71680)
        OT = [at(f"OT{b}", [2, HALF], F32, M + 8192 + 4096 * b) for b in range(2)]
        GT = [at(f"GT{b}", [2, HALF], F32, M + 16384 + 4096 * b) for b in range(2)]
        OTT = at("OTT", [2, P], F32, M + 24576)
        MKF, MKR = at("MKF", [2, P], F32, M + 25600), at("MKR", [2, P], F32R, M + 26624)
        SINK = at("SINK", [16], F32, M + 27648)
        U = at("U", [4, T + TAPS - 1], F32, M)
        CA = at("CA", [4, T], F32, XREG)
        QH2 = [at(f"QH2{b}", [T], F32R, HREG + 12288 * b) for b in range(2)]
        QL2 = [at(f"QL2{b}", [T], F32R, HREG + 4096 + 12288 * b) for b in range(2)]
        KS2 = [at(f"KS2{b}", [T], F32R, HREG + 8192 + 12288 * b) for b in range(2)]
        RQ2, RK2 = at("RQ2", [T], F32, HREG + 24576), at("RK2", [T], F32, HREG + 28672)
        RV2 = at("RV2", [NB_T, P], F32, HREG + 32768)
        NBC = [at(f"NBC{b}", [T], F32, HREG + 36864 + 4096 * b) for b in range(2)]
        PB2 = [at(f"PB2{b}", [4, T], F32, HREG + 45056 + 16384 * b) for b in range(2)]
        PT2H, PT2L = at("PT2H", [8, HALF], F32R, XREG), at("PT2L", [8, HALF], F32R, XREG + 16384)
        VS2 = [at(f"VS2{b}", [NB_T, P], F32R, XREG + 32768 + 4096 * b) for b in range(2)]
        OT2 = [at(f"OT2{b}", [T], F32, M + 8192 + 4096 * b) for b in range(2)]
        OTT2 = at("OTT2", [HALF], F32, M + 16384)
        MKF2, MKR2 = at("MKF2", [P], F32, M + 20480), at("MKR2", [P], F32R, M + 20992)
        FL = [at(f"FL{i}", [T], F32, M + 17408 + 4096 * i) for i in range(3)]
        OUTS = [at(f"OUTS{b}", [2048], F32, HREG + 8192 * b) for b in range(2)]
        Y = at("Y", [KT, T], F32, M)
        LR = [at(f"LR{b}", [KT, HALF], F32, M + 16384 * b) for b in range(2)]
        PS = ctx.enter_context(nc.psum_tensor("PS", [P, 8, HALF], F32))

        def scratch(name, shape):
            return nc.dram_tensor(name, shape, F32, kind="Internal").ap()

        XR = scratch("XR", [P, KT, T])
        ABD = scratch("ABD", [T + C, D])
        QD, GD, OD = (scratch(n, [P, KT, T]) for n in ("QD", "GD", "OD"))
        XCD = scratch("XCD", [P, KT, C])
        KD2 = scratch("KD2", [P, 4, T])
        VD2 = scratch("VD2", [T, HALF])
        CUM = scratch("CUM", [8, T])

        counts = {}

        def did(semaphore, *names, by=1):
            counts[semaphore.name] = counts.get(semaphore.name, 0) + by
            for n in names:
                marks[n] = (semaphore, counts[semaphore.name])

        def so_far(semaphore):
            return counts[semaphore.name]

        def upto(*name):
            return of(*name)[1]

        def of(*name):
            name = name[0] if len(name) == 1 else name
            if not old:
                return products_done, 1
            s, v = old[name]
            return semaphores[s.name], v

        semaphores = {}

        def sem(name):
            semaphores[name] = ctx.enter_context(nc.semaphore(name))
            return semaphores[name]

        products_done, scalar_done = sem("products_done"), sem("scalar_done")
        vector_done, gpsimd_done = sem("vector_done"), sem("gpsimd_done")
        rows_loaded, x_loaded, tables_loaded = sem("rows_loaded"), sem("x_loaded"), sem("tables_loaded")
        late_loaded, spilled, cum_stored = sem("late_loaded"), sem("spilled"), sem("cum_stored")
        raw_loaded = [sem(f"raw_loaded{r}") for r in range(RSLOTS)]
        stage_free = [sem(f"stage_free{r}") for r in range(3)]
        ab_loaded, rq_loaded, g_loaded, ot_stored, nb_loaded, h_loaded = (
            [sem(f"{n}{b}") for b in range(2)]
            for n in ("ab_loaded", "rq_loaded", "g_loaded", "ot_stored", "nb_loaded", "h_loaded"))

        def uses(e):
            k, l, g = e["kind"], e.get("layer"), e.get("group")
            w4 = 2 if e.get("part") == "c" else 4
            if k == "ada":
                return 2
            if k in ("sum",):
                return 16 if e["n"] == 2 else 8
            if k in ("stat", "statpost"):
                return 1 if e["n"] == 2 else 0
            if k in ("apply", "resid"):
                return 8
            if k == "spat" or k == "cmean":
                return 4
            if k == "kv":
                return 2 if e["part"] == "c" else 4
            if k == "tok" and l == "ab":
                return w4
            if k in ("lin", "tok"):
                if g in ("ga", "cg", "q2", "k2", "v2") or (l == "c" and g[0] == "g"):
                    return 4
                if l == "c":
                    return 8
                if l == "fi":
                    return 2
            return 0

        TMID = []
        for e in TL:
            TMID += [(e["name"], i) for i in range(uses(e))]
        TMAT = {x: i for i, x in enumerate(TMID)}

        def tm_before(name, i):
            n = TMAT[(name, i)]
            return [TMID[n - 3]] if n >= 3 else []

        def tm(name, i, w=HALF, p0=0, p1=P):
            return TM[TMAT[(name, i)] % 3][p0:p1, 0:w]


        def tcount(z, which):
            if which == "c":
                return sum(4 if y % 8 in (0, 7) else 5 for y in range(z))
            return sum(4 if y % 2 == 0 else 8 for y in range(z))

        def spread(which):
            steps = 32 if which == "c" else 16
            tiles = {}
            for z in range(steps):
                n = tcount(z + 1, which) - tcount(z, which)
                first = 0
                for h, m in zip((1, 2, 3), {4: (2, 1, 1), 5: (2, 2, 1), 8: (3, 3, 2)}[n]):
                    tiles[4 * (z + 1) + h] = [(z, first + x) for x in range(m)]
                    first += m
            return tiles

        def key_blocks(z):
            return list(range(1 if z % 8 in (0, 7) else 0, 5))

        splits = [n for n, x in enumerate(SLOTS) if x[0] == "split"]
        WPOS = {n: i % WSLOTS for i, n in enumerate(splits)}
        WPREV = {n: splits[i - WSLOTS] for i, n in enumerate(splits) if i >= WSLOTS}

        order = []
        for e in TL:
            if e["kind"] in ("params", "tx", "ada", "adac", "stat", "lin", "tok", "kv", "chan", "spat", "dft",
                             "dftc", "flog", "cmean", "cvar", "out", "small"):
                order.append((e["name"], e))
                if e.get("mid"):
                    order.append((e["mid"], e))
            if e["kind"] in ("attc", "attf"):
                order.append((e["name"], e))
        setof, prev, lastin = {}, {}, {0: None, 1: None}
        cur = 0
        for name, e in order:
            if e["kind"] in ("attc", "attf"):
                prev[name] = [x for x in lastin.values() if x]
                lastin = {0: name, 1: name}
                cur = 0
                continue
            if e.get("mid") == name:
                s = 1 - setof[e["name"]]
            else:
                s = cur
                cur = 1 - cur
            setof[name] = s
            prev[name] = [lastin[s]] if lastin[s] else []
            lastin[s] = name

        def bank(name, b, n=HALF, p0=0, p1=P):
            return PS[p0:p1, 4 * setof[name] + b, 0:n]


        def hs(part, k, lo):
            off, n = PARTS[part]
            if part == "c":
                return (HCL if lo else HCH)[:, k, :]
            return (HXL if lo else HXH)[:, k, off:off + n]

        def xs(part, k):
            off, n = PARTS[part]
            return XC[:, k, :] if part == "c" else XX[:, k, off:off + n]

        def ys(part, k):
            off, n = PARTS[part]
            return Y[:, k, off:off + n]

        def col(name, i=0):
            b = ROWS[name][0] + i
            return PC[:, b:b + 1]

        def cols(name, i=0, n=None):
            b, m = ROWS[name]
            return PC[:, b + i:b + i + (n or m)]

        def mod(v, part, k):
            return MOD[:, v, 1 if part == "c" else 0, k:k + 1]

        def acoef(n, part, k):
            i = {0: 0, 1: 2, 2: 4, 4: 5}[n] + (1 if part == "c" else 0)
            return CO[:, i, k:k + 1]

        def shift(n, part, k):
            return mod({0: 0, 1: 3, 2: 6, 4: 9}[n], part, k)

        HREADERS = {0: {}, 1: {p: ("abo", 1, p) for p in PARTS}, 2: {p: ("co", 1, p) for p in PARTS},
                    4: {p: ("wo", 1, p) for p in PARTS}}
        HMAKER = {"ab": ("apply", 0), "abo": ("ysplit", 0), "c": ("apply", 1), "co": ("hload", 1),
                  "b2": ("apply", 2), "wo": ("hload", 2), "fi": ("apply", 4)}

        block = ctx.enter_context(nc.Block())

        @block.sync
        def _(sp):

            with nc.allow_non_contiguous_dma(reason="small parameters"):
                sp.dma_start(IDF[:, :], a["t_ident"]).then_inc(rows_loaded, 16)
                did(rows_loaded, "rows", by=16)
                sp.dma_start(SM[0:8, 48:49], a["b_f_2"].rearrange("l h -> h l")).then_inc(rows_loaded, 16)
                did(rows_loaded, "rows", by=16)
                for name, src in (("norm_g", a["norm_g"].rearrange("l (k p) -> (l k) p", p=P)),
                                  ("ada_b", a["ada_b"].rearrange("l (k p) -> (l k) p", p=P)),
                                  ("c", a["c"].rearrange("b (k p) -> (b k) p", p=P)),
                                  ("c_ctx", a["c_ctx"].rearrange("(k p) -> k p", p=P)),
                                  ("c_2", a["c_2"].rearrange("b (k p) -> (b k) p", p=P)),
                                  ("v_norm_g", a["v_norm_g"].rearrange("l (k p) -> (l k) p", p=P)),
                                  ("final_g", a["final_g"].rearrange("(k p) -> k p", p=P)),
                                  *[(n, a[n].rearrange("l (k p) -> (l k) p", p=P)) for n in
                                    ("conv_b_2", "conv_ln_g_2", "conv_ln_b_2", "mix_pre_g_2", "mix_post_g_2",
                                     "ffn_pre_g_2", "ffn_post_g_2", "ada_b_2")],
                                  ("conv_w_2", a["conv_w_2"].rearrange("l j (k p) -> (l j k) p", p=P))):
                    r, n = ROWS[name]
                    sp.dma_start(PROW[r % P:r % P + n, r // P, :], src).then_inc(rows_loaded, 16)
                    did(rows_loaded, "rows", by=16)
            x_rows = a["x"].rearrange("b (t p) d -> p (b t) d", p=P)
            c_rows = a["ctx"].rearrange("b (t p) d -> p (b t) d", p=P)
            for b in range(2):
                sp.dma_start(XRAW[:, 4 * b:4 * b + 4, :], x_rows[:, 4 * b:4 * b + 4, :]).then_inc(x_loaded, 16)
                did(x_loaded, "xraw", by=16)
            sp.dma_start(XRAW[:, 8:10, :], c_rows).then_inc(x_loaded, 16)
            did(x_loaded, "xraw", by=16)
            sp.dma_start(SWRAW[:, :, :], a["spatial_w"].rearrange("l h q p -> q (l h) p")).then_inc(tables_loaded, 16)
            did(tables_loaded, "smallraw", by=16)
            sp.dma_start(CHRAW[:, :], a["t_chan"]).then_inc(tables_loaded, 16)
            did(tables_loaded, "smallraw", by=16)
            sb = a["spatial_b"].rearrange("l h q -> (l h q)")
            sp.dma_start(SBB[:, :, :].rearrange("p h q -> p (h q)"),
                         sb.partition_broadcast(P)).then_inc(tables_loaded, 16)
            did(tables_loaded, "smallraw", by=16)
            for n, (kind, src, _) in enumerate(SLOTS):
                r = n % RSLOTS
                if n >= RSLOTS:
                    sp.wait_ge(*of("rawfree", n - RSLOTS))
                w = 8 if src[:2] == ("b2", "f") else HALF
                dst = RAW[:, r, 0:w]
                l, g, k = src[0], src[1], src[2]
                rows = slice(k * P, (k + 1) * P)
                if l == "ada":
                    v, n2 = g, src[3]
                    m, c0 = (a["ada_w"][v // 3], (v % 3) * D) if v < 6 else (a["ada_w_2"][0], (v - 6) * D)
                    s = [m[rows, c0 + n2 * HALF:c0 + (n2 + 1) * HALF]]
                elif l == "ab":
                    c0 = ("u", "v", "ga", "xb", "gb").index(g) * HALF
                    s = [a["w_in_ab"][0][rows, c0:c0 + HALF]]
                elif l == "abo":
                    s = [a["w_out_ab"][0][rows, g * HALF:(g + 1) * HALF]]
                elif l == "co":
                    s = [a["w_out_c"][0][rows, g * HALF:(g + 1) * HALF]]
                elif l == "wo":
                    s = [a["w_o_2"][0][rows, g * HALF:(g + 1) * HALF]]
                elif l == "c":
                    c0 = 1024 if g == "kv" else (0 if g[0] == "q" else 1536) + g[1] * HALF
                    s = [a["w_in_c"][0][rows, c0:c0 + HALF]]
                elif l == "b2":
                    c0 = {"q2": 0, "k2": 512, "v2": 1024, "f": 1536, "cv": 1544, "cg": 2056}[g]
                    s = [a["w_in_2"][0][rows, c0:c0 + w]]
                elif l == "fi":
                    m = a["w_ffn_in_2"][0]
                    s = [m[rows, g * 256:(g + 1) * 256], m[rows, HID + g * 256:HID + (g + 1) * 256]]
                elif l == "fo":
                    ch, gg = g
                    s = [a["w_ffn_out_2"][0][ch * 256 + k * P:ch * 256 + (k + 1) * P, gg * HALF:(gg + 1) * HALF]]
                elif l == "dft":
                    s = [a["t_dft"][g]]
                wd = w // len(s)
                for i, x in enumerate(s):
                    sp.dma_start(dst[:, i * wd:(i + 1) * wd], x).then_inc(raw_loaded[r], 16)
                    did(raw_loaded[r], ("raw", n), by=16)

        @block.gpsimd
        def _(pool):
            g = nc.gpsimd

            def split(n):
                r, w = n % RSLOTS, n % WSLOTS
                m = 8 if SLOTS[n][1][:2] == ("b2", "f") else HALF
                pool.wait_ge(raw_loaded[n % RSLOTS], upto("raw", n))
                if n in WPREV:
                    pool.wait_ge(products_done, upto("used", WPREV[n]))
                sw = WPOS[n]
                g.tensor_scalar(WH[:, sw, 0:m], RAW[:, r, 0:m], 1.0, 0.0, ALU.mult, ALU.add).then_inc(gpsimd_done, 1)
                did(gpsimd_done, ("whi", n))
                pool.wait_ge(gpsimd_done, so_far(gpsimd_done))
                g.tensor_tensor(WL[:, sw, 0:m], RAW[:, r, 0:m], WH[:, sw, 0:m].bitcast(F32), ALU.subtract).then_inc(gpsimd_done, 1)
                did(gpsimd_done, ("w", n), ("rawfree", n))

            done = [0]

            def split_until(n):
                while done[0] < min(n, len(SLOTS)):
                    if SLOTS[done[0]][0] == "split":
                        split(done[0])
                    done[0] += 1

            g.memset(ONF[:, :], 1.0).then_inc(gpsimd_done, 1)
            did(gpsimd_done, "ones")
            g.memset(EPT[:, :], EPS).then_inc(gpsimd_done, 1)
            did(gpsimd_done, "eps")
            for e in TL:
                if e["kind"] not in ("attc", "attf"):
                    continue
                ahead = [x["ws"][-1] for x in TL[:TL.index(e)] if x.get("ws")]
                n0 = max(ahead) + 1
                split_until(n0)
                more = n0
                while more < len(SLOTS) and more < n0 + WSLOTS and SLOTS[more][0] == "split":
                    more += 1
                split_until(more)
                if e["kind"] == "attc":
                    for s in range(32):
                        i = s % 8
                        lo = 128 if i in (0, 7) else 0
                        for h in range(4):
                            pool.wait_ge(vector_done, upto("rc", "c", 4 * s + h))
                            x = PB[s % 2][:, h, lo:640]
                            g.tensor_scalar(x, x, RC[s % 2][:, h:h + 1], 1.0, ALU.mult, ALU.mult).then_inc(gpsimd_done, 1)
                            did(gpsimd_done, ("P", "c", s, h))
                else:
                    for s in range(16):
                        for i4 in range(4):
                            n = (4 * (s % 2) + i4 + 1) * P
                            pool.wait_ge(vector_done, upto("rc", "f", 4 * s + i4))
                            x = PB2[s % 2][:, i4, 0:n]
                            g.tensor_scalar(x, x, RC[s % 2][:, i4:i4 + 1], 1.0, ALU.mult, ALU.mult).then_inc(gpsimd_done, 1)
                            did(gpsimd_done, ("P", "f", s, i4))
            split_until(len(SLOTS))

        @block.tensor
        def _(pe):
            mm = nc.tensor.matmul

            def three(out, wh, wl, xh, xl, first, last, group=True):
                kw = {} if group else {"skip_group_check": True}
                mm(out, wh, xh, start=first, stop=False, **kw)
                mm(out, wh, xl, start=False, stop=False, **kw)
                return mm(out, wl, xh, start=False, stop=last, **kw)

            def stat(name, n, part):
                w = PARTS[part][1]
                pe.wait_ge(gpsimd_done, upto("ones"))
                pe.wait_ge(vector_done, upto("sum", n, part))
                for job_before in prev[name]:
                    pe.wait_ge(*of("free", job_before))
                mm(bank(name, 0, w), ONF[:, :], SUM[:, 0:w], start=True, stop=True).then_inc(products_done, 1)
                did(products_done, ("job", name))
                if n == 2:
                    pe.wait_ge(vector_done, upto("sumg", n, part))
                    mm(bank(name, 1, w), ONF[:, :], RST[:, 0:w], start=True, stop=True).then_inc(products_done, 1)
                    did(products_done, ("job", name))

            def ada_sums(name, v, n):
                for job_before in prev[name]:
                    pe.wait_ge(*of("free", job_before))
                for x in range(2):
                    pe.wait_ge(vector_done, upto("ada_acc", v, n, KT - 1, x))
                    for j in range(4):
                        c0 = 2 * (4 * n + j) + x if n is not None else 2 * (4 * x + j)
                        ins = mm(bank(name, 0)[:, c0:c0 + 1], (SUM, RST)[x][:, j * P:(j + 1) * P], ONF[:, 0:1],
                                 start=True, stop=True)
                ins.then_inc(products_done, 1)
                did(products_done, ("job", name))

            for e in TL:
                kind, name = e["kind"], e["name"]
                if kind in ("sum", "apply", "coef", "spill", "abload", "ysplit", "reload", "statpost", "conv",
                            "hload", "resid", "adav", "adapost"):
                    continue
                part = e.get("part")
                if kind not in ("attc", "attf", "stat"):
                    for job_before in prev[name]:
                        pe.wait_ge(*of("free", job_before))
                if kind == "params":
                    pe.wait_ge(rows_loaded, upto("rows"))
                    for b in range(3):
                        nr = (P, 64, 124)[b]
                        ins = nc.tensor.transpose(PS[:, 0, b * P:b * P + nr], PROW[0:nr, b, :], IDF[0:nr, 0:nr])
                    ins.then_inc(products_done, 1)
                    did(products_done, ("job", name))
                elif kind == "tx":
                    pe.wait_ge(x_loaded, upto("xraw"))
                    pe.wait_ge(rows_loaded, upto("rows"))
                    for tb in range(10):
                        ins = nc.tensor.transpose(bank(name, tb // 4)[:, (tb % 4) * P:(tb % 4 + 1) * P],
                                                  XRAW[:, tb, e["k"] * P:(e["k"] + 1) * P], IDF[:, :])
                    ins.then_inc(products_done, 1)
                    did(products_done, ("job", name))
                elif kind == "ada":
                    pe.wait_ge(scalar_done, upto("cs"))
                    cond = 0 if e["v"] < 6 else 2
                    for i, n in enumerate(e["ws"]):
                        k, b = i // 2, i % 2
                        pe.wait_ge(raw_loaded[n % RSLOTS], upto("raw", n))
                        mm(bank(name, b, p1=2), CS[:, k, cond:cond + 2], RAW[:, n % RSLOTS, :],
                               start=k == 0, stop=k == KT - 1).then_inc(products_done, 1)
                        did(products_done, ("rawfree", n), ("job", name))
                elif kind == "adac":
                    pe.wait_ge(scalar_done, upto("arow", e["v"]))
                    an = ("ada", e["v"])
                    for k in range(KT):
                        ins = mm(bank(name, 0)[:, 2 * k:2 * k + 2], tm(an, k // 4, p1=2)[:, (k % 4) * P:(k % 4 + 1) * P],
                                 IDF[0:2, 0:2], start=True, stop=True)
                    ins.then_inc(products_done, 1)
                    did(products_done, ("job", name), ("tm", (an, 0)), ("tm", (an, 1)))
                elif kind == "small":
                    pe.wait_ge(tables_loaded, upto("smallraw"))
                    for h in range(4):
                        ins = nc.tensor.transpose(bank(name, 0)[:, h * P:(h + 1) * P], SWRAW[:, h, :], IDF[:, :])
                    ins.then_inc(products_done, 1)
                    did(products_done, ("job", name))
                elif kind == "stat":
                    stat(name, e["n"], e["part"])
                elif kind in ("lin", "tok", "kv"):
                    part, kts = e["part"], e["kts"]
                    off, n = PARTS[part]
                    mk = HMAKER.get(e["layer"])
                    for k in range(kts):
                        sw = WPOS[e["ws"][k]]
                        pe.wait_ge(gpsimd_done, upto("w", e["ws"][k]))
                        if e["h"] == "H":
                            pe.wait_ge(vector_done, upto("H", mk[0], mk[1], part, k))
                            xh, xl = hs(part, k, 0), hs(part, k, 1)
                        else:
                            pe.wait_ge(vector_done, upto("A", e["ch"], part, k))
                            xh, xl = AHH[:, k, off:off + n], AHL[:, k, off:off + n]
                        f, l = k == 0, k == kts - 1
                        if kind == "lin":
                            for j in range(4):
                                ws = slice(j * P, (j + 1) * P)
                                ins = three(bank(name, j, n), WH[:, sw, ws], WL[:, sw, ws], xh, xl, f, l)
                        elif kind == "tok":
                            for tb in range(n // P):
                                ts = slice(tb * P, (tb + 1) * P)
                                ins = three(bank(name, tb), xh[:, ts], xl[:, ts], WH[:, sw, :], WL[:, sw, :], f, l)
                        else:
                            for j in range(2):
                                ws = slice(j * P, (j + 1) * P)
                                ins = three(bank(name, j, n), WH[:, sw, ws], WL[:, sw, ws], xh, xl, f, l)
                            for tb in range(n // P):
                                ts = slice(tb * P, (tb + 1) * P)
                                o_ = bank(name, 2 + tb // 2)[:, (tb % 2) * 256:(tb % 2) * 256 + 256]
                                ins = three(o_, xh[:, ts], xl[:, ts], WH[:, sw, 256:512], WL[:, sw, 256:512],
                                            f and tb % 2 == 0, l, group=False)
                        nm = []
                        if e["last"]:
                            nm.append(("used", e["ws"][k]))
                        if l:
                            nm.append(("job", name))
                        if nm:
                            ins.then_inc(products_done, 1)
                            did(products_done, *nm)
                        if e["mid"] and k == 5:
                            if e["mid"][0] == "adac":
                                ada_sums(e["mid"], e["mid"][1], e["mid"][2])
                            else:
                                stat(e["mid"], e["mid"][1], e["mid"][2])
                elif kind == "chan":
                    part, half = e["part"], e["half"]
                    pe.wait_ge(vector_done, upto("xbs", part))
                    pe.wait_ge(vector_done, upto("small_split"))
                    for t2 in range(2):
                        for g in range(4):
                            tb = 2 * half + t2
                            ts = slice(tb * P, (tb + 1) * P)
                            o_ = bank(name, 2 * t2 + g // 2)[:, (g % 2) * 256:(g % 2) * 256 + 256]
                            ins = three(o_, VBH[:, g, ts], VBL[:, g, ts], CHH[:, :], CHL[:, :],
                                        True, True)
                    ins.then_inc(products_done, 1)
                    did(products_done, ("job", name))
                elif kind == "spat":
                    part = e["part"]
                    pe.wait_ge(vector_done, upto("small_split"))
                    for tb in range(PARTS[part][1] // P):
                        pe.wait_ge(vector_done, upto("vn", part, tb))
                        for h in range(4):
                            c_ = slice(h * P, (h + 1) * P)
                            ins = three(bank(name, h)[:, tb * P:(tb + 1) * P], VBH[:, tb, c_], VBL[:, tb, c_],
                                        SWH[:, h, :], SWL[:, h, :], True, True)
                    ins.then_inc(products_done, 1)
                    did(products_done, ("job", name))
                elif kind == "dft":
                    for kt in range(4):
                        hk = kt + 4 * e["odd"]
                        pe.wait_ge(vector_done, upto("AB", hk))
                        for cs in range(2):
                            n = e["ws"][2 * kt + cs]
                            pe.wait_ge(gpsimd_done, upto("w", n))
                            for g in range(4):
                                c_ = slice(g * 256 + cs * P, g * 256 + cs * P + P)
                                ins = three(bank(name, g), HXH[:, hk, c_], HXL[:, hk, c_], WH[:, WPOS[n], :],
                                            WL[:, WPOS[n], :], kt + cs == 0, kt == 3 and cs == 1)
                            ins.then_inc(products_done, 1)
                            did(products_done, ("used", n), ("job", name))
                elif kind == "dftc":
                    pe.wait_ge(vector_done, upto("AB", "c"))
                    hc = [x[:, :, :].rearrange("p k c -> p (k c)") for x in (HCH, HCL)]
                    for kt in range(2):
                        n = e["ws"][kt]
                        pe.wait_ge(gpsimd_done, upto("w", n))
                        for cs in range(2):
                            w_ = slice(cs * 256, cs * 256 + 256)
                            for g in range(4):
                                c0 = kt * D + g * 256 + cs * P
                                ins = three(bank(name, g, C), hc[0][:, c0:c0 + P], hc[1][:, c0:c0 + P],
                                            WH[:, WPOS[n], w_], WL[:, WPOS[n], w_], kt + cs == 0, kt + cs == 2)
                        ins.then_inc(products_done, 1)
                        did(products_done, ("used", n), ("job", name))
                elif kind == "flog":
                    for k in range(KT):
                        n = e["ws"][k]
                        pe.wait_ge(gpsimd_done, upto("w", n))
                        for b, p in enumerate(("h0", "h1")):
                            pe.wait_ge(vector_done, upto("H", "apply", 2, p, k))
                            ins = three(bank(name, b, p1=8), WH[:, WPOS[n], 0:8], WL[:, WPOS[n], 0:8],
                                        hs(p, k, 0), hs(p, k, 1), k == 0, k == KT - 1)
                        ins.then_inc(products_done, 1)
                        did(products_done, ("used", n), ("job", name))
                elif kind in ("cmean", "cvar"):
                    pe.wait_ge(vector_done, upto(kind + "_sum", e["part"]))
                    mm(bank(name, 0), ONF[:, :], SUM[:, :], start=True, stop=True).then_inc(products_done, 1)
                    did(products_done, ("job", name))
                elif kind == "out":
                    off = PARTS[e["part"]][0] + e["half"] * 256
                    for t2 in range(2):
                        for k in range(KT):
                            pe.wait_ge(vector_done, upto("xfin", e["part"], k))
                            ins = nc.tensor.transpose(bank(name, 2 * t2 + k // 4)[:, (k % 4) * P:(k % 4 + 1) * P],
                                                      XX[:, k, off + t2 * P:off + (t2 + 1) * P], IDF[:, :])
                    ins.then_inc(products_done, 1)
                    did(products_done, ("job", name))
                elif kind == "attc":
                    for job_before in prev[name]:
                        pe.wait_ge(*of("free", job_before))
                    pe.wait_ge(scalar_done, upto("masks"))
                    pe.wait_ge(vector_done, upto("nsk"))
                    tiles = spread("c")
                    for u in range(4 * 32 + 6):
                        s, h = u // 4, u % 4
                        if s < 32:
                            kv, i = s // 8, s % 8
                            sb = 2 * (u % 2)
                            if u >= 2:
                                pe.wait_ge(scalar_done, upto("exp", "c", u - 2))
                            pe.wait_ge(vector_done, upto("qs", s // 4, h // 2))
                            q = slice((i % 4) * P, (i % 4 + 1) * P)
                            qh, ql = (QS[(s // 4) % 2][x][:, h, q] for x in range(2))
                            p0 = 1 if i in (0, 7) else 0
                            b0 = i - 1 if i > 0 else 0
                            nblk = 3 - p0
                            A_ = PS[:, sb, (1 + p0) * P:HALF]
                            kx = KS[:, kv, b0 * P:(b0 + nblk) * P]
                            mm(A_, qh, kx, start=True, stop=False, skip_group_check=True)
                            mm(A_, ql, kx, start=False, stop=False, skip_group_check=True)
                            if i > 0:
                                o_ = (1 + p0) * P
                                mm(PS[:, sb, o_:o_ + P], IDR[:, :], MKR[:, 0, :], start=False, stop=i == 7,
                                   skip_group_check=True)
                            if i < 7:
                                mm(PS[:, sb, 3 * P:4 * P], IDR[:, :], MKR[:, 1, :], start=False, stop=True,
                                   skip_group_check=True)
                            B_ = PS[:, sb + 1, 0:256]
                            mm(B_, qh, KS[:, kv, T:T + C], start=True, stop=False)
                            mm(B_, ql, KS[:, kv, T:T + C], start=False, stop=True)
                            hd = kv * 4 + h
                            mm(PS[:, sb + 1, 256:257], ONF[0:1, :], NSK[0:1, hd:hd + 1], start=True,
                               stop=True).then_inc(products_done, 1)
                            did(products_done, ("sc", "c", u))
                        if h == 0 and s >= 2:
                            z = s - 2
                            kv, i = z // 8, z % 8
                            pos = key_blocks(z)
                            if z >= 2:
                                pe.wait_ge(vector_done, upto("pvfree", "c", z - 2))
                            for ti, p_ in enumerate(pos):
                                blk = 8 + p_ - 3 if p_ >= 3 else (p_ - 1 if i == 0 else 5 + p_ if i == 7 else i - 1 + p_)
                                pe.wait_ge(vector_done, upto("ptl", "c", tcount(z, "c") + ti))
                                mm(PS[:, 6 + z % 2, :], VS[:, blk, kv, :], PTH[:, p_, :], start=ti == 0, stop=False)
                                ins = mm(PS[:, 6 + z % 2, :], VS[:, blk, kv, :], PTL[:, p_, :], start=False,
                                         stop=ti == len(pos) - 1)
                            ins.then_inc(products_done, 1)
                            did(products_done, ("pv", "c", z))
                        for z, ti in tiles.get(u, []):
                            tb = tcount(z, "c") + ti
                            p_ = key_blocks(z)[ti]
                            if tb >= 2:
                                pe.wait_ge(vector_done, upto("ptl", "c", tb - 2))
                            for hh in range(4):
                                pe.wait_ge(gpsimd_done, upto("P", "c", z, hh))
                                ins = nc.tensor.transpose(PS[:, 4 + tb % 2, hh * P:(hh + 1) * P],
                                                          PB[z % 2][:, hh, p_ * P:(p_ + 1) * P], IDF[:, :])
                            ins.then_inc(products_done, 1)
                            did(products_done, ("tr", "c", tb))
                elif kind == "attf":
                    for job_before in prev[name]:
                        pe.wait_ge(scalar_done, upto("free", job_before))
                    pe.wait_ge(scalar_done, upto("masks2"))
                    tiles = spread("f")
                    for u in range(4 * 16 + 6):
                        s, i4 = u // 4, u % 4
                        if s < 16:
                            hd, G = s // 2, s % 2
                            i = 4 * G + i4
                            n = (i + 1) * P
                            sb = 2 * (u % 2)
                            if u >= 2:
                                pe.wait_ge(vector_done, upto("mx", "f", u - 2))
                            pe.wait_ge(vector_done, upto("ql2", hd))
                            q = slice(i * P, (i + 1) * P)
                            for b in range(G + 1):
                                w_ = min(n - b * HALF, HALF)
                                o_ = PS[:, sb + b, 0:w_]
                                kx = KS2[hd % 2][:, b * HALF:b * HALF + w_]
                                mm(o_, QH2[hd % 2][:, q], kx, start=True, stop=False, skip_group_check=True)
                                ins = mm(o_, QL2[hd % 2][:, q], kx, start=False, stop=b < G, skip_group_check=True)
                                if b == G:
                                    ins = mm(PS[:, sb + b, w_ - P:w_], IDR[:, :], MKR2[:, :], start=False,
                                             stop=True, skip_group_check=True)
                            ins.then_inc(products_done, 1)
                            did(products_done, ("sc", "f", u))
                        if i4 == 0 and s >= 2:
                            z = s - 2
                            hd, G = z // 2, z % 2
                            pe.wait_ge(vector_done, upto("vs2", hd))
                            if z >= 2:
                                pe.wait_ge(vector_done, upto("pvfree", "f", z - 2))
                            nj = 4 * G + 4
                            for j in range(nj):
                                c0 = max(0, j - 4 * G) * P
                                pe.wait_ge(vector_done, upto("ptl", "f", tcount(z, "f") + j))
                                for x, t_ in enumerate((PT2H, PT2L)):
                                    ins = mm(PS[:, 6 + z % 2, c0:HALF], VS2[hd % 2][:, j, :], t_[:, j, c0:HALF],
                                             start=j == 0 and x == 0, stop=j == nj - 1 and x == 1,
                                             skip_group_check=True)
                            ins.then_inc(products_done, 1)
                            did(products_done, ("pv", "f", z))
                        for z, j in tiles.get(u, []):
                            tb = tcount(z, "f") + j
                            if tb >= 2:
                                pe.wait_ge(vector_done, upto("ptl", "f", tb - 2))
                            for q4 in range(max(0, j - 4 * (z % 2)), 4):
                                pe.wait_ge(gpsimd_done, upto("P", "f", z, q4))
                                ins = nc.tensor.transpose(PS[:, 4 + tb % 2, q4 * P:(q4 + 1) * P],
                                                          PB2[z % 2][:, q4, j * P:(j + 1) * P], IDF[:, :])
                            ins.then_inc(products_done, 1)
                            did(products_done, ("tr", "f", tb))

        @block.scalar
        def _(act):
            A = nc.scalar.activation



            stg, outn = [0], []

            def qdma(name, group, j, off, w):
                act.wait_ge(vector_done, upto("kr", name, j))
                act.dma_start(QD[:, group[1] * 4 + j, off:off + w],
                              tm(name, 2 * j)).then_inc(stage_free[TMAT[(name, 2 * j)] % 3], 16)
                did(stage_free[TMAT[(name, 2 * j)] % 3], ("tm", (name, 2 * j)), by=16)

            def load_q(act, b):
                kv, hf = b // 2, b % 2
                if b >= 2:
                    act.wait_ge(vector_done, upto("qs", b - 2, 1))
                act.dma_start(RQ[b % 2][:, :, :],
                              QD[:, 2 * kv:2 * kv + 2, hf * HALF:(hf + 1) * HALF]).then_inc(rq_loaded[b % 2], 16)
                did(rq_loaded[b % 2], ("rql", b), by=16)

            def prep_q_act(b, t):
                act.wait_ge(rq_loaded[b % 2], upto("rql", b))
                if b >= 2:
                    act.wait_ge(products_done, upto("sc", "c", 16 * (b - 1) - 1))
                x, q = RQ[b % 2][:, t, :], QS[b % 2][0]
                for half in range(2):
                    own_ = slice(64 * half, 64 * half + 64)
                    for o_ in (slice(0, 64), slice(64, P)):
                        A(q[o_, 2 * t + half, :], x[own_, :], ACT.Copy).then_inc(scalar_done, 1)
                        did(scalar_done, ("qh", b, t))

            def weights_high(z, ti):
                tb = tcount(z, "c") + ti
                act.wait_ge(products_done, upto("tr", "c", tb))
                if z >= 1:
                    act.wait_ge(products_done, upto("pv", "c", z - 1))
                A(PTH[:, key_blocks(z)[ti], :], PS[:, 4 + tb % 2, :], ACT.Copy).then_inc(scalar_done, 1)
                did(scalar_done, ("pth", "c", tb))

            def weights_high2(z, j):
                tb = tcount(z, "f") + j
                c0 = max(0, j - 4 * (z % 2)) * P
                act.wait_ge(products_done, upto("tr", "f", tb))
                if z >= 1:
                    act.wait_ge(products_done, upto("pv", "f", z - 1))
                A(PT2H[:, j, c0:HALF], PS[:, 4 + tb % 2, c0:HALF], ACT.Copy).then_inc(scalar_done, 1)
                did(scalar_done, ("pth", "f", tb))

            def pv_act(z):
                act.wait_ge(products_done, upto("pv", "c", z))
                if z:
                    act.wait_ge(vector_done, upto("ota", z - 1))
                src = PS[:, 6 + z % 2, :].rearrange("p (r e q) -> p e r q", e=2, q=P)
                A(OTT[0:64, :, :], src[64:P, 0, :, :], ACT.Copy).then_inc(scalar_done, 1)
                did(scalar_done, ("ott", z))
                A(OTT[64:P, :, :], src[0:64, 1, :, :], ACT.Copy).then_inc(scalar_done, 1)
                did(scalar_done, ("ott", z))

            def store_o(act, b):
                act.wait_ge(vector_done, upto("og", b))
                kv, hf = b // 2, b % 2
                act.dma_start(OD[:, 2 * kv:2 * kv + 2, hf * HALF:(hf + 1) * HALF],
                              OT[b % 2][:, :, :]).then_inc(ot_stored[b % 2], 16)
                did(ot_stored[b % 2], ("ost", "c", b), by=16)

            def load_pair(act, p_):
                if p_:
                    act.wait_ge(vector_done, upto("vs2", 2 * p_ - 1))
                for dst, src in ((RQ2[:, :], QD[:, p_, :]), (RK2[:, :], KD2[:, p_, :]),
                                 (RV2[:, :, :], VD2[:, p_ * P:(p_ + 1) * P].rearrange("(t q) n -> q t n", q=P))):
                    act.dma_start(dst, src).then_inc(rq_loaded[0], 16)
                    did(rq_loaded[0], ("pair", p_), by=16)

            def load_nb(act, hd):
                if hd >= 2:
                    act.wait_ge(vector_done, upto("mx", "f", 4 * (2 * (hd - 2) + 1) + 3))
                act.dma_start(NBC[hd % 2][:, :], CUM[hd, :].partition_broadcast(P)).then_inc(nb_loaded[hd % 2], 16)
                did(nb_loaded[hd % 2], ("nbl", hd), by=16)

            def prep2_act(hd):
                b, half = hd % 2, hd % 2
                act.wait_ge(rq_loaded[0], upto("pair", hd // 2))
                if hd >= 2:
                    act.wait_ge(products_done, upto("sc", "f", 8 * hd - 9))
                own_ = slice(64 * half, 64 * half + 64)
                for o_ in (slice(0, 64), slice(64, P)):
                    A(QH2[b][o_, :], RQ2[own_, :], ACT.Copy).then_inc(scalar_done, 1)
                    did(scalar_done, ("qh2", hd))
                A(KS2[b][own_, :], RK2[own_, :], ACT.Copy).then_inc(scalar_done, 1)
                did(scalar_done, ("qh2", hd))

            def prep2v_act(hd):
                b, half = hd % 2, hd % 2
                act.wait_ge(rq_loaded[0], upto("pair", hd // 2))
                if hd >= 2:
                    act.wait_ge(products_done, upto("pv", "f", 2 * hd - 3))
                A(VS2[b][:, :, 0:64], RV2[:, :, 64 * half:64 * half + 64], ACT.Copy).then_inc(scalar_done, 1)
                did(scalar_done, ("vh2", hd))

            def pv2_act(z):
                hd = z // 2
                act.wait_ge(products_done, upto("pv", "f", z))
                if z:
                    act.wait_ge(vector_done, upto("ota2", z - 1))
                a_, b_ = (slice(0, 64), slice(64, P)) if hd % 2 == 0 else (slice(64, P), slice(0, 64))
                A(OTT2[a_, :], PS[b_, 6 + z % 2, :], ACT.Copy).then_inc(scalar_done, 1)
                did(scalar_done, ("ott2", z))

            def store_o2(act, p_):
                act.wait_ge(vector_done, upto("ota2", 4 * p_ + 3))
                act.dma_start(OD[:, p_, :], OT2[p_ % 2][:, :]).then_inc(ot_stored[p_ % 2], 16)
                did(ot_stored[p_ % 2], ("ost", "f", p_), by=16)


            for e in TL:
                kind, name = e["kind"], e["name"]
                part = e.get("part")
                if "scalar_done" in counts:
                    act.wait_ge(scalar_done, so_far(scalar_done))
                if kind == "params":
                    act.wait_ge(products_done, upto("job", name))
                    A(PC[:, 0:192], PS[:, 0, 0:192], ACT.Copy).then_inc(scalar_done, 1)
                    did(scalar_done, "pc0")
                    A(PC[:, 256:380], PS[:, 0, 256:380], ACT.Copy).then_inc(scalar_done, 1)
                    did(scalar_done, "pc", ("free", name))
                    act.wait_ge(scalar_done, so_far(scalar_done))
                    for j, nm in enumerate(("c", "c_ctx", "c_2", "c_2")):
                        A(CS[:, :, j], cols(nm), ACT.Silu).then_inc(scalar_done, 1)
                        did(scalar_done, "cs")
                    act.wait_ge(rows_loaded, upto("rows"))
                    A(IDR[:, :], IDF[:, :], ACT.Copy).then_inc(scalar_done, 1)
                    did(scalar_done, "idr")
                elif kind == "tx":
                    act.wait_ge(products_done, upto("job", name))
                    k = e["k"]
                    A(XX[:, k, :].rearrange("p (b n) -> p b n", n=HALF), PS[:, 4 * setof[name]:4 * setof[name] + 2, :],
                          ACT.Copy).then_inc(scalar_done, 1)
                    did(scalar_done, ("xt", k))
                    A(XC[:, k, :], bank(name, 2, C), ACT.Copy).then_inc(scalar_done, 1)
                    did(scalar_done, ("X", 0, k), ("free", name))
                elif kind == "ada":
                    act.wait_ge(products_done, upto("job", name))
                    for i in range(2):
                        for use_before in tm_before(name, i):
                            act.wait_ge(*of("tm", use_before))
                        A(tm(name, i, p1=2), bank(name, i, p1=2), ACT.Copy).then_inc(scalar_done, 1)
                        did(scalar_done, ("arow", e["v"]), ("free", name))
                elif kind == "small":
                    act.wait_ge(products_done, upto("job", name))
                    A(SWH[:, :, :].rearrange("p h q -> p (h q)"), bank(name, 0), ACT.Copy).then_inc(scalar_done, 1)
                    did(scalar_done, "swh")
                    A(CHH[:, :], CHRAW[:, :], ACT.Copy).then_inc(scalar_done, 1)
                    did(scalar_done, "smallh")
                elif kind == "sum":
                    n = e["n"]
                    w = PARTS[part][1]
                    for k in range(KT):
                        src = xs(part, k) if n in (0, 1, 2, 4) else ys(part, k)
                        if n == 0:
                            act.wait_ge(*of("X", n, k))
                        else:
                            act.wait_ge(*of("X", n, part, k))
                        for use_before in tm_before(name, k):
                            act.wait_ge(*of("tm", use_before))
                        A(tm(name, k, w), src, ACT.Square).then_inc(scalar_done, 1)
                        did(scalar_done, ("sq", n, part, k))
                    if n == 2:
                        for k in range(KT):
                            for use_before in tm_before(name, 8 + k):
                                act.wait_ge(vector_done, upto("tm", use_before))
                            A(tm(name, 8 + k, w), xs(part, k), ACT.Square, scale=col("final_g", k)).then_inc(scalar_done, 1)
                            did(scalar_done, ("sqg", n, part, k))
                elif kind in ("stat", "statpost"):
                    n = e["n"]
                    w = PARTS[part][1]
                    nm = ("stat", n, part)
                    act.wait_ge(products_done, upto("job", nm))
                    act.wait_ge(gpsimd_done, upto("eps"))
                    if n == 2:
                        A(SUM[:, 0:w], bank(nm, 0, w), ACT.Sqrt, scale=1.0 / D, bias=EPT[:, :]).then_inc(scalar_done, 1)
                        did(scalar_done, ("sq1", n, part))
                        act.wait_ge(vector_done, upto("r1sq", n, part))
                        A(RST[:, 0:w], tm(name, 0, w), ACT.Sqrt, scale=1.0 / D, bias=EPT[:, :]).then_inc(scalar_done, 1)
                        did(scalar_done, ("sqrt", n, part), ("tm", (name, 0)))
                    else:
                        A((RST0[part] if n == 0 else RST)[:, 0:w], bank(nm, 0, w), ACT.Sqrt, scale=1.0 / D, bias=EPT[:, :]).then_inc(scalar_done, 1)
                        did(scalar_done, ("sqrt", n, part), ("free", nm))
                elif kind == "apply":
                    n = e["n"]
                    w = PARTS[part][1]
                    for k in range(KT):
                        act.wait_ge(vector_done, upto("t", n, part, k))
                        act.wait_ge(vector_done, upto("mod", {0: 1, 1: 4, 2: 7, 4: 10}[n]))
                        act.wait_ge(vector_done, upto("coef", n))
                        t_ = tm(name, k, w)
                        A(t_, t_, ACT.Identity, scale=acoef(n, part, k), bias=shift(n, part, k)).then_inc(scalar_done, 1)
                        did(scalar_done, ("h", n, part, k))
                        act.wait_ge(scalar_done, so_far(scalar_done))
                        if n in HREADERS and part in HREADERS[n]:
                            act.wait_ge(products_done, upto("job", HREADERS[n][part]))
                        elif n == 0:
                            act.wait_ge(products_done, upto("job", ("tx", 7)))
                            act.wait_ge(products_done, upto("job", ("adac", 1)))
                        A(hs(part, k, 0), t_, ACT.Copy).then_inc(scalar_done, 1)
                        did(scalar_done, ("hi", n, part, k))
                elif kind == "spill":
                    n = e["n"]
                    if n == 0:
                        act.wait_ge(scalar_done, upto("X", n, 7))
                    else:
                        act.wait_ge(vector_done, upto("XW", n))
                    if n == 0:
                        act.dma_start(XCD, XC[:, :, :]).then_inc(spilled, 16)
                        did(spilled, ("spill", n), by=16)
                    act.dma_start(XR, XX[:, :, :]).then_inc(spilled, 16)
                    did(spilled, ("spill", n), by=16)
                    if n == 1:
                        act.wait_ge(vector_done, upto("AB", 7))
                        act.wait_ge(vector_done, upto("AB", "c"))
                        act.dma_start(ROPE[:, :, :], a["t_rope"]).then_inc(tables_loaded, 16)
                        did(tables_loaded, "rope", by=16)
                elif kind == "reload":
                    n = e["n"]
                    if n == 0:
                        act.wait_ge(vector_done, upto("H", "ysplit", 0, "c", 7))
                        act.wait_ge(scalar_done, so_far(scalar_done))
                        act.dma_start(XC[:, :, :], XCD).then_inc(x_loaded, 16)
                        did(x_loaded, ("reload", n), by=16)
                    elif n == 1:
                        act.wait_ge(products_done, upto("pv", "c", 31))
                        act.wait_ge(spilled, upto("spill", 1))
                    else:
                        act.wait_ge(products_done, upto("pv", "f", 15))
                        act.wait_ge(spilled, upto("spill", 2))
                    act.dma_start(XX[:, :, :], XR).then_inc(x_loaded, 16)
                    did(x_loaded, ("reload", n), by=16)
                elif kind in ("lin", "tok", "kv"):
                    layer, group = e["layer"], e["group"]
                    act.wait_ge(products_done, upto("job", name))
                    off, w = PARTS[part]
                    if layer == "ab" and group == "xb":
                        if part != "h0":
                            act.wait_ge(products_done, upto("job", ("chan", {"h1": "h0", "c": "h1"}[part], 1)))
                        for g in range(4):
                            A(VBH[:, g, 0:w], bank(name, g, w), ACT.Copy).then_inc(scalar_done, 1)
                            did(scalar_done, ("vbh", part, g))
                    elif layer == "ab" and group in ("u", "gb"):
                        act.wait_ge(spilled, upto("spill", 0))
                        act.wait_ge(vector_done, upto("H", "apply", 0, "c", 7))
                        k0, f = (0, ACT.Copy) if group == "u" else (4, ACT.Silu)
                        src = PS[:, 4 * setof[name]:4 * setof[name] + 4, 0:w]
                        dst = XC[:, k0:k0 + 4, :] if part == "c" else XX[:, k0:k0 + 4, off:off + w]
                        A(dst, src, f).then_inc(scalar_done, 1)
                        did(scalar_done, (group, part), ("free", name))
                    elif layer == "ab" and group == "ga":
                        for j in range(4):
                            for use_before in tm_before(name, j):
                                act.wait_ge(*of("tm", use_before))
                            A(tm(name, j, w), bank(name, j, w), ACT.Silu).then_inc(scalar_done, 1)
                            did(scalar_done, ("gasilu", part, j), ("free", name))
                    elif layer == "ab" and group == "v":
                        act.wait_ge(vector_done, upto("mv", part))
                        act.wait_ge(gpsimd_done, upto("eps"))
                        nt = w // P
                        A(SM[:, 0:nt], MV[:, 0:nt, 1], ACT.Sqrt, bias=EPT[:, :]).then_inc(scalar_done, 1)
                        did(scalar_done, ("vsd", part))
                        for tb in range(nt):
                            act.wait_ge(vector_done, upto("vf", part, tb))
                            A(VBH[:, tb, :], tm(name, tb), ACT.Copy).then_inc(scalar_done, 1)
                            did(scalar_done, ("vh", part, tb))
                    elif layer == "c" and group == "kv":
                        per = 1 if part == "c" else 2
                        for j in range(2):
                            for use_before in tm_before(name, per * j):
                                act.wait_ge(vector_done, upto("tm", use_before))
                            src = tm(name, per * j, w)
                            A(src, bank(name, j, w), ACT.Copy).then_inc(scalar_done, 1)
                            did(scalar_done, ("kf", name, j))
                            if part == "c":
                                act.wait_ge(scalar_done, so_far(scalar_done))
                            else:
                                act.wait_ge(vector_done, upto("kr", name, j))
                            c0 = T if part == "c" else off
                            act.wait_ge(spilled, upto("spill", 1))
                            A(KS[0:64, 2 * j, c0:c0 + w], src[0:64, :], ACT.Copy).then_inc(scalar_done, 1)
                            did(scalar_done, ("khi", part, j, 0))
                            A(KS[64:P, 2 * j + 1, c0:c0 + w], src[64:P, :], ACT.Copy).then_inc(scalar_done, 1)
                            did(scalar_done, ("khi", part, j, 1))
                        for tb in range(0, w // P, 2):
                            b = (8 if part == "c" else off // P) + tb
                            A(VS[:, b:b + 2, :, 0:64], bank(name, 2 + tb // 2).rearrange("p (t h d) -> p t h d", d=64, h=4),
                                  ACT.Copy).then_inc(scalar_done, 1)
                            did(scalar_done, ("vhi", part, tb))
                    elif layer == "c":
                        if group[0] == "q":
                            for j in range(4):
                                for use_before in tm_before(name, 2 * j):
                                    act.wait_ge(*of("tm", use_before))
                                A(tm(name, 2 * j), bank(name, j), ACT.Copy, scale=-SCALE).then_inc(scalar_done, 1)
                                did(scalar_done, ("kf", name, j), ("free", name))
                                if j:
                                    qdma(name, group, j - 1, off, w)
                            qdma(name, group, 3, off, w)
                        else:
                            for j in range(4):
                                for use_before in tm_before(name, j):
                                    act.wait_ge(*of("tm", use_before))
                                A(tm(name, j), bank(name, j), ACT.Silu).then_inc(scalar_done, 1)
                                did(scalar_done, ("gs", name, j), ("free", name))
                                act.wait_ge(scalar_done, so_far(scalar_done))
                                act.dma_start(GD[:, group[1] * 4 + j, off:off + w],
                                              tm(name, j)).then_inc(stage_free[TMAT[(name, j)] % 3], 16)
                                did(stage_free[TMAT[(name, j)] % 3], ("tm", (name, j)), by=16)
                    elif layer == "b2":
                        if group == "cv":
                            if part == "h0":
                                act.wait_ge(vector_done, upto("upad"))
                            src = PS[:, 4 * setof[name]:4 * setof[name] + 4, 0:w]
                            A(U[:, :, 30 + off:30 + off + w], src, ACT.Copy).then_inc(scalar_done, 1)
                            did(scalar_done, ("uv", part), ("free", name))
                        elif group == "cg":
                            for j in range(4):
                                for use_before in tm_before(name, j):
                                    act.wait_ge(vector_done, upto("tm", use_before))
                                A(tm(name, j, w), bank(name, j, w), ACT.Sigmoid).then_inc(scalar_done, 1)
                                did(scalar_done, ("gasilu", name, j), ("free", name))
                        else:
                            for j in range(4):
                                for use_before in tm_before(name, j):
                                    act.wait_ge(*of("tm", use_before))
                                A(tm(name, j), bank(name, j), ACT.Copy,
                                  scale=-SCALE if group == "q2" else 1.0).then_inc(scalar_done, 1)
                                did(scalar_done, ("gs", name, j), ("free", name))
                                act.wait_ge(scalar_done, so_far(scalar_done))
                                dst = (QD[:, j, off:off + w] if group == "q2" else KD2[:, j, off:off + w]
                                       if group == "k2" else VD2[off + j * P:off + (j + 1) * P, :])
                                act.dma_start(dst, tm(name, j)).then_inc(stage_free[TMAT[(name, j)] % 3], 16)
                                did(stage_free[TMAT[(name, j)] % 3], ("tm", (name, j)), by=16)
                    elif layer == "wo":
                        if group == 0 and part == "h0":
                            act.wait_ge(vector_done, upto("H", "hload", 2, "h1", 7))
                        for j in range(4):
                            A(Y[:, group * 4 + j, off:off + w], bank(name, j), ACT.Copy).then_inc(scalar_done, 1)
                            did(scalar_done, ("X", 3, part, group * 4 + j), ("free", name))
                    elif layer == "fi":
                        ch = group
                        for j in range(2):
                            for use_before in tm_before(name, j):
                                act.wait_ge(vector_done, upto("tm", use_before))
                            A(tm(name, j), bank(name, j), ACT.Silu).then_inc(scalar_done, 1)
                            did(scalar_done, ("gsl", ch, part, j))
                        for j in range(2):
                            act.wait_ge(vector_done, upto("av", ch, part, j))
                            if ch:
                                act.wait_ge(products_done, upto("job", ("fo", ch - 1, 1, part)))
                            A(AHH[:, j, off:off + w], tm(name, j), ACT.Copy).then_inc(scalar_done, 1)
                            did(scalar_done, ("ahi", ch, part, j))
                    elif layer == "fo" and e["ch"] == 0:
                        src = PS[:, 4 * setof[name]:4 * setof[name] + 4, 0:w]
                        A(Y[:, group * 4:group * 4 + 4, off:off + w], src, ACT.Copy).then_inc(scalar_done, 1)
                        did(scalar_done, ("yacc", group, part), ("free", name))
                elif kind == "chan":
                    act.wait_ge(products_done, upto("job", name))
                    if stg[0]:
                        act.wait_ge(spilled, upto("abst", stg[0] - 1))
                    A(STG[:, :], PS[:, 4 * setof[name]:4 * setof[name] + 4, :].rearrange("p b n -> p (b n)"),
                          ACT.Copy).then_inc(scalar_done, 1)
                    did(scalar_done, ("free", name))
                    act.wait_ge(scalar_done, so_far(scalar_done))
                    t0 = (T if part == "c" else PARTS[part][0]) + e["half"] * 256
                    act.dma_start(ABD[t0:t0 + 256, :].rearrange("(t p) n -> p t n", p=P),
                                  STG[:, :].rearrange("p (t n) -> p t n", n=D)).then_inc(spilled, 16)
                    did(spilled, ("abst", stg[0]), by=16)
                    stg[0] += 1
                elif kind == "abload":
                    a_ = e["a"]
                    if a_ == 0:
                        act.wait_ge(spilled, upto("abst", stg[0] - 1))
                        act.wait_ge(products_done, upto("job", ("spat", "c")))
                    else:
                        act.wait_ge(vector_done, upto("abs", 3 if a_ == "c" else a_ - 1, 1))
                    idx = (8, 9) if a_ == "c" else (a_, a_ + 4)
                    for x in range(2):
                        act.dma_start(ARAW[:, x, :], ABD[idx[x] * P:(idx[x] + 1) * P, :]).then_inc(ab_loaded[x], 16)
                        did(ab_loaded[x], ("abl", a_, x), by=16)
                    for x in range(2):
                        act.wait_ge(products_done, upto("job", ("gb", "c")))
                        if a_ != "c":
                            act.wait_ge(vector_done, upto("abs", a_, x))
                        if a_ == "c":
                            hh = HCH[:, :, :].rearrange("p k c -> p (k c)")[:, x * D:(x + 1) * D]
                            act.wait_ge(ab_loaded[x], upto("abl", a_, x))
                            src = ARAW[:, x, :]
                        else:
                            hh = HXH[:, a_ + 4 * x, :]
                            src = ASD[:, x, :]
                        A(hh, src, ACT.Copy).then_inc(scalar_done, 1)
                        did(scalar_done, ("abh", a_, x))
                elif kind == "ysplit":
                    act.wait_ge(products_done, upto("job", ("dft", 1 if part != "c" else "c")))
                    if part == "h0":
                        act.wait_ge(vector_done, upto("yb", 0))
                        act.wait_ge(vector_done, upto("yb", 1))
                        act.wait_ge(vector_done, upto("ya", "h0"))
                    act.wait_ge(vector_done, upto("ya", part))
                    if part == "c":
                        act.wait_ge(vector_done, upto("yb", "c"))
                    else:
                        act.wait_ge(vector_done, upto("yb", 1))
                    for k in range(KT):
                        A(hs(part, k, 0), xs(part, k), ACT.Copy).then_inc(scalar_done, 1)
                        did(scalar_done, ("yh", part, k))
                elif kind == "hload":
                    n = e["n"]
                    b = 0 if part == "h0" else 1
                    off, w = PARTS[part]
                    if n == 1:
                        act.wait_ge(ot_stored[0], upto("ost", "c", 6))
                        act.wait_ge(ot_stored[1], upto("ost", "c", 7))
                    else:
                        act.wait_ge(ot_stored[1], upto("ost", "f", 3))
                        act.wait_ge(spilled, upto("ust", "h1"))
                        act.wait_ge(ot_stored[0], upto("ost", "f", 2))
                    if b == 0:
                        for b_, p_ in enumerate(("h0", "h1")):
                            act.dma_start(LR[b_][:, :, :],
                                          OD[:, :, b_ * HALF:(b_ + 1) * HALF]).then_inc(h_loaded[b_], 16)
                            did(h_loaded[b_], ("lr", n, p_), by=16)
                    act.wait_ge(h_loaded[b], upto("lr", n, part))
                    if n == 1:
                        act.wait_ge(products_done, upto("pv", "c", 31))
                    else:
                        act.wait_ge(products_done, upto("pv", "f", 15))
                    for k in range(KT):
                        A(hs(part, k, 0), LR[b][:, k, :], ACT.Copy).then_inc(scalar_done, 1)
                        did(scalar_done, ("lh", n, part, k))
                elif kind == "spat":
                    pass
                elif kind == "flog":
                    act.wait_ge(products_done, upto("job", name))
                    act.wait_ge(vector_done, upto("fmin"))
                    FA, FB, FC = (x[0:8, :] for x in FL)
                    A(FB, FA, ACT.Abs).then_inc(scalar_done, 1)
                    did(scalar_done, "fabs")
                    act.wait_ge(scalar_done, so_far(scalar_done))
                    A(FB, FB, ACT.Exp, scale=-1.0).then_inc(scalar_done, 1)
                    did(scalar_done, "fexp")
                    act.wait_ge(scalar_done, so_far(scalar_done))
                    A(FB, FB, ACT.Ln, bias=ONF[0:8, 0:1]).then_inc(scalar_done, 1)
                    did(scalar_done, "fln")
                    act.wait_ge(vector_done, upto("cum"))
                    act.dma_start(CUM, FB).then_inc(cum_stored, 16)
                    did(cum_stored, "cumst", by=16)
                elif kind == "cmean":
                    act.wait_ge(products_done, upto("job", name))
                    A(RST[:, :], bank(name, 0), ACT.Copy, scale=1.0 / 512).then_inc(scalar_done, 1)
                    did(scalar_done, ("cmu", part), ("free", name))
                    for j in range(4):
                        act.wait_ge(vector_done, upto("cc", part, j))
                        for use_before in tm_before(name, j):
                            act.wait_ge(*of("tm", use_before))
                        off = PARTS[part][0]
                        A(tm(name, j), CA[:, j, off:off + HALF], ACT.Square).then_inc(scalar_done, 1)
                        did(scalar_done, ("csq", part, j))
                elif kind == "cvar":
                    off = PARTS[part][0]
                    act.wait_ge(products_done, upto("job", name))
                    act.wait_ge(vector_done, upto("cc", part, 3))
                    A(RST[:, :], bank(name, 0), ACT.Sqrt, scale=1.0 / 512, bias=EPT[:, :]).then_inc(scalar_done, 1)
                    did(scalar_done, ("csd", part), ("free", name))
                    for j in range(4):
                        act.wait_ge(vector_done, upto("cn", part, j))
                        x = CA[:, j, off:off + HALF]
                        A(x, x, ACT.Silu, scale=col("conv_ln_g_2", j), bias=col("conv_ln_b_2", j)).then_inc(scalar_done, 1)
                        did(scalar_done, ("cu", part))
                    act.wait_ge(scalar_done, so_far(scalar_done))
                    act.dma_start(OD[:, 4:8, off:off + HALF], CA[:, :, off:off + HALF]).then_inc(spilled, 16)
                    did(spilled, ("ust", part), by=16)
                elif kind == "out":
                    act.wait_ge(products_done, upto("job", name))
                    off = PARTS[part][0] + e["half"] * 256
                    b = len(outn) % 2
                    if len(outn) >= 2:
                        act.wait_ge(ot_stored[(len(outn) - 2) % 2], upto("outst", len(outn) - 2))
                    dst = OUTS[b][:, :]
                    A(dst, PS[:, 4 * setof[name]:4 * setof[name] + 4, :].rearrange("p b n -> p (b n)"), ACT.Copy).then_inc(scalar_done, 1)
                    did(scalar_done, ("free", name))
                    act.wait_ge(scalar_done, so_far(scalar_done))
                    act.dma_start(a["out"][0][off:off + 256, :].rearrange("(t p) d -> p t d", p=P),
                                  dst.rearrange("p (t d) -> p t d", d=D)).then_inc(ot_stored[b], 16)
                    did(ot_stored[b], ("outst", len(outn)), by=16)
                    outn.append(1)
                elif kind == "attc":
                    for job_before in prev[name]:
                        act.wait_ge(*of("free", job_before))
                    act.wait_ge(products_done, upto("job", ("g", 1, "h1")))
                    tiles = spread("c")
                    for u in range(4 * 33 + 3):
                        s, h = u // 4, u % 4
                        if h == 0 and s % 4 == 0 and s < 32:
                            if s == 0:
                                for j in range(1, 4):
                                    act.wait_ge(*of("tm", (("q", 1, "h1"), 2 * j)))
                                for j in range(1, 4):
                                    act.wait_ge(*of("tm", (("g", 1, "h1"), j)))
                                act.dma_start(SINK[:, :],
                                              a["sink_logit"].rearrange("l h -> (l h)").partition_broadcast(P)).then_inc(late_loaded, 16)
                                did(late_loaded, "sinkm", by=16)
                                act.dma_start(MKF[:, :, :], a["t_mask"]).then_inc(late_loaded, 16)
                                did(late_loaded, "sinkm", by=16)
                                act.wait_ge(late_loaded, upto("sinkm"))
                                A(MKR[:, :, :], MKF[:, :, :], ACT.Copy).then_inc(scalar_done, 1)
                                did(scalar_done, "masks")
                                load_q(act, 0)
                                prep_q_act(0, 0)
                                prep_q_act(0, 1)
                            b = s // 4
                            if b + 1 < 8:
                                load_q(act, b + 1)
                            if b >= 2:
                                act.wait_ge(vector_done, upto("og", b - 2))
                            kv, hf = b // 2, b % 2
                            act.dma_start(GT[b % 2][:, :, :],
                                          GD[:, 2 * kv:2 * kv + 2, hf * HALF:(hf + 1) * HALF]).then_inc(g_loaded[b % 2], 16)
                            did(g_loaded[b % 2], ("gl", b), by=16)
                        if h == 0 and s >= 3 and (s - 3) % 4 == 3:
                            store_o(act, (s - 3) // 4)
                        for z, ti in tiles.get(u, [])[:1]:
                            weights_high(z, ti)
                        if s < 32:
                            i = s % 8
                            lo = 256 if i in (0, 7) else 128
                            src = PS[:, 2 * (u % 2):2 * (u % 2) + 2, :].rearrange("p b n -> p (b n)")[:, lo:769]
                            act.wait_ge(vector_done, upto("mx", "c", u))
                            if s >= 2:
                                act.wait_ge(products_done, upto("tr", "c", tcount(s - 1, "c") - 1))
                            A(PB[s % 2][:, h, lo - 128:641], src, ACT.Exp, scale=-1.0, bias=MX[s % 2][:, h:h + 1],
                              accum_out=SU[s % 2][:, h:h + 1]).then_inc(scalar_done, 1)
                            did(scalar_done, ("exp", "c", u))
                        for z, ti in tiles.get(u, [])[1:]:
                            weights_high(z, ti)
                        if h == 1 and s >= 2:
                            pv_act(s - 2)
                        if h == 3 and s < 32 and s % 4 in (1, 2) and s // 4 + 1 < 8:
                            prep_q_act(s // 4 + 1, s % 4 - 1)
                    store_o(act, 7)
                elif kind == "attf":
                    for job_before in prev[name]:
                        act.wait_ge(scalar_done, upto("free", job_before))
                    act.wait_ge(products_done, upto("job", "flog"))
                    act.wait_ge(cum_stored, upto("cumst"))
                    act.wait_ge(spilled, upto("ust", "h1"))
                    for j in range(1, 4):
                        act.wait_ge(*of("tm", (("v2", "h1"), j)))
                    act.dma_start(MKF2[:, :], a["t_mask"][:, 1, :]).then_inc(late_loaded, 16)
                    did(late_loaded, "mask2l", by=16)
                    act.wait_ge(late_loaded, upto("mask2l"))
                    act.wait_ge(vector_done, upto("cum"))
                    A(MKR2[:, :], MKF2[:, :], ACT.Copy).then_inc(scalar_done, 1)
                    did(scalar_done, "masks2")
                    load_pair(act, 0)
                    load_nb(act, 0)
                    prep2_act(0)
                    prep2v_act(0)
                    load_nb(act, 1)
                    tiles = spread("f")
                    for u in range(4 * 17 + 3):
                        s, i4 = u // 4, u % 4
                        if i4 == 0 and s >= 3 and (s - 3) % 4 == 3:
                            store_o2(act, (s - 3) // 4)
                        if i4 == 0 and s < 16 and s % 2 == 0 and s > 0 and s // 2 + 1 < 8:
                            load_nb(act, s // 2 + 1)
                        for z, j in tiles.get(u, [])[:1]:
                            weights_high2(z, j)
                        if s < 16:
                            n = (4 * (s % 2) + i4 + 1) * P
                            x = PB2[s % 2][:, i4, 0:n]
                            act.wait_ge(vector_done, upto("mx", "f", u))
                            A(x, x, ACT.Exp, scale=-1.0, bias=MX[s % 2][:, i4:i4 + 1],
                              accum_out=SU[s % 2][:, i4:i4 + 1]).then_inc(scalar_done, 1)
                            did(scalar_done, ("exp", "f", u))
                        for z, j in tiles.get(u, [])[1:]:
                            weights_high2(z, j)
                        if i4 == 1 and s >= 2:
                            pv2_act(s - 2)
                        if i4 == 3 and s < 14 and s % 2 == 0:
                            hd = s // 2 + 1
                            if hd % 2 == 0:
                                load_pair(act, hd // 2)
                            prep2_act(hd)
                        if i4 == 3 and s < 14 and s % 2 == 1:
                            prep2v_act(s // 2 + 1)
                    store_o2(act, 3)
            act.wait_ge(ot_stored[(len(outn) - 2) % 2], upto("outst", len(outn) - 2))
            act.wait_ge(ot_stored[(len(outn) - 1) % 2], upto("outst", len(outn) - 1))

        @block.vector
        def _(dve):
            v = nc.vector



            def rope(name, j, off, w):
                dve.wait_ge(scalar_done, upto("kf", name, j))
                dve.wait_ge(tables_loaded, upto("rope"))
                for use_before in tm_before(name, 2 * j + 1):
                    dve.wait_ge(*of("tm", use_before))
                x, y = tm(name, 2 * j, w), tm(name, 2 * j + 1, w)
                v.stream_shuffle(y, x, [(i + 16) % 32 for i in range(32)]).then_inc(vector_done, 1)
                did(vector_done, ("shuf", name, j))
                dve.wait_ge(vector_done, so_far(vector_done))
                v.tensor_tensor(x, x, ROPE[:, 0, off:off + w], ALU.mult).then_inc(vector_done, 1)
                did(vector_done, ("rc1", name, j))
                v.tensor_tensor(y, y, ROPE[:, 1, off:off + w], ALU.mult).then_inc(vector_done, 1)
                did(vector_done, ("rs1", name, j))
                dve.wait_ge(vector_done, so_far(vector_done))
                v.tensor_tensor(x, x, y, ALU.add).then_inc(vector_done, 1)
                did(vector_done, ("kr", name, j), ("tm", (name, 2 * j + 1)))

            def prep_q_dve(b, t):
                dve.wait_ge(scalar_done, upto("qh", b, t))
                x, q, ql = RQ[b % 2][:, t, :], QS[b % 2][0], QS[b % 2][1]
                for half in range(2):
                    own_ = slice(64 * half, 64 * half + 64)
                    for o_ in (slice(0, 64), slice(64, P)):
                        v.tensor_tensor(ql[o_, 2 * t + half, :], x[own_, :], q[own_, 2 * t + half, :].bitcast(F32),
                                            ALU.subtract).then_inc(vector_done, 1)
                        did(vector_done, ("qs", b, t))

            def pv_dve(z):
                b, i = z // 4, z % 4
                dve.wait_ge(scalar_done, upto("ott", z))
                if i == 0 and b >= 2:
                    dve.wait_ge(ot_stored[(b - 2) % 2], upto("ost", "c", b - 2))
                src = PS[:, 6 + z % 2, :].rearrange("p (r e q) -> p e r q", e=2, q=P)
                o_ = OT[b % 2][:, :, i * P:(i + 1) * P]
                v.tensor_tensor(o_[0:64], src[0:64, 0, :, :], OTT[0:64, :, :], ALU.add).then_inc(vector_done, 1)
                did(vector_done, ("ota", z))
                v.tensor_tensor(o_[64:P], src[64:P, 1, :, :], OTT[64:P, :, :], ALU.add).then_inc(vector_done, 1)
                did(vector_done, ("ota", z), ("pvfree", "c", z), ("free", "attc"))
                if i == 3:
                    dve.wait_ge(vector_done, so_far(vector_done))
                    dve.wait_ge(g_loaded[b % 2], upto("gl", b))
                    v.tensor_tensor(OT[b % 2][:, :, :], OT[b % 2][:, :, :], GT[b % 2][:, :, :], ALU.mult).then_inc(vector_done, 1)
                    did(vector_done, ("og", b))

            def prep2_dve(hd):
                b, half = hd % 2, hd % 2
                dve.wait_ge(scalar_done, upto("qh2", hd))
                own_ = slice(64 * half, 64 * half + 64)
                oth = slice(64 - 64 * half, P - 64 * half)
                for o_ in (slice(0, 64), slice(64, P)):
                    v.tensor_tensor(QL2[b][o_, :], RQ2[own_, :], QH2[b][own_, :].bitcast(F32), ALU.subtract).then_inc(vector_done, 1)
                    did(vector_done, ("ql2", hd))
                v.tensor_tensor(KS2[b][oth, :], RK2[own_, :], KS2[b][own_, :].bitcast(F32), ALU.subtract).then_inc(vector_done, 1)
                did(vector_done, ("ql2", hd))

            def prep2v_dve(hd):
                b, half = hd % 2, hd % 2
                dve.wait_ge(scalar_done, upto("vh2", hd))
                v.tensor_tensor(VS2[b][:, :, 64:P], RV2[:, :, 64 * half:64 * half + 64],
                                    VS2[b][:, :, 0:64].bitcast(F32), ALU.subtract).then_inc(vector_done, 1)
                did(vector_done, ("vs2", hd))

            def pv2_dve(z):
                hd, G = z // 2, z % 2
                dve.wait_ge(scalar_done, upto("ott2", z))
                if z % 4 == 0 and hd // 2 >= 2:
                    dve.wait_ge(ot_stored[(hd // 2 - 2) % 2], upto("ost", "f", hd // 2 - 2))
                a_ = slice(0, 64) if hd % 2 == 0 else slice(64, P)
                v.tensor_tensor(OT2[(hd // 2) % 2][a_, G * HALF:(G + 1) * HALF], PS[a_, 6 + z % 2, :], OTT2[a_, :], ALU.add).then_inc(vector_done, 1)
                did(vector_done, ("ota2", z), ("pvfree", "f", z), ("free", "attf"))

            for e in TL:
                kind, name = e["kind"], e["name"]
                part = e.get("part")
                if "vector_done" in counts:
                    dve.wait_ge(vector_done, so_far(vector_done))
                if kind == "small":
                    dve.wait_ge(scalar_done, upto("swh"))
                    dve.wait_ge(scalar_done, upto("smallh"))
                    v.tensor_tensor(SWL[:, :, :].rearrange("p h q -> p (h q)"), bank(name, 0),
                                        SWH[:, :, :].rearrange("p h q -> p (h q)").bitcast(F32), ALU.subtract).then_inc(vector_done, 1)
                    did(vector_done, ("free", name))
                    v.tensor_tensor(CHL[:, :], CHRAW[:, :], CHH[:, :].bitcast(F32), ALU.subtract).then_inc(vector_done, 1)
                    did(vector_done, "small_split")
                elif kind == "adav":
                    vv, n = e["v"], e["n"]
                    for k in range(KT):
                        for x in range(2):
                            if n is not None:
                                w_, cond = e["ws"][k], x
                            else:
                                w_, cond = e["ws"][2 * k + x], 0 if vv < 6 else 2
                            dve.wait_ge(raw_loaded[w_ % RSLOTS], upto("raw", w_))
                            c_, acc, raw = CS[:, k, cond:cond + 1], (SUM, RST)[x][:, :], RAW[:, w_ % RSLOTS, :]
                            if k == 0:
                                v.tensor_scalar(acc, raw, c_, None, ALU.mult).then_inc(vector_done, 1)
                            else:
                                dve.wait_ge(vector_done, upto("ada_acc", vv, n, k - 1, x))
                                v.scalar_tensor_tensor(acc, raw, c_, acc, ALU.mult, ALU.add).then_inc(vector_done, 1)
                            did(vector_done, ("ada_acc", vv, n, k, x), ("rawfree", w_))
                elif kind in ("adac", "adapost"):
                    vv, n = e["v"], e.get("n")
                    if kind == "adapost":
                        name = ("adac", vv, n)
                    dve.wait_ge(products_done, upto("job", name))
                    dve.wait_ge(scalar_done, upto("pc"))
                    ab = cols("ada_b", vv * 8, 8) if vv < 6 else cols("ada_b_2", (vv - 6) * 8, 8)
                    src = bank(name, 0)[:, 0:16].rearrange("p (k c) -> p c k", c=2)
                    ks = slice(0, KT) if n is None else slice(4 * n, 4 * n + 4)
                    for c_ in range(2 if kind == "adac" or n is not None else 1):
                        v.tensor_tensor(MOD[:, vv, c_, ks], src[:, c_, ks], ab[:, ks], ALU.add).then_inc(vector_done, 1)
                        did(vector_done, ("mod", vv), ("free", name))
                    if n == 0:
                        continue
                    dve.wait_ge(vector_done, so_far(vector_done))
                    if vv in (1, 4):
                        l = vv // 3
                        for c_ in range(2):
                            v.scalar_tensor_tensor(CO[:, 2 * l + c_, :], MOD[:, vv, c_, :], 1.0,
                                                       cols("norm_g", l * 8, 8), ALU.add, ALU.mult).then_inc(vector_done, 1)
                            did(vector_done, ("coef", l))
                    if vv == 7:
                        v.scalar_tensor_tensor(CO[:, 4, :], MOD[:, vv, 0, :], 1.0, cols("mix_pre_g_2"),
                                                   ALU.add, ALU.mult).then_inc(vector_done, 1)
                        did(vector_done, ("coefa", 2))
                        dve.wait_ge(vector_done, so_far(vector_done))
                        v.tensor_tensor(CO[:, 4, :], CO[:, 4, :], cols("final_g"), ALU.mult).then_inc(vector_done, 1)
                        did(vector_done, ("coef", 2))
                    if vv == 10:
                        v.scalar_tensor_tensor(CO[:, 5, :], MOD[:, vv, 0, :], 1.0, cols("ffn_pre_g_2"),
                                                   ALU.add, ALU.mult).then_inc(vector_done, 1)
                        did(vector_done, ("coef", 4))
                    if vv == 8:
                        v.tensor_tensor(CO[:, 6, :], MOD[:, 8, 0, :], cols("mix_post_g_2"), ALU.mult).then_inc(vector_done, 1)
                        did(vector_done, ("gate", 3))
                    if vv == 11:
                        v.tensor_tensor(CO[:, 7, :], MOD[:, 11, 0, :], cols("ffn_post_g_2"), ALU.mult).then_inc(vector_done, 1)
                        did(vector_done, ("gate", 5))
                elif kind == "sum":
                    n = e["n"]
                    w = PARTS[part][1]
                    for k in range(1, KT):
                        dve.wait_ge(scalar_done, upto("sq", n, part, k))
                        in1 = tm(name, 0, w) if k == 1 else SUM[:, 0:w]
                        v.tensor_tensor(SUM[:, 0:w], tm(name, k, w), in1, ALU.add).then_inc(vector_done, 1)
                        did(vector_done, ("sum", n, part),
                            ("tm", (name, k)), *([("tm", (name, 0))] if k == 1 else []))
                        dve.wait_ge(vector_done, so_far(vector_done))
                    if n == 2:
                        for k in range(1, KT):
                            dve.wait_ge(scalar_done, upto("sqg", n, part, k))
                            in1 = tm(name, 8, w) if k == 1 else RST[:, 0:w]
                            v.tensor_tensor(RST[:, 0:w], tm(name, 8 + k, w), in1, ALU.add).then_inc(vector_done, 1)
                            did(vector_done, ("sumg", n, part),
                                ("tm", (name, 8 + k)), *([("tm", (name, 8))] if k == 1 else []))
                            dve.wait_ge(vector_done, so_far(vector_done))
                elif kind in ("stat", "statpost"):
                    n = e["n"]
                    w = PARTS[part][1]
                    if n == 2:
                        dve.wait_ge(scalar_done, upto("sq1", n, part))
                        v.reciprocal(SUM[:, 0:w], SUM[:, 0:w]).then_inc(vector_done, 1)
                        did(vector_done, ("r1", n, part))
                        dve.wait_ge(vector_done, so_far(vector_done))
                        for use_before in tm_before(name, 0):
                            dve.wait_ge(vector_done, upto("tm", use_before))
                        t_ = tm(name, 0, w)
                        v.tensor_tensor(t_, bank(("stat", n, part), 1, w), SUM[:, 0:w], ALU.mult).then_inc(vector_done, 1)
                        did(vector_done, ("free", ("stat", n, part)))
                        dve.wait_ge(vector_done, so_far(vector_done))
                        v.tensor_tensor(t_, t_, SUM[:, 0:w], ALU.mult).then_inc(vector_done, 1)
                        did(vector_done, ("r1sq", n, part))
                        dve.wait_ge(scalar_done, upto("sqrt", n, part))
                        v.reciprocal(RST[:, 0:w], RST[:, 0:w]).then_inc(vector_done, 1)
                        did(vector_done, ("r2", n, part))
                        dve.wait_ge(vector_done, so_far(vector_done))
                        v.tensor_tensor(RST[:, 0:w], RST[:, 0:w], SUM[:, 0:w], ALU.mult).then_inc(vector_done, 1)
                        did(vector_done, ("rstd", n, part))
                    else:
                        dve.wait_ge(scalar_done, upto("sqrt", n, part))
                        r_ = RST0[part] if n == 0 else RST
                        v.reciprocal(r_[:, 0:w], r_[:, 0:w]).then_inc(vector_done, 1)
                        did(vector_done, ("rstd", n, part))
                    dve.wait_ge(vector_done, so_far(vector_done))
                elif kind == "apply":
                    n = e["n"]
                    w = PARTS[part][1]

                    def lo(k):
                        dve.wait_ge(scalar_done, upto("hi", n, part, k))
                        v.tensor_tensor(hs(part, k, 1), tm(name, k, w), hs(part, k, 0).bitcast(F32), ALU.subtract).then_inc(vector_done, 1)
                        did(vector_done, ("H", "apply", n, part, k), ("tm", (name, k)))

                    for k in range(KT):
                        for use_before in tm_before(name, k):
                            dve.wait_ge(*of("tm", use_before))
                        v.tensor_tensor(tm(name, k, w), xs(part, k), (RST0[part] if n == 0 else RST)[:, 0:w], ALU.mult).then_inc(vector_done, 1)
                        did(vector_done, ("t", n, part, k))
                        if k >= 2:
                            lo(k - 2)
                    lo(KT - 2)
                    lo(KT - 1)
                    if n == 2:
                        for k in range(KT):
                            v.scalar_tensor_tensor(xs(part, k), xs(part, k), col("final_g", k), SUM[:, 0:w],
                                                       ALU.mult, ALU.mult).then_inc(vector_done, 1)
                            did(vector_done, ("XW", 2))
                        if part == "h1":
                            v.memset(U[:, :, 0:TAPS - 1], 0.0).then_inc(vector_done, 1)
                            did(vector_done, "upad")
                elif kind in ("lin", "tok", "kv"):
                    layer, group = e["layer"], e["group"]
                    off, w = PARTS[part]
                    if layer == "ab" and group == "xb":
                        dve.wait_ge(products_done, upto("job", name))
                        for g in range(4):
                            dve.wait_ge(scalar_done, upto("vbh", part, g))
                            v.tensor_tensor(VBL[:, g, 0:w], bank(name, g, w), VBH[:, g, 0:w].bitcast(F32), ALU.subtract).then_inc(vector_done, 1)
                            did(vector_done, ("xbs", part), ("free", name))
                    elif layer == "ab" and group == "ga":
                        for j in range(4):
                            dve.wait_ge(scalar_done, upto("gasilu", part, j))
                            dve.wait_ge(scalar_done, upto("u", part))
                            x = xs(part, j)
                            v.tensor_tensor(x, x, tm(name, j, w), ALU.mult).then_inc(vector_done, 1)
                            did(vector_done, ("ug", part), ("tm", (name, j)))
                    elif layer == "ab" and group == "v":
                        dve.wait_ge(products_done, upto("job", name))
                        nt = w // P
                        for tb in range(nt):
                            v.bn_stats(BST[:, tb, :], bank(name, tb)).then_inc(vector_done, 1)
                            did(vector_done, ("bs", part, tb))
                        for tb in range(nt):
                            dve.wait_ge(vector_done, upto("bs", part, tb))
                            v.bn_aggr(MV[:, tb, :], BST[:, tb, :]).then_inc(vector_done, 1)
                            did(vector_done, ("mv", part))
                        dve.wait_ge(scalar_done, upto("vsd", part))
                        v.reciprocal(SM[:, 8:8 + nt], SM[:, 0:nt]).then_inc(vector_done, 1)
                        did(vector_done, ("vr", part))
                        dve.wait_ge(vector_done, so_far(vector_done))
                        for tb in range(nt):
                            for use_before in tm_before(name, tb):
                                dve.wait_ge(*of("tm", use_before))
                            if tb == 0 and part != "h0":
                                dve.wait_ge(products_done, upto("job", ("spat", {"h1": "h0", "c": "h1"}[part])))
                            if tb == 0 and part == "h0":
                                dve.wait_ge(products_done, upto("job", ("chan", "c", 0)))
                            v.tensor_scalar(tm(name, tb), bank(name, tb), MV[:, tb, 0:1], SM[:, 8 + tb:9 + tb],
                                                ALU.subtract, ALU.mult).then_inc(vector_done, 1)
                            did(vector_done, ("vf", part, tb), ("free", name))
                            dve.wait_ge(scalar_done, upto("vh", part, tb))
                            v.tensor_tensor(VBL[:, tb, :], tm(name, tb), VBH[:, tb, :].bitcast(F32), ALU.subtract).then_inc(vector_done, 1)
                            did(vector_done, ("vn", part, tb), ("tm", (name, tb)))
                    elif layer in ("abo", "co"):
                        dve.wait_ge(products_done, upto("job", name))
                        n = 1 if layer == "abo" else 2
                        dve.wait_ge(x_loaded, upto("reload", n - 1))
                        dve.wait_ge(vector_done, upto("mod", 2 if n == 1 else 5))
                        for j in range(4):
                            k = group * 4 + j
                            x = xs(part, k)
                            v.scalar_tensor_tensor(x, bank(name, j, w), mod(2 if n == 1 else 5, part, k), x,
                                                       ALU.mult, ALU.add).then_inc(vector_done, 1)
                            did(vector_done, ("X", n, part, k), ("free", name), ("XW", n))
                    elif layer == "c" and group == "kv":
                        dve.wait_ge(products_done, upto("job", name))
                        per = 1 if part == "c" else 2
                        c0 = T if part == "c" else off
                        for j in range(2):
                            if part != "c":
                                rope(name, j, off, w)
                            src = tm(name, per * j, w)
                            dve.wait_ge(scalar_done, upto("khi", part, j, 1))
                            v.tensor_tensor(KS[64:P, 2 * j, c0:c0 + w], src[0:64, :],
                                                KS[0:64, 2 * j, c0:c0 + w].bitcast(F32), ALU.subtract).then_inc(vector_done, 1)
                            did(vector_done, ("klo", part, j))
                            v.tensor_tensor(KS[0:64, 2 * j + 1, c0:c0 + w], src[64:P, :],
                                                KS[64:P, 2 * j + 1, c0:c0 + w].bitcast(F32), ALU.subtract).then_inc(vector_done, 1)
                            did(vector_done, ("tm", (name, per * j)))
                        for tb in range(0, w // P, 2):
                            b = (8 if part == "c" else off // P) + tb
                            dve.wait_ge(scalar_done, upto("vhi", part, tb))
                            src = bank(name, 2 + tb // 2).rearrange("p (t h d) -> p t h d", d=64, h=4)
                            v.tensor_tensor(VS[:, b:b + 2, :, 64:P], src, VS[:, b:b + 2, :, 0:64].bitcast(F32),
                                                ALU.subtract).then_inc(vector_done, 1)
                            did(vector_done, ("free", name))
                    elif layer == "c" and group[0] == "q":
                        for j in range(4):
                            rope(name, j, off, w)
                    elif layer == "b2" and group == "cg":
                        for j in range(4):
                            dve.wait_ge(scalar_done, upto("gasilu", name, j))
                            dve.wait_ge(scalar_done, upto("uv", part))
                            x = U[:, j, 30 + off:30 + off + w]
                            v.tensor_tensor(x, x, tm(name, j, w), ALU.mult).then_inc(vector_done, 1)
                            did(vector_done, ("ug2", part), ("tm", (name, j)))
                    elif layer == "fi":
                        ch = group
                        for j in range(2):
                            dve.wait_ge(scalar_done, upto("gsl", ch, part, j))
                            v.tensor_tensor(tm(name, j), bank(name, 2 + j), tm(name, j), ALU.mult).then_inc(vector_done, 1)
                            did(vector_done, ("av", ch, part, j), ("free", name))
                        for j in range(2):
                            dve.wait_ge(scalar_done, upto("ahi", ch, part, j))
                            v.tensor_tensor(AHL[:, j, off:off + w], tm(name, j), AHH[:, j, off:off + w].bitcast(F32),
                                                ALU.subtract).then_inc(vector_done, 1)
                            did(vector_done, ("A", ch, part, j), ("tm", (name, j)))
                    elif layer == "fo" and e["ch"] > 0:
                        dve.wait_ge(products_done, upto("job", name))
                        dve.wait_ge(scalar_done, upto("yacc", group, part))
                        y = Y[:, group * 4:group * 4 + 4, off:off + w]
                        if e["ch"] > 1:
                            dve.wait_ge(vector_done, upto("yadd", e["ch"] - 1, group, part))
                        v.tensor_tensor(y, PS[:, 4 * setof[name]:4 * setof[name] + 4, 0:w], y, ALU.add).then_inc(vector_done, 1)
                        did(vector_done, ("yadd", e["ch"], group, part),
                            ("free", name), *[("X", 5, part, group * 4 + j) for j in range(4)])
                elif kind == "spat":
                    dve.wait_ge(products_done, upto("job", name))
                    nt = PARTS[part][1] // P
                    w = nt * P
                    for h in range(4):
                        for use_before in tm_before(name, h):
                            dve.wait_ge(vector_done, upto("tm", use_before))
                        t_ = tm(name, h, w).rearrange("p (t q) -> p t q", q=P)
                        src = bank(name, h, w).rearrange("p (t q) -> p t q", q=P)
                        sb = SBB[:, h:h + 1, :].broadcast_to([P, nt, P])
                        v.scalar_tensor_tensor(t_, src, col("v_norm_g", h), sb, ALU.mult, ALU.add).then_inc(vector_done, 1)
                        did(vector_done, ("free", name), ("sv", part, h))
                        dve.wait_ge(vector_done, so_far(vector_done))
                        x = xs(part, h)
                        v.tensor_tensor(x, x, tm(name, h, w), ALU.mult).then_inc(vector_done, 1)
                        did(vector_done, ("ya", part), ("tm", (name, h)))
                elif kind == "abload":
                    a_ = e["a"]
                    for x in range(2):
                        dve.wait_ge(ab_loaded[x], upto("abl", a_, x))
                        dve.wait_ge(products_done, upto("job", ("gb", "c")))
                    if a_ == "c":
                        for x in range(2):
                            dve.wait_ge(scalar_done, upto("abh", a_, x))
                            hh, hl = (t_[:, :, :].rearrange("p k c -> p (k c)")[:, x * D:(x + 1) * D] for t_ in (HCH, HCL))
                            v.tensor_tensor(hl, ARAW[:, x, :], hh.bitcast(F32), ALU.subtract).then_inc(vector_done, 1)
                            did(vector_done, ("AB", "c"))
                    else:
                        for x, op in enumerate((ALU.add, ALU.subtract)):
                            if a_ == 0:
                                dve.wait_ge(products_done, upto("job", ("spat", "c")))
                            v.tensor_tensor(ASD[:, x, :], ARAW[:, 0, :], ARAW[:, 1, :], op).then_inc(vector_done, 1)
                            did(vector_done, ("abs", a_, x))
                        for x in range(2):
                            dve.wait_ge(scalar_done, upto("abh", a_, x))
                            v.tensor_tensor(HXL[:, a_ + 4 * x, :], ASD[:, x, :], HXH[:, a_ + 4 * x, :].bitcast(F32),
                                                ALU.subtract).then_inc(vector_done, 1)
                            did(vector_done, ("AB", a_ + 4 * x), ("abr", a_))
                        dve.wait_ge(vector_done, so_far(vector_done))
                elif kind == "dft":
                    dve.wait_ge(products_done, upto("job", name))
                    dve.wait_ge(scalar_done, upto("gb", "h0"))
                    dve.wait_ge(scalar_done, upto("gb", "h1"))
                    y = XX[:, 4:8, e["odd"]:T:2]
                    v.tensor_tensor(y, PS[:, 4 * setof[name]:4 * setof[name] + 4, :], y, ALU.mult).then_inc(vector_done, 1)
                    did(vector_done, ("yb", e["odd"]), ("free", name))
                elif kind == "dftc":
                    dve.wait_ge(products_done, upto("job", name))
                    dve.wait_ge(scalar_done, upto("gb", "c"))
                    y = XC[:, 4:8, :]
                    v.tensor_tensor(y, PS[:, 4 * setof[name]:4 * setof[name] + 4, 0:C], y, ALU.mult).then_inc(vector_done, 1)
                    did(vector_done, ("yb", "c"), ("free", name))
                elif kind == "ysplit":
                    for k in range(KT):
                        dve.wait_ge(scalar_done, upto("yh", part, k))
                        v.tensor_tensor(hs(part, k, 1), xs(part, k), hs(part, k, 0).bitcast(F32), ALU.subtract).then_inc(vector_done, 1)
                        did(vector_done, ("H", "ysplit", 0, part, k))
                elif kind == "hload":
                    n = e["n"]
                    b = 0 if part == "h0" else 1
                    for k in range(KT):
                        dve.wait_ge(scalar_done, upto("lh", n, part, k))
                        v.tensor_tensor(hs(part, k, 1), LR[b][:, k, :], hs(part, k, 0).bitcast(F32), ALU.subtract).then_inc(vector_done, 1)
                        did(vector_done, ("H", "hload", n, part, k))
                elif kind == "resid":
                    n = e["n"]
                    off, w = PARTS[part]
                    dve.wait_ge(vector_done, upto("gate", n))
                    dve.wait_ge(x_loaded, upto("reload", 2))
                    for k in range(KT):
                        for use_before in tm_before(name, k):
                            dve.wait_ge(vector_done, upto("tm", use_before))
                        v.tensor_tensor(tm(name, k), ys(part, k), RST[:, :], ALU.mult).then_inc(vector_done, 1)
                        did(vector_done, ("rt", n, part, k))
                        dve.wait_ge(vector_done, so_far(vector_done))
                        x = xs(part, k)
                        v.scalar_tensor_tensor(x, tm(name, k), CO[:, 6 if n == 3 else 7, k:k + 1], x, ALU.mult, ALU.add).then_inc(vector_done, 1)
                        did(vector_done, ("X", 4, part, k) if n == 3 else ("xfin", part, k), ("tm", (name, k)))
                elif kind == "conv":
                    i = e["i"]
                    if i == 0:
                        dve.wait_ge(vector_done, upto("ug2", "h0"))
                        dve.wait_ge(vector_done, upto("ug2", "h1"))
                        dve.wait_ge(spilled, upto("spill", 2))
                    per = -(-4 * TAPS // 6)
                    for z in range(i * per, min((i + 1) * per, 4 * TAPS)):
                        j, t_ = z // TAPS, z % TAPS
                        wc = PC[:, 256 + 4 * t_ + j:257 + 4 * t_ + j]
                        src = U[:, j, t_:t_ + T]
                        if t_ == 0:
                            v.tensor_scalar(CA[:, j, :], src, wc, col("conv_b_2", j), ALU.mult, ALU.add).then_inc(vector_done, 1)
                            did(vector_done, ("conv", j))
                        else:
                            dve.wait_ge(vector_done, so_far(vector_done))
                            v.scalar_tensor_tensor(CA[:, j, :], src, wc, CA[:, j, :], ALU.mult, ALU.add).then_inc(vector_done, 1)
                            did(vector_done, ("conv", j))
                elif kind == "flog":
                    dve.wait_ge(products_done, upto("job", name))
                    dve.wait_ge(vector_done, so_far(vector_done))
                    FA, FB, FC = (x[0:8, :] for x in FL)
                    dve.wait_ge(rows_loaded, upto("rows"))
                    src = PS[0:8, 4 * setof[name]:4 * setof[name] + 2, :].rearrange("p b n -> p (b n)")
                    v.tensor_scalar(FA, src, SM[0:8, 48:49], None, ALU.add).then_inc(vector_done, 1)
                    did(vector_done, "fz", ("free", name))
                    dve.wait_ge(vector_done, so_far(vector_done))
                    v.tensor_scalar(FC, FA, 0.0, None, ALU.min).then_inc(vector_done, 1)
                    did(vector_done, "fmin")
                    dve.wait_ge(scalar_done, upto("fln"))
                    v.tensor_tensor(FC, FC, FB, ALU.subtract).then_inc(vector_done, 1)
                    did(vector_done, "logf")
                    v.memset(FA, 1.0).then_inc(vector_done, 1)
                    did(vector_done, "f1")
                    dve.wait_ge(vector_done, so_far(vector_done))
                    v.tensor_tensor_scan(FB, FA, FC, 0.0, ALU.mult, ALU.add).then_inc(vector_done, 1)
                    did(vector_done, "cum")
                elif kind == "cmean":
                    off = PARTS[part][0]
                    for j in range(1, 4):
                        dve.wait_ge(vector_done, so_far(vector_done))
                        x = CA[:, j, off:off + HALF]
                        in1 = CA[:, 0, off:off + HALF] if j == 1 else SUM[:, :]
                        if j == 1 and part == "h1":
                            dve.wait_ge(products_done, upto("job", ("cvar", "h0")))
                        v.tensor_tensor(SUM[:, :], x, in1, ALU.add).then_inc(vector_done, 1)
                        did(vector_done, ("cmean_sum", part))
                    dve.wait_ge(scalar_done, upto("cmu", part))
                    for j in range(4):
                        x = CA[:, j, off:off + HALF]
                        v.tensor_tensor(x, x, RST[:, :], ALU.subtract).then_inc(vector_done, 1)
                        did(vector_done, ("cc", part, j))
                    for j in range(1, 4):
                        dve.wait_ge(scalar_done, upto("csq", part, j))
                        in1 = tm(name, 0) if j == 1 else SUM[:, :]
                        v.tensor_tensor(SUM[:, :], tm(name, j), in1, ALU.add).then_inc(vector_done, 1)
                        did(vector_done, ("cvar_sum", part),
                            ("tm", (name, j)), *([("tm", (name, 0))] if j == 1 else []))
                        dve.wait_ge(vector_done, so_far(vector_done))
                elif kind == "cvar":
                    off = PARTS[part][0]
                    dve.wait_ge(scalar_done, upto("csd", part))
                    v.reciprocal(RST[:, :], RST[:, :]).then_inc(vector_done, 1)
                    did(vector_done, ("crs", part))
                    dve.wait_ge(vector_done, so_far(vector_done))
                    for j in range(4):
                        x = CA[:, j, off:off + HALF]
                        v.tensor_tensor(x, x, RST[:, :], ALU.mult).then_inc(vector_done, 1)
                        did(vector_done, ("cn", part, j))
                elif kind == "attc":
                    dve.wait_ge(late_loaded, upto("sinkm"))
                    v.tensor_scalar(NSK[:, :], SINK[:, :], -1.0, None, ALU.mult).then_inc(vector_done, 1)
                    did(vector_done, "nsk")
                    dve.wait_ge(vector_done, so_far(vector_done))
                    prep_q_dve(0, 0)
                    prep_q_dve(0, 1)
                    tiles = spread("c")
                    for u in range(4 * 33 + 4):
                        s, h = u // 4, u % 4
                        if 1 <= u <= 128:
                            y, b, hh = u - 1, (u - 1) // 4 % 2, (u - 1) % 4
                            dve.wait_ge(scalar_done, upto("exp", "c", y))
                            if y >= 8:
                                dve.wait_ge(gpsimd_done, upto("P", "c", y // 4 - 2, hh))
                            v.reciprocal(RC[b][:, hh:hh + 1], SU[b][:, hh:hh + 1]).then_inc(vector_done, 1)
                            did(vector_done, ("rc", "c", y))
                        if s < 32:
                            i = s % 8
                            lo_ = 256 if i in (0, 7) else 128
                            src = PS[:, 2 * (u % 2):2 * (u % 2) + 2, :].rearrange("p b n -> p (b n)")[:, lo_:769]
                            dve.wait_ge(products_done, upto("sc", "c", u))
                            v.tensor_reduce(MX[s % 2][:, h:h + 1], src, AX.X, ALU.min).then_inc(vector_done, 1)
                            did(vector_done, ("mx", "c", u))
                        for z, ti in tiles.get(u, []):
                            tb = tcount(z, "c") + ti
                            dve.wait_ge(scalar_done, upto("pth", "c", tb))
                            p_ = key_blocks(z)[ti]
                            v.tensor_tensor(PTL[:, p_, :], PS[:, 4 + tb % 2, :], PTH[:, p_, :].bitcast(F32),
                                            ALU.subtract).then_inc(vector_done, 1)
                            did(vector_done, ("ptl", "c", tb))
                        if h == 2 and s >= 2:
                            pv_dve(s - 2)
                        if h == 0 and s < 32 and (s - 1) % 4 in (1, 2) and s // 4 + 1 < 8:
                            prep_q_dve(s // 4 + 1, (s - 1) % 4 - 1)
                elif kind == "attf":
                    prep2_dve(0)
                    prep2v_dve(0)
                    tiles = spread("f")
                    for u in range(4 * 17 + 4):
                        s, i4 = u // 4, u % 4
                        if 1 <= u <= 64:
                            y, b, hh = u - 1, (u - 1) // 4 % 2, (u - 1) % 4
                            dve.wait_ge(scalar_done, upto("exp", "f", y))
                            if y >= 8:
                                dve.wait_ge(gpsimd_done, upto("P", "f", y // 4 - 2, hh))
                            v.reciprocal(RC[b][:, hh:hh + 1], SU[b][:, hh:hh + 1]).then_inc(vector_done, 1)
                            did(vector_done, ("rc", "f", y))
                        if s < 16:
                            hd = s // 2
                            n = (4 * (s % 2) + i4 + 1) * P
                            src = PS[:, 2 * (u % 2):2 * (u % 2) + 2, :].rearrange("p b n -> p (b n)")[:, 0:n]
                            dve.wait_ge(products_done, upto("sc", "f", u))
                            dve.wait_ge(nb_loaded[hd % 2], upto("nbl", hd))
                            if s >= 2:
                                dve.wait_ge(products_done, upto("tr", "f", tcount(s - 1, "f") - 1))
                            v.tensor_tensor_reduce(out=PB2[s % 2][:, i4, 0:n], in0=src, in1=NBC[hd % 2][:, 0:n],
                                                   scale=1.0, scalar=3e38, op0=ALU.add, op1=ALU.min,
                                                   accum_out=MX[s % 2][:, i4:i4 + 1]).then_inc(vector_done, 1)
                            did(vector_done, ("mx", "f", u))
                        for z, j in tiles.get(u, []):
                            tb = tcount(z, "f") + j
                            c0 = max(0, j - 4 * (z % 2)) * P
                            dve.wait_ge(scalar_done, upto("pth", "f", tb))
                            v.tensor_tensor(PT2L[:, j, c0:HALF], PS[:, 4 + tb % 2, c0:HALF],
                                            PT2H[:, j, c0:HALF].bitcast(F32), ALU.subtract).then_inc(vector_done, 1)
                            did(vector_done, ("ptl", "f", tb))
                        if i4 == 2 and s >= 2:
                            pv2_dve(s - 2)
                        if i4 == 0 and s < 15 and s % 2 == 1:
                            prep2_dve(s // 2 + 1)
                        if i4 == 0 and 2 <= s < 15 and s % 2 == 0:
                            prep2v_dve(s // 2)
    return nc


INPUTS = ["x", "c", "ctx", "c_ctx", "norm_g", "ada_w", "ada_b", "w_in_ab", "v_norm_g", "spatial_w", "spatial_b",
          "w_out_ab", "w_in_c", "sink_logit", "w_out_c", "final_g", "c_2", "w_in_2", "b_f_2", "conv_w_2", "conv_b_2",
          "conv_ln_g_2", "conv_ln_b_2", "w_o_2", "w_ffn_in_2", "w_ffn_out_2", "mix_pre_g_2", "mix_post_g_2",
          "ffn_pre_g_2", "ffn_post_g_2", "ada_w_2", "ada_b_2"]


def build(nc, arrays, old):
    a = {n[3:]: nc.dram_tensor(n, x.shape, mybir.dt.from_np(x.dtype), kind="ExternalInput").ap()
         for n, x in arrays.items()}
    a["out"] = nc.dram_tensor("out_y", (1, T, D), F32, kind="ExternalOutput").ap()
    marks = {}
    program(nc, a, marks, old)
    return marks


def kernel(**inputs):
    import concourse.bacc as bacc
    from concourse.bass_utils import run_bass_kernel_spmd

    arrays = {f"in_{n}": np.ascontiguousarray(inputs[n]) for n in INPUTS}
    arrays.update({f"in_{n}": x for n, x in shape_tables().items()})
    counted = build(bacc.Bacc("TRN2", target_bir_lowering=False, num_devices=1), arrays, {})
    nc = bacc.Bacc("TRN2", target_bir_lowering=False, num_devices=1)
    build(nc, arrays, counted)
    r = run_bass_kernel_spmd(nc, [arrays], core_ids=[0])
    return r.results[0]["out_y"]
```

```python
import math
from contextlib import ExitStack

import numpy as np

import concourse.bass as bass
from concourse import mybir

F32 = mybir.dt.float32
F32R = mybir.dt.float32r
ALU = mybir.AluOpType
ACT = mybir.ActivationFunctionType
AX = mybir.AxisListType

P = 128
D = 1024
KT = D // P
T = 1024
C = 256
HALF = 512
NB_T = T // P
EPS = 1e-6
NEG = -1e30
SCALE = 0.125
HID = 2816
TAPS = 31
EARLY_TAPS = 16
CONV_SHARES = {0: range(0, 10), 2: range(10, 20), 4: range(20, TAPS)}
WSLOTS, RSLOTS = 8, 4
PARTS = {"h0": (0, 512), "h1": (512, 512), "c": (0, 256)}

ROWS = {}
_at = 0
for _name, _n in (("norm_g", 16), ("ada_b", 48), ("c", 8), ("c_ctx", 8), ("c_2", 8), ("v_norm_g", 4),
                  ("final_g", 8), ("conv_b_2", 4), ("conv_ln_g_2", 4), ("conv_ln_b_2", 4),
                  ("mix_pre_g_2", 8), ("mix_post_g_2", 8),
                  ("ffn_pre_g_2", 8), ("ffn_post_g_2", 8), ("ada_b_2", 48)):
    ROWS[_name] = (_at, _n)
    _at += _n
ROWS["conv_w_2"] = (256, TAPS * 4)


def shape_tables():
    k = np.arange(512)
    l = np.arange(512)
    s = 1.0 / math.sqrt(T * P)
    slots = []
    for odd in (0, 1):
        ang = 2 * np.pi * ((l[:, None] * (2 * k[None, :] + odd)) % T) / T
        cs, sn = np.cos(ang) * s, -np.sin(ang) * s
        for kt in range(4):
            slots += [cs[kt * P:(kt + 1) * P], sn[kt * P:(kt + 1) * P]]
    n = np.arange(C)
    ang = 2 * np.pi * ((n[:, None] * n[None, :]) % C) / C
    s = 1.0 / math.sqrt(C * P)
    both = np.concatenate([np.cos(ang) * s, -np.sin(ang) * s], axis=1)
    slots += [both[:P], both[P:]]
    n = np.arange(P)
    ang = 2 * np.pi * ((n[:, None] * n[None, :]) % P) / P
    chan = np.concatenate([np.cos(ang), np.sin(ang)], axis=1)
    inv = 10000.0 ** (-np.arange(16, dtype=np.float32) / 16)
    t = np.arange(T)
    pos = np.where((np.arange(P) % 64 < 32)[:, None], (t // 64)[None, :], (t % 64)[None, :]).astype(np.float32)
    ang = (pos * inv.astype(np.float32)[np.arange(P) % 16][:, None]).astype(np.float32).astype(np.float64)
    sign = np.where(np.arange(P) % 32 < 16, -1.0, 1.0)[:, None]
    q, m = np.arange(P)[:, None], np.arange(P)[None, :]
    left = np.where(m >= q, 0.0, -NEG)
    right = np.where(m <= q, 0.0, -NEG)
    f = np.float32
    return {
        "t_ident": np.eye(P, dtype=f),
        "t_dft": np.stack(slots).astype(f),
        "t_chan": chan.astype(f),
        "t_rope": np.stack([np.cos(ang), np.sin(ang) * sign], axis=1).astype(f),
        "t_mask": np.stack([left, right], axis=1).astype(f),
    }


def plan():
    tl, slots = [], []

    def slot(kind, src, job):
        slots.append((kind, src, job))
        return len(slots) - 1

    def lin(name, layer, group, part, ws, kts=KT, kind="lin", mid=None, last=False, h="H", **kw):
        tl.append(dict(kind=kind, name=name, layer=layer, group=group, part=part, ws=ws, kts=kts,
                       mid=mid, last=last, h=h, **kw))

    def weights(layer, group, kts=KT):
        return [slot("split", (layer, group, k), None) for k in range(kts)]

    def ada(v):
        ws = [slot("raw", ("ada", v, k, n), None) for k in range(KT) for n in range(2)]
        tl.append(dict(kind="ada", name=("ada", v), v=v, ws=ws))
        tl.append(dict(kind="adac", name=("adac", v), v=v))

    def ev(kind, name, **kw):
        tl.append(dict(kind=kind, name=name, **kw))

    def ada_beside(*vs):
        return [(v, k, x, slot("raw", ("ada", v, k, x), None)) for v in vs for k in range(KT) for x in range(2)]

    def adav(v, n):
        ws = [slot("raw", ("ada", v, k, n), None) for k in range(KT)]
        ev("adav", ("adav", v, n), v=v, n=n, ws=ws)

    ev("params", "params")
    for k in range(KT):
        ev("tx", ("tx", k), k=k)
    ev("sum", ("sum", 0, "h0"), n=0, part="h0")
    ada(0)
    ev("stat", ("stat", 0, "h0"), n=0, part="h0")
    ev("sum", ("sum", 0, "h1"), n=0, part="h1")
    ada(1)
    ev("stat", ("stat", 0, "h1"), n=0, part="h1")
    ev("sum", ("sum", 0, "c"), n=0, part="c")
    ev("small", "small")
    ev("stat", ("stat", 0, "c"), n=0, part="c")
    for p in ("h0", "h1", "c"):
        ev("apply", ("apply", 0, p), n=0, part=p)
    ev("spill", ("spill", 0), n=0)
    x3 = ("h0", "h1", "c")

    def chans(p):
        for half in range(2 if p != "c" else 1):
            ev("chan", ("chan", p, half), part=p, half=half)

    w = weights("ab", "xb")
    lin(("xb", "h0"), "ab", "xb", "h0", w, last=True)
    w = weights("ab", "u")
    lin(("u", "h0"), "ab", "u", "h0", w, last=True)
    chans("h0")
    w = weights("ab", "xb")
    adav(2, 0)
    lin(("xb", "h1"), "ab", "xb", "h1", w, last=True)
    w = weights("ab", "u")
    ev("adapost", ("adapost", 2, 0), v=2, n=0)
    lin(("u", "h1"), "ab", "u", "h1", w, mid=("adac", 2, 0))
    chans("h1")
    lin(("u", "c"), "ab", "u", "c", w, last=True)
    w = weights("ab", "xb")
    adav(2, 1)
    lin(("xb", "c"), "ab", "xb", "c", w, last=True)
    chans("c")
    w = weights("ab", "v")
    ev("adapost", ("adapost", 2, 1), v=2, n=1)
    lin(("v", "h0"), "ab", "v", "h0", w, last=True, kind="tok", mid=("adac", 2, 1))
    w = weights("ab", "ga")
    adav(3, 0)
    lin(("ga", "h0"), "ab", "ga", "h0", w, last=True)
    ev("spat", ("spat", "h0"), part="h0")
    w = weights("ab", "v")
    ev("adapost", ("adapost", 3, 0), v=3, n=0)
    lin(("v", "h1"), "ab", "v", "h1", w, last=True, kind="tok", mid=("adac", 3, 0))
    w = weights("ab", "ga")
    adav(3, 1)
    lin(("ga", "h1"), "ab", "ga", "h1", w)
    ev("spat", ("spat", "h1"), part="h1")
    lin(("ga", "c"), "ab", "ga", "c", w, last=True)
    w = weights("ab", "v")
    ev("adapost", ("adapost", 3, 1), v=3, n=1)
    lin(("v", "c"), "ab", "v", "c", w, last=True, kind="tok", mid=("adac", 3, 1))
    w = weights("ab", "gb")
    lin(("gb", "h0"), "ab", "gb", "h0", w)
    ev("spat", ("spat", "c"), part="c")
    adav(4, 0)
    ev("adapost", ("adapost", 4, 0), v=4, n=0)
    lin(("gb", "h1"), "ab", "gb", "h1", w, mid=("adac", 4, 0))
    for a in range(4):
        ev("abload", ("abload", a), a=a)
    lin(("gb", "c"), "ab", "gb", "c", w, last=True)
    ev("abload", ("abload", "c"), a="c")
    for odd in (0, 1):
        w = [slot("split", ("dft", odd * 8 + i, 0), None) for i in range(8)]
        if odd:
            adav(4, 1)
        ev("dft", ("dft", odd), odd=odd, ws=w)
    w = [slot("split", ("dft", 16 + i, 0), None) for i in range(2)]
    ev("dftc", ("dft", "c"), ws=w)
    for p in x3:
        ev("ysplit", ("ysplit", p), part=p)
    ev("reload", ("reload", 0), n=0)
    w = {}
    for g, p in ((0, "h0"), (1, "h0"), (0, "h1"), (0, "c"), (1, "h1"), (1, "c")):
        if p != "c":
            w[g] = weights("abo", g)
        if (g, p) == (0, "h0"):
            ev("adapost", ("adapost", 4, 1), v=4, n=1)
        if (g, p) == (0, "h1"):
            ev("statpost", ("statpost", 1, "h0"), n=1, part="h0")
            ev("apply", ("apply", 1, "h0"), n=1, part="h0")
        lin(("abo", g, p), "abo", g, p, w[g], last=p != "h1", midk=7 if p == "c" else 5,
            mid={(0, "h0"): ("adac", 4, 1), (0, "h1"): ("stat", 1, "h0"), (1, "c"): ("stat", 1, "h1")}.get((g, p)))
        if (g, p) == (1, "c"):
            ev("statpost", ("statpost", 1, "h1"), n=1, part="h1")
            ev("apply", ("apply", 1, "h1"), n=1, part="h1")
        if g == 1:
            ev("sum", ("sum", 1, p), n=1, part=p)
    ev("spill", ("spill", 1), n=1)
    ev("statpost", ("statpost", 1, "c"), n=1, part="c")
    ev("apply", ("apply", 1, "c"), n=1, part="c")
    w = weights("c", "kv")
    for p in x3:
        lin(("kv", p), "c", "kv", p, w, last=p == "c", kind="kv",
            mid=("stat", 1, "c") if p == "h0" else None)
    x2 = ("h0", "h1")
    for g in range(2):
        w = weights("c", ("q", g))
        for p in x2:
            lin(("q", g, p), "c", ("q", g), p, w, last=p == "h1")
    for g in range(2):
        w = weights("c", ("g", g))
        if g == 1:
            adav(5, 1)
        for p in x2:
            mid = {(1, "h0"): ("adac", 5, 0), (1, "h1"): ("adac", 5, 1)}.get((g, p))
            if (g, p) == (1, "h1"):
                ev("attc_pre", "attc_pre")
            if mid:
                ev("adapost", ("adapost",) + mid[1:], v=mid[1], n=mid[2])
            lin(("g", g, p), "c", ("g", g), p, w, last=p == "h1", mid=mid)
            if (g, p) == (0, "h0"):
                adav(5, 0)
    w_co = weights("co", 0)
    adas = ada_beside(6, 7, 8)
    ev("attc", "attc", ada=adas)
    for v in (6, 7, 8):
        ev("adasum", ("adac", v, None), v=v, n=None)
        ev("adapost", ("adapost", v, None), v=v, n=None)
    for p in x2:
        ev("hload", ("hload", 1, p), n=1, part=p)
        if p == "h0":
            ev("reload", ("reload", 1), n=1)
    for p in x2:
        for g in (0, 1):
            w = weights("co", g) if (g, p) != (0, "h0") else w_co
            if (g, p) == (0, "h1"):
                ev("statpost", ("statpost", 2, "h0"), n=2, part="h0")
                ev("apply", ("apply", 2, "h0"), n=2, part="h0")
            lin(("co", g, p), "co", g, p, w, last=True,
                mid=("stat", 2, "h0") if (g, p) == (0, "h1") else None)
        ev("sum", ("sum", 2, p), n=2, part=p)
    for name, p in (("cv", "h0"), ("cg", "h0"), ("cv", "h1"), ("cg", "h1")):
        if (name, p) == ("cg", "h1"):
            ev("flog", "flog", ws=weights("b2", "f"))
        w = weights("b2", name)
        if (name, p) == ("cg", "h1"):
            ev("conv", ("conv", "early"), i=-1)
        lin((name, p), "b2", name, p, w, last=True, mid=("stat", 2, "h1") if (name, p) == ("cv", "h0") else None)
        if (name, p) == ("cv", "h0"):
            ev("statpost", ("statpost", 2, "h1"), n=2, part="h1")
            ev("apply", ("apply", 2, "h1"), n=2, part="h1")
            ev("spill", ("spill", 2), n=2)
    ev("mask2", "mask2")
    for name in ("q2", "k2", "v2"):
        w = weights("b2", name)
        for p in x2:
            if (name, p) == ("v2", "h1"):
                ev("csum", "csum")
                ev("cmean", ("cmean", "x"))
            else:
                ev("conv", ("conv", name, p), i=2 * ("q2", "k2", "v2").index(name) + x2.index(p))
            lin((name, p), "b2", name, p, w, last=p == "h1", kind="tok" if name == "v2" else "lin",
                mid=("cmean", "x") if (name, p) == ("v2", "h1") else None)
    ev("cvarsum", ("cvar", "x"))
    ev("attf_pre", "attf_pre")
    ev("cvar", ("cvar", "x"))
    w_wo = weights("wo", 0)
    ev("attf", "attf", ada=ada_beside(9, 10))
    for v in (9, 10):
        ev("adasum", ("adac", v, None), v=v, n=None)
        ev("adapost", ("adapost", v, None), v=v, n=None)
    for p in x2:
        ev("hload", ("hload", 2, p), n=2, part=p)
        if p == "h0":
            ev("reload", ("reload", 2), n=2)
    def stats(n, p, mid=False):
        ev("statpost" if mid else "stat", ("statpost" if mid else "stat", n, p), n=n, part=p)

    for g, p in ((0, "h0"), (1, "h0"), (0, "h1"), (1, "h1")):
        w = weights("wo", g) if (g, p) != (0, "h0") else w_wo
        if (g, p) == (0, "h1"):
            ev("sum", ("sum", 3, "h0"), n=3, part="h0")
            stats(3, "h0", mid=True)
            ev("resid", ("resid", 3, "h0"), n=3, part="h0")
            ev("sum", ("sum", 4, "h0"), n=4, part="h0")
        if (g, p) == (1, "h1"):
            stats(4, "h0", mid=True)
            ev("apply", ("apply", 4, "h0"), n=4, part="h0")
        lin(("wo", g, p), "wo", g, p, w, last=True, midk=3,
            mid={(0, "h1"): ("stat", 3, "h0"), (1, "h1"): ("stat", 4, "h0")}.get((g, p)))
    ev("sum", ("sum", 3, "h1"), n=3, part="h1")
    nch = HID // 256

    def hidden(ch, p, w, last=True, **kw):
        lin(("fi", ch, p), "fi", ch, p, w, last=last, **kw)

    def hidden_out(ch, p, w, last=True):
        for g in (0, 1):
            lin(("fo", ch, g, p), "fo", g, p, w[g], kts=2, last=last, h="A", ch=ch)

    def out_weights(ch):
        return [[slot("split", ("fo", (ch, g), k), None) for k in range(2)] for g in range(2)]

    w = weights("fi", 0)
    stats(3, "h1", mid=True)
    ev("resid", ("resid", 3, "h1"), n=3, part="h1")
    hidden(0, "h0", w, mid=("stat", 3, "h1"), midk=3)
    ev("sum", ("sum", 4, "h1"), n=4, part="h1")
    hidden_out(0, "h0", out_weights(0))
    w = weights("fi", 1)
    stats(4, "h1", mid=True)
    ev("apply", ("apply", 4, "h1"), n=4, part="h1")
    hidden(1, "h0", w, mid=("stat", 4, "h1"), midk=3)
    hidden(0, "h1", weights("fi", 0))
    hidden_out(0, "h1", out_weights(0))
    hidden(1, "h1", weights("fi", 1))
    w = out_weights(1)
    for p in x2:
        hidden_out(1, p, w, last=p == "h1")
    for ch in range(2, nch - 1):
        w = weights("fi", ch)
        if ch == 3:
            ev("adapool", "adapool", ada=ada_beside(11))
        for p in x2:
            hidden(ch, p, w, last=p == "h1", mid=("adac", 11, None) if (ch, p) == (4, "h1") else None)
            if (ch, p) == (4, "h1"):
                ev("adapost", ("adapost", 11, None), v=11, n=None)
        w = out_weights(ch)
        for p in x2:
            hidden_out(ch, p, w, last=p == "h1")
    hidden(nch - 1, "h0", weights("fi", nch - 1))
    hidden_out(nch - 1, "h0", out_weights(nch - 1))
    w = weights("fi", nch - 1)
    ev("sum", ("sum", 5, "h0"), n=5, part="h0")
    stats(5, "h0", mid=True)
    hidden(nch - 1, "h1", w, mid=("stat", 5, "h0"), midk=3)
    ev("resid", ("resid", 5, "h0"), n=5, part="h0")
    hidden_out(nch - 1, "h1", out_weights(nch - 1))
    ev("sum", ("sum", 5, "h1"), n=5, part="h1")
    for half in range(2):
        ev("out", ("out", "h0", half), part="h0", half=half)
    stats(5, "h1")
    ev("resid", ("resid", 5, "h1"), n=5, part="h1")
    for half in range(2):
        ev("out", ("out", "h1", half), part="h1", half=half)
    return tl, slots


def program(nc, a, marks, old):
    TL, SLOTS = plan()
    ctx = ExitStack()
    with ctx:
        slab = ctx.enter_context(nc.sbuf_tensor("slab", [P, 212000 // 4], F32))
        base = [None]

        def at(name, shape, dt, off):
            return nc.alloc_sbuf_tensor_at(name, [P] + shape, dt, offset=BASE + off)

        BASE = 16512
        HREG, WREG, XREG = 0, 81920, 122880
        MREG = 163840
        HXH, HXL = at("HXH", [KT, T], F32R, HREG), at("HXL", [KT, T], F32R, HREG + 32768)
        HCH, HCL = at("HCH", [KT, C], F32R, HREG + 65536), at("HCL", [KT, C], F32R, HREG + 73728)
        AHH, AHL = at("AHH", [2, T], F32R, HREG + 65536), at("AHL", [2, T], F32R, HREG + 73728)
        XRAW = at("XRAW", [10, D], F32, HREG)
        WH, WL = at("WH", [WSLOTS, HALF], F32R, WREG), at("WL", [WSLOTS, HALF], F32R, WREG + 16384)
        RAW = at("RAW", [RSLOTS, HALF], F32, WREG + 32768)
        XX, XC = at("XX", [KT, T], F32, XREG), at("XC", [KT, C], F32, XREG + 32768)
        o = [MREG + 32768]

        def small(name, shape, dt=F32):
            n = 4 * int(np.prod(shape))
            t = at(name, shape, dt, o[0])
            o[0] += -(-n // 32) * 32
            return t

        TM = [small(f"TM{i}", [HALF]) for i in range(3)]
        SUM, RST = small("SUM", [HALF]), small("RST", [HALF])
        ACCP = [at(f"ACCP{x}", [HALF], F32, MREG + 2048 * x) for x in range(4)]
        ACC = [at(f"ACC{x}", [HALF], F32, MREG + 8192 + 2048 * x) for x in range(2)]
        ATMP = [at(f"ATMP{x}", [HALF], F32, o_) for x, o_ in enumerate((HREG + 57408, MREG + 24576, XREG + 32768))]
        CTMP = [at(f"CTMP{x}", [T], F32, MREG + 16896 + 4096 * x) for x in range(3)]
        RST0 = {p: at(f"RST0{p}", [HALF], F32, MREG + 8192 + 2048 * i) for i, p in enumerate(PARTS)}
        PC = small("PC", [384])
        IDF, IDR, ONF = small("IDF", [P]), small("IDR", [P], F32R), small("ONF", [P])
        MOD = small("MOD", [12, 2, KT])
        MX, SU, RC = ([small(f"{n}{b}", [4]) for b in range(2)] for n in ("MX", "SU", "RC"))
        NSK = small("NSK", [16])
        CO = small("CO", [10, KT])
        CS = small("CS", [KT, 4])
        EPT = small("EPT", [1])
        BST, MV = small("BST", [4, 6]), small("MV", [4, 2])
        SM = small("SM", [64])
        assert BASE + o[0] <= 229368, BASE + o[0]
        M = MREG
        PROW = at("PROW", [3, P], F32, M)
        VBH, VBL = at("VBH", [4, HALF], F32R, M), at("VBL", [4, HALF], F32R, M + 8192)
        STG = at("STG", [2048], F32, M + 16384)
        SWH, SWL = at("SWH", [4, P], F32R, M + 24576), at("SWL", [4, P], F32R, M + 26624)
        SBB = at("SBB", [4, P], F32, M + 28672)
        CHH, CHL = at("CHH", [256], F32R, M + 30720), at("CHL", [256], F32R, M + 31744)
        SWRAW = at("SWRAW", [4, P], F32, M + 16384)
        CHRAW = at("CHRAW", [256], F32, M + 18432)
        ARAW = at("ARAW", [2, D], F32, M + 16384)
        ASD = at("ASD", [2, D], F32, M)
        KS, VS = at("KS", [4, T + C], F32R, XREG), at("VS", [10, 4, P], F32R, XREG + 20480)
        ROPE = at("ROPE", [2, T], F32, M)
        QS = [[at(f"QS{b}{x}", [4, HALF], F32R, HREG + 16384 * b + 8192 * x) for x in range(2)] for b in range(2)]
        RQ = [at(f"RQ{b}", [2, HALF], F32, (M + 28160, HREG + 53312)[b]) for b in range(2)]
        PB = [at(f"PB{b}", [4, 641], F32, HREG + 32768 + 10272 * b) for b in range(2)]
        PTH, PTL = at("PTH", [5, HALF], F32R, HREG + 61440), at("PTL", [5, HALF], F32R, HREG + 71680)
        OT = [at(f"OT{b}", [2, HALF], F32, M + 8192 + 4096 * b) for b in range(2)]
        GT = [at(f"GT{b}", [2, HALF], F32, M + 16384 + 4096 * b) for b in range(2)]
        OTT = at("OTT", [2, P], F32, M + 24576)
        MKF, MKR = at("MKF", [2, P], F32, M + 25600), at("MKR", [2, P], F32R, M + 26624)
        SINK = at("SINK", [16], F32, M + 27648)
        U = at("U", [4, T + TAPS - 1], F32, M)
        CSUM, CRST = at("CSUM", [T], F32, M), at("CRST", [T], F32, M + 4096)
        CSQ = [at(f"CSQ{b}", [T], F32, M + 8192 + 4096 * b) for b in range(2)]
        CA = at("CA", [4, T], F32, XREG)
        QH2 = [at(f"QH2{b}", [T], F32R, HREG + 12288 * b) for b in range(2)]
        QL2 = [at(f"QL2{b}", [T], F32R, HREG + 4096 + 12288 * b) for b in range(2)]
        KS2 = [at(f"KS2{b}", [T], F32R, HREG + 8192 + 12288 * b) for b in range(2)]
        RQ2, RK2 = at("RQ2", [T], F32, HREG + 24576), at("RK2", [T], F32, HREG + 28672)
        RV2 = at("RV2", [NB_T, P], F32, HREG + 32768)
        NBC = [at(f"NBC{b}", [T], F32, HREG + 36864 + 4096 * b) for b in range(2)]
        PB2 = [at(f"PB2{b}", [4, T], F32, HREG + 45056 + 16384 * b) for b in range(2)]
        PT2H, PT2L = at("PT2H", [8, HALF], F32R, XREG), at("PT2L", [8, HALF], F32R, XREG + 16384)
        VS2 = [at(f"VS2{b}", [NB_T, P], F32R, XREG + 32768 + 4096 * b) for b in range(2)]
        OT2 = [at(f"OT2{b}", [T], F32, M + 8192 + 4096 * b) for b in range(2)]
        OTT2 = at("OTT2", [HALF], F32, M + 16384)
        MKF2, MKR2 = at("MKF2", [P], F32, M + 29696), at("MKR2", [P], F32R, M + 30208)
        FL = [at(f"FL{i}", [T], F32, M + 17408 + 4096 * i) for i in range(3)]
        OUTS = [at(f"OUTS{b}", [2048], F32, HREG + 8192 * b) for b in range(2)]
        Y = at("Y", [KT, T], F32, M)
        LR = [at(f"LR{b}", [KT, HALF], F32, M + 16384 * b) for b in range(2)]
        PS = ctx.enter_context(nc.psum_tensor("PS", [P, 8, HALF], F32))

        def scratch(name, shape):
            return nc.dram_tensor(name, shape, F32, kind="Internal").ap()

        XR = scratch("XR", [P, KT, T])
        ABD = scratch("ABD", [T + C, D])
        QD, GD, OD = (scratch(n, [P, KT, T]) for n in ("QD", "GD", "OD"))
        XCD = scratch("XCD", [P, KT, C])
        KD2 = scratch("KD2", [P, 4, T])
        VD2 = scratch("VD2", [T, HALF])
        CUM = scratch("CUM", [8, T])

        counts = {}

        def did(semaphore, *names, by=1):
            counts[semaphore.name] = counts.get(semaphore.name, 0) + by
            for n in names:
                marks[n] = (semaphore, counts[semaphore.name])

        def so_far(semaphore):
            return counts[semaphore.name]

        def upto(*name):
            return of(*name)[1]

        def of(*name):
            name = name[0] if len(name) == 1 else name
            if not old:
                return products_done, 1
            s, v = old[name]
            return semaphores[s.name], v

        semaphores = {}

        def sem(name):
            semaphores[name] = ctx.enter_context(nc.semaphore(name))
            return semaphores[name]

        products_done, scalar_done = sem("products_done"), sem("scalar_done")
        vector_done, gpsimd_done = sem("vector_done"), sem("gpsimd_done")
        rows_loaded, x_loaded, tables_loaded = sem("rows_loaded"), sem("x_loaded"), sem("tables_loaded")
        late_loaded, spilled, cum_stored = sem("late_loaded"), sem("spilled"), sem("cum_stored")
        raw_loaded = [sem(f"raw_loaded{r}") for r in range(RSLOTS)]
        stage_free = [sem(f"stage_free{r}") for r in range(3)]
        h_loaded = [sem(f"h_loaded{k}") for k in range(4)]
        ab_loaded, rq_loaded, g_loaded, ot_stored, nb_loaded = (
            [sem(f"{n}{b}") for b in range(2)]
            for n in ("ab_loaded", "rq_loaded", "g_loaded", "ot_stored", "nb_loaded"))

        def uses(e):
            k, l, g = e["kind"], e.get("layer"), e.get("group")
            w4 = 2 if e.get("part") == "c" else 4
            if k == "ada":
                return 2
            if k in ("sum",):
                return 16 if e["n"] == 2 else 8
            if k in ("stat", "statpost"):
                return 1 if e["n"] == 2 else 0
            if k in ("apply", "resid"):
                return 8
            if k == "spat":
                return 4
            if k == "kv":
                return 2 if e["part"] == "c" else 4
            if k == "tok" and l == "ab":
                return w4
            if k in ("lin", "tok"):
                if g in ("ga", "cg", "q2", "k2", "v2") or (l == "c" and g[0] == "g"):
                    return 4
                if l == "c":
                    return 8
                if l == "fi":
                    return 2
            return 0

        TMID = []
        for e in TL:
            TMID += [(e["name"], i) for i in range(uses(e))]
        TMAT = {x: i for i, x in enumerate(TMID)}

        def tm_before(name, i):
            n = TMAT[(name, i)]
            return [TMID[n - 3]] if n >= 3 else []

        def tm(name, i, w=HALF, p0=0, p1=P):
            return TM[TMAT[(name, i)] % 3][p0:p1, 0:w]


        def tcount(z, which):
            if which == "c":
                return sum(4 if y % 8 in (0, 7) else 5 for y in range(z))
            return sum(4 if y % 2 == 0 else 8 for y in range(z))

        def spread(which):
            steps = 32 if which == "c" else 16
            tiles = {}
            for z in range(steps):
                n = tcount(z + 1, which) - tcount(z, which)
                first = 0
                for h, m in zip((1, 2, 3), {4: (2, 1, 1), 5: (2, 1, 2), 8: (2, 3, 3)}[n]):
                    tiles[4 * (z + 1) + h] = [(z, first + x) for x in range(m)]
                    first += m
            return tiles

        def key_blocks(z):
            return list(range(1 if z % 8 in (0, 7) else 0, 5))

        splits = [n for n, x in enumerate(SLOTS) if x[0] == "split"]
        WPOS = {n: i % WSLOTS for i, n in enumerate(splits)}
        WPREV = {n: splits[i - WSLOTS] for i, n in enumerate(splits) if i >= WSLOTS}

        order = []
        for e in TL:
            if e["kind"] in ("params", "tx", "ada", "adac", "stat", "lin", "tok", "kv", "chan", "spat", "dft",
                             "dftc", "flog", "out", "small", "adasum", "cvarsum"):
                order.append((e["name"], e))
                if e.get("mid"):
                    order.append((e["mid"], e))
            if e["kind"] in ("attc", "attf"):
                order.append((e["name"], e))
        setof, prev, lastin = {}, {}, {0: None, 1: None}
        cur = 0
        for name, e in order:
            if e["kind"] in ("attc", "attf"):
                prev[name] = [x for x in lastin.values() if x]
                lastin = {0: name, 1: name}
                cur = 0
                continue
            if e.get("mid") == name:
                s = 1 - setof[e["name"]]
            else:
                s = cur
                cur = 1 - cur
            setof[name] = s
            prev[name] = [lastin[s]] if lastin[s] else []
            lastin[s] = name

        def bank(name, b, n=HALF, p0=0, p1=P):
            return PS[p0:p1, 4 * setof[name] + b, 0:n]


        def hs(part, k, lo):
            off, n = PARTS[part]
            if part == "c":
                return (HCL if lo else HCH)[:, k, :]
            return (HXL if lo else HXH)[:, k, off:off + n]

        def xs(part, k):
            off, n = PARTS[part]
            return XC[:, k, :] if part == "c" else XX[:, k, off:off + n]

        def ys(part, k):
            off, n = PARTS[part]
            return Y[:, k, off:off + n]

        def col(name, i=0):
            b = ROWS[name][0] + i
            return PC[:, b:b + 1]

        def cols(name, i=0, n=None):
            b, m = ROWS[name]
            return PC[:, b + i:b + i + (n or m)]

        def ada_acc(v, n, x):
            if v < 6:
                return (ACC if (v, n) == (5, 1) else (SUM, RST))[x]
            return ((SUM, RST), ACCP[0:2], ACCP[2:4])[v % 3 if v < 11 else 0][x]

        def mod(v, part, k):
            return MOD[:, v, 1 if part == "c" else 0, k:k + 1]

        def acoef(n, part, k):
            i = {0: 0, 1: 2, 2: 4, 4: 5}[n] + (1 if part == "c" else 0)
            return CO[:, i, k:k + 1]

        def shift(n, part, k):
            return mod({0: 0, 1: 3, 2: 6, 4: 9}[n], part, k)

        HREADERS = {0: {}, 1: {p: ("abo", 1, p) for p in PARTS}, 2: {p: ("co", 1, p) for p in PARTS},
                    4: {p: ("wo", 1, p) for p in PARTS}}
        HMAKER = {"ab": ("apply", 0), "abo": ("ysplit", 0), "c": ("apply", 1), "co": ("hload", 1),
                  "b2": ("apply", 2), "wo": ("hload", 2), "fi": ("apply", 4)}

        block = ctx.enter_context(nc.Block())

        @block.sync
        def _(sp):

            with nc.allow_non_contiguous_dma(reason="small parameters"):
                sp.dma_start(IDF[:, :], a["t_ident"]).then_inc(rows_loaded, 16)
                did(rows_loaded, "rows", by=16)
                sp.dma_start(SM[0:8, 48:49], a["b_f_2"].rearrange("l h -> h l")).then_inc(rows_loaded, 16)
                did(rows_loaded, "rows", by=16)
                for name, src in (("norm_g", a["norm_g"].rearrange("l (k p) -> (l k) p", p=P)),
                                  ("ada_b", a["ada_b"].rearrange("l (k p) -> (l k) p", p=P)),
                                  ("c", a["c"].rearrange("b (k p) -> (b k) p", p=P)),
                                  ("c_ctx", a["c_ctx"].rearrange("(k p) -> k p", p=P)),
                                  ("c_2", a["c_2"].rearrange("b (k p) -> (b k) p", p=P)),
                                  ("v_norm_g", a["v_norm_g"].rearrange("l (k p) -> (l k) p", p=P)),
                                  ("final_g", a["final_g"].rearrange("(k p) -> k p", p=P)),
                                  *[(n, a[n].rearrange("l (k p) -> (l k) p", p=P)) for n in
                                    ("conv_b_2", "conv_ln_g_2", "conv_ln_b_2", "mix_pre_g_2", "mix_post_g_2",
                                     "ffn_pre_g_2", "ffn_post_g_2", "ada_b_2")],
                                  ("conv_w_2", a["conv_w_2"].rearrange("l j (k p) -> (l j k) p", p=P))):
                    r, n = ROWS[name]
                    sp.dma_start(PROW[r % P:r % P + n, r // P, :], src).then_inc(rows_loaded, 16)
                    did(rows_loaded, "rows", by=16)
            x_rows = a["x"].rearrange("b (t p) d -> p (b t) d", p=P)
            c_rows = a["ctx"].rearrange("b (t p) d -> p (b t) d", p=P)
            for b in range(2):
                sp.dma_start(XRAW[:, 4 * b:4 * b + 4, :], x_rows[:, 4 * b:4 * b + 4, :]).then_inc(x_loaded, 16)
                did(x_loaded, "xraw", by=16)
            sp.dma_start(XRAW[:, 8:10, :], c_rows).then_inc(x_loaded, 16)
            did(x_loaded, "xraw", by=16)
            sp.dma_start(SWRAW[:, :, :], a["spatial_w"].rearrange("l h q p -> q (l h) p")).then_inc(tables_loaded, 16)
            did(tables_loaded, "smallraw", by=16)
            sp.dma_start(CHRAW[:, :], a["t_chan"]).then_inc(tables_loaded, 16)
            did(tables_loaded, "smallraw", by=16)
            sb = a["spatial_b"].rearrange("l h q -> (l h q)")
            sp.dma_start(SBB[:, :, :].rearrange("p h q -> p (h q)"),
                         sb.partition_broadcast(P)).then_inc(tables_loaded, 16)
            did(tables_loaded, "smallraw", by=16)
            for n, (kind, src, _) in enumerate(SLOTS):
                r = n % RSLOTS
                if n >= RSLOTS:
                    sp.wait_ge(*of("rawfree", n - RSLOTS))
                w = 8 if src[:2] == ("b2", "f") else HALF
                dst = RAW[:, r, 0:w]
                l, g, k = src[0], src[1], src[2]
                rows = slice(k * P, (k + 1) * P)
                if l == "ada":
                    v, n2 = g, src[3]
                    m, c0 = (a["ada_w"][v // 3], (v % 3) * D) if v < 6 else (a["ada_w_2"][0], (v - 6) * D)
                    s = [m[rows, c0 + n2 * HALF:c0 + (n2 + 1) * HALF]]
                elif l == "ab":
                    c0 = ("u", "v", "ga", "xb", "gb").index(g) * HALF
                    s = [a["w_in_ab"][0][rows, c0:c0 + HALF]]
                elif l == "abo":
                    s = [a["w_out_ab"][0][rows, g * HALF:(g + 1) * HALF]]
                elif l == "co":
                    s = [a["w_out_c"][0][rows, g * HALF:(g + 1) * HALF]]
                elif l == "wo":
                    s = [a["w_o_2"][0][rows, g * HALF:(g + 1) * HALF]]
                elif l == "c":
                    c0 = 1024 if g == "kv" else (0 if g[0] == "q" else 1536) + g[1] * HALF
                    s = [a["w_in_c"][0][rows, c0:c0 + HALF]]
                elif l == "b2":
                    c0 = {"q2": 0, "k2": 512, "v2": 1024, "f": 1536, "cv": 1544, "cg": 2056}[g]
                    s = [a["w_in_2"][0][rows, c0:c0 + w]]
                elif l == "fi":
                    m = a["w_ffn_in_2"][0]
                    s = [m[rows, g * 256:(g + 1) * 256], m[rows, HID + g * 256:HID + (g + 1) * 256]]
                elif l == "fo":
                    ch, gg = g
                    s = [a["w_ffn_out_2"][0][ch * 256 + k * P:ch * 256 + (k + 1) * P, gg * HALF:(gg + 1) * HALF]]
                elif l == "dft":
                    s = [a["t_dft"][g]]
                wd = w // len(s)
                for i, x in enumerate(s):
                    sp.dma_start(dst[:, i * wd:(i + 1) * wd], x).then_inc(raw_loaded[r], 16)
                    did(raw_loaded[r], ("raw", n), by=16)

        @block.gpsimd
        def _(pool):
            g = nc.gpsimd

            def split(n):
                r, w = n % RSLOTS, n % WSLOTS
                m = 8 if SLOTS[n][1][:2] == ("b2", "f") else HALF
                pool.wait_ge(raw_loaded[n % RSLOTS], upto("raw", n))
                if n in WPREV:
                    pool.wait_ge(products_done, upto("used", WPREV[n]))
                sw = WPOS[n]
                g.tensor_scalar(WH[:, sw, 0:m], RAW[:, r, 0:m], 1.0, 0.0, ALU.mult, ALU.add).then_inc(gpsimd_done, 1)
                did(gpsimd_done, ("whi", n))
                pool.wait_ge(gpsimd_done, so_far(gpsimd_done))
                g.tensor_tensor(WL[:, sw, 0:m], RAW[:, r, 0:m], WH[:, sw, 0:m].bitcast(F32), ALU.subtract).then_inc(gpsimd_done, 1)
                did(gpsimd_done, ("w", n), ("rawfree", n))

            done = [0]

            def split_until(n):
                while done[0] < min(n, len(SLOTS)):
                    if SLOTS[done[0]][0] == "split":
                        split(done[0])
                    done[0] += 1

            g.memset(ONF[:, :], 1.0).then_inc(gpsimd_done, 1)
            did(gpsimd_done, "ones")
            g.memset(EPT[:, :], EPS).then_inc(gpsimd_done, 1)
            did(gpsimd_done, "eps")
            def ada_tile(v, k, x, n):
                acc, cond = ada_acc(v, None, x)[:, :], CS[:, k, 2:3] if v >= 6 else CS[:, k, 0:1]
                pool.wait_ge(raw_loaded[n % RSLOTS], upto("raw", n))
                if k == 0:
                    g.tensor_scalar(acc, RAW[:, n % RSLOTS, :], cond, 0.0, ALU.mult, ALU.add).then_inc(gpsimd_done, 1)
                else:
                    pool.wait_ge(gpsimd_done, so_far(gpsimd_done))
                    tmp = ATMP[0 if v < 9 else 1 if v < 11 else 2][:, :]
                    g.tensor_scalar(tmp, RAW[:, n % RSLOTS, :], cond, 0.0, ALU.mult, ALU.add).then_inc(gpsimd_done, 1)
                    did(gpsimd_done, ("ada_product", v, k, x))
                    pool.wait_ge(gpsimd_done, upto("ada_product", v, k, x))
                    g.tensor_tensor(acc, tmp, acc, ALU.add).then_inc(gpsimd_done, 1)
                did(gpsimd_done, ("ada_acc", v, None, k, x), ("rawfree", n))

            for e in TL:
                if e["kind"] == "conv":
                    ahead = sorted({x["ws"][-1] for x in TL[TL.index(e):] if x.get("ws")})
                    split_until(ahead[1 if e["i"] % 2 and e["i"] > 0 else 0] + 1)
                    for t_ in CONV_SHARES.get(e["i"], ()):
                        if t_ == 0:
                            continue
                        pool.wait_ge(scalar_done, upto("tap", t_))
                        if t_ > 1:
                            pool.wait_ge(gpsimd_done, upto("conv", 3, t_ - 1, 1))
                        g.tensor_tensor(CA[:, 3, :], CTMP[t_ % 3][:, :], CA[:, 3, :], ALU.add).then_inc(gpsimd_done, 1)
                        did(gpsimd_done, ("conv", 3, t_, 0), ("conv", 3, t_, 1))
                if e["kind"] == "adapool":
                    split_until(e["ada"][0][-1])
                    done[0] = e["ada"][-1][-1] + 1
                    pool.wait_ge(vector_done, upto("H", "apply", 4, "h1", KT - 1))
                    for tile in e["ada"]:
                        ada_tile(*tile)
                if e["kind"] not in ("attc", "attf"):
                    continue
                ahead = [x["ws"][-1] for x in TL[:TL.index(e)] if x.get("ws")]
                n0 = max(ahead) + 1
                split_until(n0)
                more = n0
                while more < len(SLOTS) and more < n0 + WSLOTS and SLOTS[more][0] == "split":
                    more += 1
                split_until(more)
                left = list(e["ada"])
                done[0] = left[-1][-1] + 1
                if e["kind"] == "attc":
                    pool.wait_ge(products_done, upto("job", ("adac", 5, 1)))
                    pool.wait_ge(vector_done, upto("kr", ("q", 1, "h1"), 3))
                    pool.wait_ge(products_done, upto("job", ("g", 1, "h1")))
                else:
                    pool.wait_ge(vector_done, upto("cn", 3))
                    pool.wait_ge(cum_stored, upto("cumst"))
                if e["kind"] == "attc":
                    for s in range(32):
                        i = s % 8
                        lo = 128 if i in (0, 7) else 0
                        for h in range(4):
                            pool.wait_ge(vector_done, upto("rc", "c", 4 * s + h))
                            x = PB[s % 2][:, h, lo:640]
                            g.tensor_scalar(x, x, RC[s % 2][:, h:h + 1], 1.0, ALU.mult, ALU.mult).then_inc(gpsimd_done, 1)
                            did(gpsimd_done, ("P", "c", s, h))
                            if left and h in (0, 1):
                                ada_tile(*left.pop(0))
                else:
                    for s in range(16):
                        for i4 in range(4):
                            n = (4 * (s % 2) + i4 + 1) * P
                            pool.wait_ge(vector_done, upto("rc", "f", 4 * s + i4))
                            x = PB2[s % 2][:, i4, 0:n]
                            g.tensor_scalar(x, x, RC[s % 2][:, i4:i4 + 1], 1.0, ALU.mult, ALU.mult).then_inc(gpsimd_done, 1)
                            did(gpsimd_done, ("P", "f", s, i4))
                            if left and i4 in (0, 1):
                                ada_tile(*left.pop(0))
            split_until(len(SLOTS))

        @block.tensor
        def _(pe):
            mm = nc.tensor.matmul

            def three(out, wh, wl, xh, xl, first, last, group=True):
                kw = {} if group else {"skip_group_check": True}
                mm(out, wh, xh, start=first, stop=False, **kw)
                mm(out, wh, xl, start=False, stop=False, **kw)
                return mm(out, wl, xh, start=False, stop=last, **kw)

            def stat(name, n, part):
                w = PARTS[part][1]
                pe.wait_ge(gpsimd_done, upto("ones"))
                pe.wait_ge(vector_done, upto("sum", n, part))
                for job_before in prev[name]:
                    pe.wait_ge(*of("free", job_before))
                mm(bank(name, 0, w), ONF[:, :], SUM[:, 0:w], start=True, stop=True).then_inc(products_done, 1)
                did(products_done, ("job", name))
                if n == 2:
                    pe.wait_ge(vector_done, upto("sumg", n, part))
                    mm(bank(name, 1, w), ONF[:, :], RST[:, 0:w], start=True, stop=True).then_inc(products_done, 1)
                    did(products_done, ("job", name))

            def conv_sums(name):
                for job_before in prev[name]:
                    pe.wait_ge(*of("free", job_before))
                pe.wait_ge(vector_done, upto(name[0] + "_sum"))
                for b in range(2):
                    ins = mm(bank(name, b), ONF[:, :], CSUM[:, b * HALF:(b + 1) * HALF], start=True, stop=True)
                ins.then_inc(products_done, 1)
                did(products_done, ("job", name))

            def ada_sums(name, v, n):
                for job_before in prev[name]:
                    pe.wait_ge(*of("free", job_before))
                for x in range(2):
                    pe.wait_ge(*of("ada_acc", v, n, KT - 1, x))
                    for j in range(4):
                        c0 = 2 * (4 * n + j) + x if n is not None else 2 * (4 * x + j)
                        ins = mm(bank(name, 0)[:, c0:c0 + 1], ada_acc(v, n, x)[:, j * P:(j + 1) * P], ONF[:, 0:1],
                                 start=True, stop=True)
                ins.then_inc(products_done, 1)
                did(products_done, ("job", name))

            for e in TL:
                kind, name = e["kind"], e["name"]
                if kind in ("sum", "apply", "coef", "spill", "abload", "ysplit", "reload", "statpost", "conv",
                            "hload", "resid", "adav", "adapost", "attc_pre", "attf_pre", "csum", "cmean", "cvar", "adapool", "mask2"):
                    continue
                part = e.get("part")
                if kind not in ("attc", "attf", "stat"):
                    for job_before in prev[name]:
                        pe.wait_ge(*of("free", job_before))
                if kind == "params":
                    pe.wait_ge(rows_loaded, upto("rows"))
                    for b in range(3):
                        nr = (P, 64, 124)[b]
                        ins = nc.tensor.transpose(PS[:, 0, b * P:b * P + nr], PROW[0:nr, b, :], IDF[0:nr, 0:nr])
                    ins.then_inc(products_done, 1)
                    did(products_done, ("job", name))
                elif kind == "tx":
                    pe.wait_ge(x_loaded, upto("xraw"))
                    pe.wait_ge(rows_loaded, upto("rows"))
                    for tb in range(10):
                        ins = nc.tensor.transpose(bank(name, tb // 4)[:, (tb % 4) * P:(tb % 4 + 1) * P],
                                                  XRAW[:, tb, e["k"] * P:(e["k"] + 1) * P], IDF[:, :])
                    ins.then_inc(products_done, 1)
                    did(products_done, ("job", name))
                elif kind == "ada":
                    pe.wait_ge(scalar_done, upto("cs"))
                    cond = 0 if e["v"] < 6 else 2
                    for i, n in enumerate(e["ws"]):
                        k, b = i // 2, i % 2
                        pe.wait_ge(raw_loaded[n % RSLOTS], upto("raw", n))
                        mm(bank(name, b, p1=2), CS[:, k, cond:cond + 2], RAW[:, n % RSLOTS, :],
                               start=k == 0, stop=k == KT - 1).then_inc(products_done, 1)
                        did(products_done, ("rawfree", n), ("job", name))
                elif kind == "adasum":
                    ada_sums(name, e["v"], e["n"])
                elif kind == "adac":
                    pe.wait_ge(scalar_done, upto("arow", e["v"]))
                    an = ("ada", e["v"])
                    for k in range(KT):
                        ins = mm(bank(name, 0)[:, 2 * k:2 * k + 2], tm(an, k // 4, p1=2)[:, (k % 4) * P:(k % 4 + 1) * P],
                                 IDF[0:2, 0:2], start=True, stop=True)
                    ins.then_inc(products_done, 1)
                    did(products_done, ("job", name), ("tm", (an, 0)), ("tm", (an, 1)))
                elif kind == "small":
                    pe.wait_ge(tables_loaded, upto("smallraw"))
                    for h in range(4):
                        ins = nc.tensor.transpose(bank(name, 0)[:, h * P:(h + 1) * P], SWRAW[:, h, :], IDF[:, :])
                    ins.then_inc(products_done, 1)
                    did(products_done, ("job", name))
                elif kind == "stat":
                    stat(name, e["n"], e["part"])
                elif kind in ("lin", "tok", "kv"):
                    part, kts = e["part"], e["kts"]
                    off, n = PARTS[part]
                    mk = HMAKER.get(e["layer"])
                    for k in range(kts):
                        sw = WPOS[e["ws"][k]]
                        pe.wait_ge(gpsimd_done, upto("w", e["ws"][k]))
                        if e["h"] == "H":
                            pe.wait_ge(vector_done, upto("H", mk[0], mk[1], part, k))
                            xh, xl = hs(part, k, 0), hs(part, k, 1)
                        else:
                            pe.wait_ge(vector_done, upto("A", e["ch"], part, k))
                            xh, xl = AHH[:, k, off:off + n], AHL[:, k, off:off + n]
                        f, l = k == 0, k == kts - 1
                        if kind == "lin":
                            for j in range(4):
                                ws = slice(j * P, (j + 1) * P)
                                ins = three(bank(name, j, n), WH[:, sw, ws], WL[:, sw, ws], xh, xl, f, l)
                        elif kind == "tok":
                            for tb in range(n // P):
                                ts = slice(tb * P, (tb + 1) * P)
                                ins = three(bank(name, tb), xh[:, ts], xl[:, ts], WH[:, sw, :], WL[:, sw, :], f, l)
                        else:
                            for j in range(2):
                                ws = slice(j * P, (j + 1) * P)
                                ins = three(bank(name, j, n), WH[:, sw, ws], WL[:, sw, ws], xh, xl, f, l)
                            for tb in range(n // P):
                                ts = slice(tb * P, (tb + 1) * P)
                                o_ = bank(name, 2 + tb // 2)[:, (tb % 2) * 256:(tb % 2) * 256 + 256]
                                ins = three(o_, xh[:, ts], xl[:, ts], WH[:, sw, 256:512], WL[:, sw, 256:512],
                                            f and tb % 2 == 0, l, group=False)
                        nm = []
                        if e["last"]:
                            nm.append(("used", e["ws"][k]))
                        if l:
                            nm.append(("job", name))
                        if nm:
                            ins.then_inc(products_done, 1)
                            did(products_done, *nm)
                        if e["mid"] and k == e.get("midk", 5):
                            if e["mid"][0] == "adac":
                                ada_sums(e["mid"], e["mid"][1], e["mid"][2])
                            elif e["mid"][0] == "cmean":
                                conv_sums(e["mid"])
                            else:
                                stat(e["mid"], e["mid"][1], e["mid"][2])
                elif kind == "chan":
                    part, half = e["part"], e["half"]
                    pe.wait_ge(vector_done, upto("xbs", part))
                    pe.wait_ge(vector_done, upto("small_split"))
                    for t2 in range(2):
                        for g in range(4):
                            tb = 2 * half + t2
                            ts = slice(tb * P, (tb + 1) * P)
                            o_ = bank(name, 2 * t2 + g // 2)[:, (g % 2) * 256:(g % 2) * 256 + 256]
                            ins = three(o_, VBH[:, g, ts], VBL[:, g, ts], CHH[:, :], CHL[:, :],
                                        True, True)
                    ins.then_inc(products_done, 1)
                    did(products_done, ("job", name))
                elif kind == "spat":
                    part = e["part"]
                    pe.wait_ge(vector_done, upto("small_split"))
                    for tb in range(PARTS[part][1] // P):
                        pe.wait_ge(vector_done, upto("vn", part, tb))
                        for h in range(4):
                            c_ = slice(h * P, (h + 1) * P)
                            ins = three(bank(name, h)[:, tb * P:(tb + 1) * P], VBH[:, tb, c_], VBL[:, tb, c_],
                                        SWH[:, h, :], SWL[:, h, :], True, True)
                    ins.then_inc(products_done, 1)
                    did(products_done, ("job", name))
                elif kind == "dft":
                    for kt in range(4):
                        hk = kt + 4 * e["odd"]
                        pe.wait_ge(vector_done, upto("AB", hk))
                        for cs in range(2):
                            n = e["ws"][2 * kt + cs]
                            pe.wait_ge(gpsimd_done, upto("w", n))
                            for g in range(4):
                                c_ = slice(g * 256 + cs * P, g * 256 + cs * P + P)
                                ins = three(bank(name, g), HXH[:, hk, c_], HXL[:, hk, c_], WH[:, WPOS[n], :],
                                            WL[:, WPOS[n], :], kt + cs == 0, kt == 3 and cs == 1)
                            ins.then_inc(products_done, 1)
                            did(products_done, ("used", n), ("job", name))
                elif kind == "dftc":
                    pe.wait_ge(vector_done, upto("AB", "c"))
                    hc = [x[:, :, :].rearrange("p k c -> p (k c)") for x in (HCH, HCL)]
                    for kt in range(2):
                        n = e["ws"][kt]
                        pe.wait_ge(gpsimd_done, upto("w", n))
                        for cs in range(2):
                            w_ = slice(cs * 256, cs * 256 + 256)
                            for g in range(4):
                                c0 = kt * D + g * 256 + cs * P
                                ins = three(bank(name, g, C), hc[0][:, c0:c0 + P], hc[1][:, c0:c0 + P],
                                            WH[:, WPOS[n], w_], WL[:, WPOS[n], w_], kt + cs == 0, kt + cs == 2)
                        ins.then_inc(products_done, 1)
                        did(products_done, ("used", n), ("job", name))
                elif kind == "flog":
                    for k in range(KT):
                        n = e["ws"][k]
                        pe.wait_ge(gpsimd_done, upto("w", n))
                        for b, p in enumerate(("h0", "h1")):
                            pe.wait_ge(vector_done, upto("H", "apply", 2, p, k))
                            ins = three(bank(name, b, p1=8), WH[:, WPOS[n], 0:8], WL[:, WPOS[n], 0:8],
                                        hs(p, k, 0), hs(p, k, 1), k == 0, k == KT - 1)
                        ins.then_inc(products_done, 1)
                        did(products_done, ("used", n), ("job", name))
                elif kind == "cvarsum":
                    conv_sums(name)
                elif kind == "out":
                    off = PARTS[e["part"]][0] + e["half"] * 256
                    for k in range(KT):
                        pe.wait_ge(vector_done, upto("xfin", e["part"], k))
                        for t2 in range(2):
                            ins = nc.tensor.transpose(bank(name, 2 * t2 + k // 4)[:, (k % 4) * P:(k % 4 + 1) * P],
                                                      XX[:, k, off + t2 * P:off + (t2 + 1) * P], IDF[:, :])
                    ins.then_inc(products_done, 1)
                    did(products_done, ("job", name))
                elif kind == "attc":
                    for job_before in prev[name]:
                        pe.wait_ge(*of("free", job_before))
                    pe.wait_ge(scalar_done, upto("masks"))
                    pe.wait_ge(vector_done, upto("nsk"))
                    tiles = spread("c")
                    for u in range(4 * 32 + 6):
                        s, h = u // 4, u % 4
                        if s < 32:
                            kv, i = s // 8, s % 8
                            sb = 2 * (u % 2)
                            if u >= 2:
                                pe.wait_ge(scalar_done, upto("exp", "c", u - 2))
                            pe.wait_ge(vector_done, upto("qs", s // 4, h // 2))
                            q = slice((i % 4) * P, (i % 4 + 1) * P)
                            qh, ql = (QS[(s // 4) % 2][x][:, h, q] for x in range(2))
                            p0 = 1 if i in (0, 7) else 0
                            b0 = i - 1 if i > 0 else 0
                            nblk = 3 - p0
                            A_ = PS[:, sb, (1 + p0) * P:HALF]
                            kx = KS[:, kv, b0 * P:(b0 + nblk) * P]
                            mm(A_, qh, kx, start=True, stop=False, skip_group_check=True)
                            mm(A_, ql, kx, start=False, stop=False, skip_group_check=True)
                            if i > 0:
                                o_ = (1 + p0) * P
                                mm(PS[:, sb, o_:o_ + P], IDR[:, :], MKR[:, 0, :], start=False, stop=i == 7,
                                   skip_group_check=True)
                            if i < 7:
                                mm(PS[:, sb, 3 * P:4 * P], IDR[:, :], MKR[:, 1, :], start=False, stop=True,
                                   skip_group_check=True)
                            B_ = PS[:, sb + 1, 0:256]
                            mm(B_, qh, KS[:, kv, T:T + C], start=True, stop=False)
                            mm(B_, ql, KS[:, kv, T:T + C], start=False, stop=True)
                            hd = kv * 4 + h
                            mm(PS[:, sb + 1, 256:257], ONF[0:1, :], NSK[0:1, hd:hd + 1], start=True,
                               stop=True).then_inc(products_done, 1)
                            did(products_done, ("sc", "c", u))
                        if h == 0 and s >= 2:
                            z = s - 2
                            kv, i = z // 8, z % 8
                            pos = key_blocks(z)
                            if z >= 2:
                                pe.wait_ge(vector_done, upto("pvfree", "c", z - 2))
                            for ti, p_ in enumerate(pos):
                                blk = 8 + p_ - 3 if p_ >= 3 else (p_ - 1 if i == 0 else 5 + p_ if i == 7 else i - 1 + p_)
                                pe.wait_ge(vector_done, upto("ptl", "c", tcount(z, "c") + ti))
                                mm(PS[:, 6 + z % 2, :], VS[:, blk, kv, :], PTH[:, p_, :], start=ti == 0, stop=False)
                                ins = mm(PS[:, 6 + z % 2, :], VS[:, blk, kv, :], PTL[:, p_, :], start=False,
                                         stop=ti == len(pos) - 1)
                            ins.then_inc(products_done, 1)
                            did(products_done, ("pv", "c", z))
                        for z, ti in tiles.get(u, []):
                            tb = tcount(z, "c") + ti
                            p_ = key_blocks(z)[ti]
                            if tb >= 2:
                                pe.wait_ge(vector_done, upto("ptl", "c", tb - 2))
                            for hh in range(4):
                                pe.wait_ge(gpsimd_done, upto("P", "c", z, hh))
                                ins = nc.tensor.transpose(PS[:, 4 + tb % 2, hh * P:(hh + 1) * P],
                                                          PB[z % 2][:, hh, p_ * P:(p_ + 1) * P], IDF[:, :])
                            ins.then_inc(products_done, 1)
                            did(products_done, ("tr", "c", tb))
                elif kind == "attf":
                    for job_before in prev[name]:
                        pe.wait_ge(*of("free", job_before))
                    pe.wait_ge(scalar_done, upto("masks2"))
                    tiles = spread("f")
                    for u in range(4 * 16 + 6):
                        s, i4 = u // 4, u % 4
                        if s < 16:
                            hd, G = s // 2, s % 2
                            i = 4 * G + i4
                            n = (i + 1) * P
                            sb = 2 * (u % 2)
                            if u >= 2:
                                pe.wait_ge(vector_done, upto("mx", "f", u - 2))
                            pe.wait_ge(vector_done, upto("ql2", hd))
                            q = slice(i * P, (i + 1) * P)
                            for b in range(G + 1):
                                w_ = min(n - b * HALF, HALF)
                                o_ = PS[:, sb + b, 0:w_]
                                kx = KS2[hd % 2][:, b * HALF:b * HALF + w_]
                                mm(o_, QH2[hd % 2][:, q], kx, start=True, stop=False, skip_group_check=True)
                                ins = mm(o_, QL2[hd % 2][:, q], kx, start=False, stop=b < G, skip_group_check=True)
                                if b == G:
                                    ins = mm(PS[:, sb + b, w_ - P:w_], IDR[:, :], MKR2[:, :], start=False,
                                             stop=True, skip_group_check=True)
                            ins.then_inc(products_done, 1)
                            did(products_done, ("sc", "f", u))
                        if i4 == 0 and s >= 2:
                            z = s - 2
                            hd, G = z // 2, z % 2
                            pe.wait_ge(vector_done, upto("vs2", hd))
                            if z >= 2:
                                pe.wait_ge(vector_done, upto("pvfree", "f", z - 2))
                            nj = 4 * G + 4
                            for j in range(nj):
                                c0 = max(0, j - 4 * G) * P
                                pe.wait_ge(vector_done, upto("ptl", "f", tcount(z, "f") + j))
                                for x, t_ in enumerate((PT2H, PT2L)):
                                    ins = mm(PS[:, 6 + z % 2, c0:HALF], VS2[hd % 2][:, j, :], t_[:, j, c0:HALF],
                                             start=j == 0 and x == 0, stop=j == nj - 1 and x == 1,
                                             skip_group_check=True)
                            ins.then_inc(products_done, 1)
                            did(products_done, ("pv", "f", z))
                        for z, j in tiles.get(u, []):
                            tb = tcount(z, "f") + j
                            if tb >= 2:
                                pe.wait_ge(vector_done, upto("ptl", "f", tb - 2))
                            for q4 in range(max(0, j - 4 * (z % 2)), 4):
                                pe.wait_ge(gpsimd_done, upto("P", "f", z, q4))
                                ins = nc.tensor.transpose(PS[:, 4 + tb % 2, q4 * P:(q4 + 1) * P],
                                                          PB2[z % 2][:, q4, j * P:(j + 1) * P], IDF[:, :])
                            ins.then_inc(products_done, 1)
                            did(products_done, ("tr", "f", tb))

        @block.scalar
        def _(act):
            A = nc.scalar.activation



            stg, outn = [0], []

            def qdma(name, group, j, off, w):
                act.wait_ge(vector_done, upto("kr", name, j))
                act.dma_start(QD[:, group[1] * 4 + j, off:off + w],
                              tm(name, 2 * j)).then_inc(stage_free[TMAT[(name, 2 * j)] % 3], 16)
                did(stage_free[TMAT[(name, 2 * j)] % 3], ("tm", (name, 2 * j)), by=16)

            def load_q(act, b):
                kv, hf = b // 2, b % 2
                if b >= 2:
                    act.wait_ge(vector_done, upto("qs", b - 2, 1))
                act.dma_start(RQ[b % 2][:, :, :],
                              QD[:, 2 * kv:2 * kv + 2, hf * HALF:(hf + 1) * HALF]).then_inc(rq_loaded[b % 2], 16)
                did(rq_loaded[b % 2], ("rql", b), by=16)

            def prep_q_act(b, t):
                act.wait_ge(rq_loaded[b % 2], upto("rql", b))
                if b >= 2:
                    act.wait_ge(products_done, upto("sc", "c", 16 * (b - 1) - 1))
                x, q = RQ[b % 2][:, t, :], QS[b % 2][0]
                for half in range(2):
                    own_ = slice(64 * half, 64 * half + 64)
                    for o_ in (slice(0, 64), slice(64, P)):
                        A(q[o_, 2 * t + half, :], x[own_, :], ACT.Copy).then_inc(scalar_done, 1)
                        did(scalar_done, ("qh", b, t))

            def weights_high(z, ti):
                tb = tcount(z, "c") + ti
                act.wait_ge(products_done, upto("tr", "c", tb))
                if z >= 1:
                    act.wait_ge(products_done, upto("pv", "c", z - 1))
                A(PTH[:, key_blocks(z)[ti], :], PS[:, 4 + tb % 2, :], ACT.Copy).then_inc(scalar_done, 1)
                did(scalar_done, ("pth", "c", tb))

            def weights_high2(z, j):
                tb = tcount(z, "f") + j
                c0 = max(0, j - 4 * (z % 2)) * P
                if z == 0:
                    act.wait_ge(spilled, upto("ust"))
                act.wait_ge(products_done, upto("tr", "f", tb))
                if z >= 1:
                    act.wait_ge(products_done, upto("pv", "f", z - 1))
                A(PT2H[:, j, c0:HALF], PS[:, 4 + tb % 2, c0:HALF], ACT.Copy).then_inc(scalar_done, 1)
                did(scalar_done, ("pth", "f", tb))

            def pv_act(z):
                act.wait_ge(products_done, upto("pv", "c", z))
                if z:
                    act.wait_ge(vector_done, upto("ota", z - 1))
                src = PS[:, 6 + z % 2, :].rearrange("p (r e q) -> p e r q", e=2, q=P)
                A(OTT[0:64, :, :], src[64:P, 0, :, :], ACT.Copy).then_inc(scalar_done, 1)
                did(scalar_done, ("ott", z))
                A(OTT[64:P, :, :], src[0:64, 1, :, :], ACT.Copy).then_inc(scalar_done, 1)
                did(scalar_done, ("ott", z))

            def store_o(act, b):
                act.wait_ge(vector_done, upto("og", b))
                kv, hf = b // 2, b % 2
                act.dma_start(OD[:, 2 * kv:2 * kv + 2, hf * HALF:(hf + 1) * HALF],
                              OT[b % 2][:, :, :]).then_inc(ot_stored[b % 2], 16)
                did(ot_stored[b % 2], ("ost", "c", b), by=16)

            def load_pair(act, p_):
                if p_:
                    act.wait_ge(vector_done, upto("vs2", 2 * p_ - 1))
                for dst, src in ((RQ2[:, :], QD[:, p_, :]), (RK2[:, :], KD2[:, p_, :]),
                                 (RV2[:, :, :], VD2[:, p_ * P:(p_ + 1) * P].rearrange("(t q) n -> q t n", q=P))):
                    act.dma_start(dst, src).then_inc(rq_loaded[0], 16)
                    did(rq_loaded[0], ("pair", p_), by=16)

            def load_nb(act, hd):
                if hd >= 2:
                    act.wait_ge(vector_done, upto("mx", "f", 4 * (2 * (hd - 2) + 1) + 3))
                act.dma_start(NBC[hd % 2][:, :], CUM[hd, :].partition_broadcast(P)).then_inc(nb_loaded[hd % 2], 16)
                did(nb_loaded[hd % 2], ("nbl", hd), by=16)

            def prep2_act(hd):
                b, half = hd % 2, hd % 2
                act.wait_ge(rq_loaded[0], upto("pair", hd // 2))
                if hd >= 2:
                    act.wait_ge(products_done, upto("sc", "f", 8 * hd - 9))
                own_ = slice(64 * half, 64 * half + 64)
                for o_ in (slice(0, 64), slice(64, P)):
                    A(QH2[b][o_, :], RQ2[own_, :], ACT.Copy).then_inc(scalar_done, 1)
                    did(scalar_done, ("qh2", hd))
                A(KS2[b][own_, :], RK2[own_, :], ACT.Copy).then_inc(scalar_done, 1)
                did(scalar_done, ("qh2", hd))

            def prep2v_act(hd):
                b, half = hd % 2, hd % 2
                act.wait_ge(rq_loaded[0], upto("pair", hd // 2))
                if hd >= 2:
                    act.wait_ge(products_done, upto("pv", "f", 2 * hd - 3))
                A(VS2[b][:, :, 0:64], RV2[:, :, 64 * half:64 * half + 64], ACT.Copy).then_inc(scalar_done, 1)
                did(scalar_done, ("vh2", hd))

            def pv2_act(z):
                hd = z // 2
                act.wait_ge(products_done, upto("pv", "f", z))
                if z:
                    act.wait_ge(vector_done, upto("ota2", z - 1))
                a_, b_ = (slice(0, 64), slice(64, P)) if hd % 2 == 0 else (slice(64, P), slice(0, 64))
                A(OTT2[a_, :], PS[b_, 6 + z % 2, :], ACT.Copy).then_inc(scalar_done, 1)
                did(scalar_done, ("ott2", z))

            def store_o2(act, p_):
                act.wait_ge(vector_done, upto("ota2", 4 * p_ + 3))
                act.dma_start(OD[:, p_, :], OT2[p_ % 2][:, :]).then_inc(ot_stored[p_ % 2], 16)
                did(ot_stored[p_ % 2], ("ost", "f", p_), by=16)


            for e in TL:
                kind, name = e["kind"], e["name"]
                part = e.get("part")
                if "scalar_done" in counts:
                    act.wait_ge(scalar_done, so_far(scalar_done))
                if kind == "params":
                    act.wait_ge(products_done, upto("job", name))
                    A(PC[:, 0:192], PS[:, 0, 0:192], ACT.Copy).then_inc(scalar_done, 1)
                    did(scalar_done, "pc0")
                    A(PC[:, 256:380], PS[:, 0, 256:380], ACT.Copy).then_inc(scalar_done, 1)
                    did(scalar_done, "pc", ("free", name))
                    act.wait_ge(scalar_done, so_far(scalar_done))
                    for j, nm in enumerate(("c", "c_ctx", "c_2", "c_2")):
                        A(CS[:, :, j], cols(nm), ACT.Silu).then_inc(scalar_done, 1)
                        did(scalar_done, "cs")
                    act.wait_ge(rows_loaded, upto("rows"))
                    A(IDR[:, :], IDF[:, :], ACT.Copy).then_inc(scalar_done, 1)
                    did(scalar_done, "idr")
                elif kind == "tx":
                    act.wait_ge(products_done, upto("job", name))
                    k = e["k"]
                    A(XX[:, k, :].rearrange("p (b n) -> p b n", n=HALF), PS[:, 4 * setof[name]:4 * setof[name] + 2, :],
                          ACT.Copy).then_inc(scalar_done, 1)
                    did(scalar_done, ("xt", k))
                    A(XC[:, k, :], bank(name, 2, C), ACT.Copy).then_inc(scalar_done, 1)
                    did(scalar_done, ("X", 0, k), ("free", name))
                elif kind == "ada":
                    act.wait_ge(products_done, upto("job", name))
                    for i in range(2):
                        for use_before in tm_before(name, i):
                            act.wait_ge(*of("tm", use_before))
                        A(tm(name, i, p1=2), bank(name, i, p1=2), ACT.Copy).then_inc(scalar_done, 1)
                        did(scalar_done, ("arow", e["v"]), ("free", name))
                elif kind == "small":
                    act.wait_ge(products_done, upto("job", name))
                    A(SWH[:, :, :].rearrange("p h q -> p (h q)"), bank(name, 0), ACT.Copy).then_inc(scalar_done, 1)
                    did(scalar_done, "swh")
                    A(CHH[:, :], CHRAW[:, :], ACT.Copy).then_inc(scalar_done, 1)
                    did(scalar_done, "smallh")
                elif kind == "sum":
                    n = e["n"]
                    w = PARTS[part][1]
                    for k in range(KT):
                        src = xs(part, k) if n in (0, 1, 2, 4) else ys(part, k)
                        if n == 0:
                            act.wait_ge(*of("X", n, k))
                        else:
                            act.wait_ge(*of("X", n, part, k))
                        for use_before in tm_before(name, k):
                            act.wait_ge(*of("tm", use_before))
                        A(tm(name, k, w), src, ACT.Square).then_inc(scalar_done, 1)
                        did(scalar_done, ("sq", n, part, k))
                    if n == 2:
                        for k in range(KT):
                            for use_before in tm_before(name, 8 + k):
                                act.wait_ge(*of("tm", use_before))
                            A(tm(name, 8 + k, w), xs(part, k), ACT.Square, scale=col("final_g", k)).then_inc(scalar_done, 1)
                            did(scalar_done, ("sqg", n, part, k))
                elif kind in ("stat", "statpost"):
                    n = e["n"]
                    w = PARTS[part][1]
                    nm = ("stat", n, part)
                    act.wait_ge(products_done, upto("job", nm))
                    act.wait_ge(gpsimd_done, upto("eps"))
                    if n == 2:
                        A(SUM[:, 0:w], bank(nm, 0, w), ACT.Sqrt, scale=1.0 / D, bias=EPT[:, :]).then_inc(scalar_done, 1)
                        did(scalar_done, ("sq1", n, part))
                        act.wait_ge(vector_done, upto("r1sq", n, part))
                        A(RST[:, 0:w], tm(name, 0, w), ACT.Sqrt, scale=1.0 / D, bias=EPT[:, :]).then_inc(scalar_done, 1)
                        did(scalar_done, ("sqrt", n, part), ("tm", (name, 0)))
                    else:
                        A((RST0[part] if n == 0 else RST)[:, 0:w], bank(nm, 0, w), ACT.Sqrt, scale=1.0 / D, bias=EPT[:, :]).then_inc(scalar_done, 1)
                        did(scalar_done, ("sqrt", n, part), ("free", nm))
                elif kind == "apply":
                    n = e["n"]
                    w = PARTS[part][1]
                    for k in range(KT):
                        act.wait_ge(vector_done, upto("t", n, part, k))
                        act.wait_ge(vector_done, upto("mod", {0: 1, 1: 4, 2: 7, 4: 10}[n]))
                        act.wait_ge(vector_done, upto("coef", n))
                        t_ = tm(name, k, w)
                        A(t_, t_, ACT.Identity, scale=acoef(n, part, k), bias=shift(n, part, k)).then_inc(scalar_done, 1)
                        did(scalar_done, ("h", n, part, k))
                        act.wait_ge(scalar_done, so_far(scalar_done))
                        if n in HREADERS and part in HREADERS[n]:
                            act.wait_ge(products_done, upto("job", HREADERS[n][part]))
                        elif n == 0:
                            act.wait_ge(products_done, upto("job", ("tx", 7)))
                            act.wait_ge(products_done, upto("job", ("adac", 1)))
                        A(hs(part, k, 0), t_, ACT.Copy).then_inc(scalar_done, 1)
                        did(scalar_done, ("hi", n, part, k))
                elif kind == "spill":
                    n = e["n"]
                    if n == 0:
                        act.wait_ge(scalar_done, upto("X", n, 7))
                    else:
                        act.wait_ge(vector_done, upto("XW", n))
                    if n == 0:
                        act.dma_start(XCD, XC[:, :, :]).then_inc(spilled, 16)
                        did(spilled, ("spill", n), by=16)
                    act.dma_start(XR, XX[:, :, :]).then_inc(spilled, 16)
                    did(spilled, ("spill", n), by=16)
                    if n == 1:
                        act.wait_ge(vector_done, upto("AB", 7))
                        act.wait_ge(vector_done, upto("AB", "c"))
                        act.dma_start(ROPE[:, :, :], a["t_rope"]).then_inc(tables_loaded, 16)
                        did(tables_loaded, "rope", by=16)
                elif kind == "reload":
                    n = e["n"]
                    if n == 0:
                        act.wait_ge(vector_done, upto("H", "ysplit", 0, "c", 7))
                        act.wait_ge(scalar_done, so_far(scalar_done))
                        act.dma_start(XC[:, :, :], XCD).then_inc(x_loaded, 16)
                        did(x_loaded, ("reload", n), by=16)
                    elif n == 1:
                        act.wait_ge(products_done, upto("pv", "c", 31))
                        act.wait_ge(spilled, upto("spill", 1))
                    else:
                        act.wait_ge(products_done, upto("pv", "f", 15))
                        act.wait_ge(spilled, upto("spill", 2))
                    act.dma_start(XX[:, :, :], XR).then_inc(x_loaded, 16)
                    did(x_loaded, ("reload", n), by=16)
                elif kind in ("lin", "tok", "kv"):
                    layer, group = e["layer"], e["group"]
                    act.wait_ge(products_done, upto("job", name))
                    off, w = PARTS[part]
                    if layer == "ab" and group == "xb":
                        if part != "h0":
                            act.wait_ge(products_done, upto("job", ("chan", {"h1": "h0", "c": "h1"}[part], 1)))
                        for g in range(4):
                            A(VBH[:, g, 0:w], bank(name, g, w), ACT.Copy).then_inc(scalar_done, 1)
                            did(scalar_done, ("vbh", part, g))
                    elif layer == "ab" and group in ("u", "gb"):
                        act.wait_ge(spilled, upto("spill", 0))
                        act.wait_ge(vector_done, upto("H", "apply", 0, "c", 7))
                        k0, f = (0, ACT.Copy) if group == "u" else (4, ACT.Silu)
                        src = PS[:, 4 * setof[name]:4 * setof[name] + 4, 0:w]
                        dst = XC[:, k0:k0 + 4, :] if part == "c" else XX[:, k0:k0 + 4, off:off + w]
                        A(dst, src, f).then_inc(scalar_done, 1)
                        did(scalar_done, (group, part), ("free", name))
                    elif layer == "ab" and group == "ga":
                        for j in range(4):
                            for use_before in tm_before(name, j):
                                act.wait_ge(*of("tm", use_before))
                            A(tm(name, j, w), bank(name, j, w), ACT.Silu).then_inc(scalar_done, 1)
                            did(scalar_done, ("gasilu", part, j), ("free", name))
                    elif layer == "ab" and group == "v":
                        act.wait_ge(vector_done, upto("mv", part))
                        act.wait_ge(gpsimd_done, upto("eps"))
                        nt = w // P
                        A(SM[:, 0:nt], MV[:, 0:nt, 1], ACT.Sqrt, bias=EPT[:, :]).then_inc(scalar_done, 1)
                        did(scalar_done, ("vsd", part))
                        for tb in range(nt):
                            act.wait_ge(vector_done, upto("vf", part, tb))
                            A(VBH[:, tb, :], tm(name, tb), ACT.Copy).then_inc(scalar_done, 1)
                            did(scalar_done, ("vh", part, tb))
                    elif layer == "c" and group == "kv":
                        per = 1 if part == "c" else 2
                        for j in range(2):
                            for use_before in tm_before(name, per * j):
                                act.wait_ge(*of("tm", use_before))
                            src = tm(name, per * j, w)
                            A(src, bank(name, j, w), ACT.Copy).then_inc(scalar_done, 1)
                            did(scalar_done, ("kf", name, j))
                            if part == "c":
                                act.wait_ge(scalar_done, so_far(scalar_done))
                            else:
                                act.wait_ge(vector_done, upto("kr", name, j))
                            c0 = T if part == "c" else off
                            act.wait_ge(spilled, upto("spill", 1))
                            A(KS[0:64, 2 * j, c0:c0 + w], src[0:64, :], ACT.Copy).then_inc(scalar_done, 1)
                            did(scalar_done, ("khi", part, j, 0))
                            A(KS[64:P, 2 * j + 1, c0:c0 + w], src[64:P, :], ACT.Copy).then_inc(scalar_done, 1)
                            did(scalar_done, ("khi", part, j, 1))
                        for tb in range(0, w // P, 2):
                            b = (8 if part == "c" else off // P) + tb
                            A(VS[:, b:b + 2, :, 0:64], bank(name, 2 + tb // 2).rearrange("p (t h d) -> p t h d", d=64, h=4),
                                  ACT.Copy).then_inc(scalar_done, 1)
                            did(scalar_done, ("vhi", part, tb))
                    elif layer == "c":
                        if group[0] == "q":
                            for j in range(4):
                                for use_before in tm_before(name, 2 * j):
                                    act.wait_ge(*of("tm", use_before))
                                A(tm(name, 2 * j), bank(name, j), ACT.Copy, scale=-SCALE).then_inc(scalar_done, 1)
                                did(scalar_done, ("kf", name, j), ("free", name))
                                if j:
                                    qdma(name, group, j - 1, off, w)
                            qdma(name, group, 3, off, w)
                        else:
                            for j in range(4):
                                for use_before in tm_before(name, j):
                                    act.wait_ge(*of("tm", use_before))
                                A(tm(name, j), bank(name, j), ACT.Silu).then_inc(scalar_done, 1)
                                did(scalar_done, ("gs", name, j), ("free", name))
                                act.wait_ge(scalar_done, so_far(scalar_done))
                                act.dma_start(GD[:, group[1] * 4 + j, off:off + w],
                                              tm(name, j)).then_inc(stage_free[TMAT[(name, j)] % 3], 16)
                                did(stage_free[TMAT[(name, j)] % 3], ("tm", (name, j)), by=16)
                    elif layer == "b2":
                        if group == "cv":
                            if part == "h0":
                                act.wait_ge(vector_done, upto("upad"))
                            src = PS[:, 4 * setof[name]:4 * setof[name] + 4, 0:w]
                            A(U[:, :, 30 + off:30 + off + w], src, ACT.Copy).then_inc(scalar_done, 1)
                            did(scalar_done, ("uv", part), ("free", name))
                        elif group == "cg":
                            for j in range(4):
                                for use_before in tm_before(name, j):
                                    act.wait_ge(*of("tm", use_before))
                                A(tm(name, j, w), bank(name, j, w), ACT.Sigmoid).then_inc(scalar_done, 1)
                                did(scalar_done, ("gasilu", name, j), ("free", name))
                        else:
                            for j in range(4):
                                for use_before in tm_before(name, j):
                                    act.wait_ge(*of("tm", use_before))
                                A(tm(name, j), bank(name, j), ACT.Copy,
                                  scale=-SCALE if group == "q2" else 1.0).then_inc(scalar_done, 1)
                                did(scalar_done, ("gs", name, j), ("free", name))
                                act.wait_ge(scalar_done, so_far(scalar_done))
                                dst = (QD[:, j, off:off + w] if group == "q2" else KD2[:, j, off:off + w]
                                       if group == "k2" else VD2[off + j * P:off + (j + 1) * P, :])
                                act.dma_start(dst, tm(name, j)).then_inc(stage_free[TMAT[(name, j)] % 3], 16)
                                did(stage_free[TMAT[(name, j)] % 3], ("tm", (name, j)), by=16)
                    elif layer == "wo":
                        if group == 0 and part == "h0":
                            act.wait_ge(vector_done, upto("H", "hload", 2, "h1", 7))
                        for j in range(4):
                            A(Y[:, group * 4 + j, off:off + w], bank(name, j), ACT.Copy).then_inc(scalar_done, 1)
                            did(scalar_done, ("X", 3, part, group * 4 + j), ("free", name))
                    elif layer == "fi":
                        ch = group
                        for j in range(2):
                            for use_before in tm_before(name, j):
                                act.wait_ge(*of("tm", use_before))
                            A(tm(name, j), bank(name, j), ACT.Silu).then_inc(scalar_done, 1)
                            did(scalar_done, ("gsl", ch, part, j))
                        for j in range(2):
                            act.wait_ge(vector_done, upto("av", ch, part, j))
                            if ch:
                                act.wait_ge(products_done, upto("job", ("fo", ch - 1, 1, part)))
                            A(AHH[:, j, off:off + w], tm(name, j), ACT.Copy).then_inc(scalar_done, 1)
                            did(scalar_done, ("ahi", ch, part, j))
                    elif layer == "fo" and e["ch"] == 0:
                        src = PS[:, 4 * setof[name]:4 * setof[name] + 4, 0:w]
                        A(Y[:, group * 4:group * 4 + 4, off:off + w], src, ACT.Copy).then_inc(scalar_done, 1)
                        did(scalar_done, ("yacc", group, part), ("free", name))
                elif kind == "chan":
                    act.wait_ge(products_done, upto("job", name))
                    if stg[0]:
                        act.wait_ge(spilled, upto("abst", stg[0] - 1))
                    A(STG[:, :], PS[:, 4 * setof[name]:4 * setof[name] + 4, :].rearrange("p b n -> p (b n)"),
                          ACT.Copy).then_inc(scalar_done, 1)
                    did(scalar_done, ("free", name))
                    act.wait_ge(scalar_done, so_far(scalar_done))
                    t0 = (T if part == "c" else PARTS[part][0]) + e["half"] * 256
                    act.dma_start(ABD[t0:t0 + 256, :].rearrange("(t p) n -> p t n", p=P),
                                  STG[:, :].rearrange("p (t n) -> p t n", n=D)).then_inc(spilled, 16)
                    did(spilled, ("abst", stg[0]), by=16)
                    stg[0] += 1
                elif kind == "abload":
                    a_ = e["a"]
                    if a_ == 0:
                        act.wait_ge(spilled, upto("abst", stg[0] - 1))
                        act.wait_ge(products_done, upto("job", ("spat", "c")))
                    else:
                        act.wait_ge(vector_done, upto("abs", 3 if a_ == "c" else a_ - 1, 1))
                    idx = (8, 9) if a_ == "c" else (a_, a_ + 4)
                    for x in range(2):
                        act.dma_start(ARAW[:, x, :], ABD[idx[x] * P:(idx[x] + 1) * P, :]).then_inc(ab_loaded[x], 16)
                        did(ab_loaded[x], ("abl", a_, x), by=16)
                    for x in range(2):
                        act.wait_ge(products_done, upto("job", ("gb", "c" if a_ == "c" else "h1")))
                        if a_ != "c":
                            act.wait_ge(vector_done, upto("abs", a_, x))
                        if a_ == "c":
                            hh = HCH[:, :, :].rearrange("p k c -> p (k c)")[:, x * D:(x + 1) * D]
                            act.wait_ge(ab_loaded[x], upto("abl", a_, x))
                            src = ARAW[:, x, :]
                        else:
                            hh = HXH[:, a_ + 4 * x, :]
                            src = ASD[:, x, :]
                        A(hh, src, ACT.Copy).then_inc(scalar_done, 1)
                        did(scalar_done, ("abh", a_, x))
                elif kind == "ysplit":
                    act.wait_ge(products_done, upto("job", ("dft", 1 if part != "c" else "c")))
                    if part == "h0":
                        act.wait_ge(vector_done, upto("yb", 0))
                        act.wait_ge(vector_done, upto("yb", 1))
                        act.wait_ge(vector_done, upto("ya", "h0"))
                    act.wait_ge(vector_done, upto("ya", part))
                    if part == "c":
                        act.wait_ge(vector_done, upto("yb", "c"))
                    else:
                        act.wait_ge(vector_done, upto("yb", 1))
                    for k in range(KT):
                        A(hs(part, k, 0), xs(part, k), ACT.Copy).then_inc(scalar_done, 1)
                        did(scalar_done, ("yh", part, k))
                elif kind == "hload":
                    n = e["n"]
                    b = 0 if part == "h0" else 1
                    off, w = PARTS[part]
                    act.wait_ge(products_done, upto("job", ("adac", 8 if n == 1 else 10, None)))
                    if n == 1:
                        act.wait_ge(ot_stored[0], upto("ost", "c", 6))
                        act.wait_ge(ot_stored[1], upto("ost", "c", 7))
                    else:
                        act.wait_ge(ot_stored[1], upto("ost", "f", 3))
                        act.wait_ge(spilled, upto("ust"))
                        act.wait_ge(ot_stored[0], upto("ost", "f", 2))
                    for k in range(0, KT, 2):
                        act.dma_start(LR[b][:, k:k + 2, :], OD[:, k:k + 2, off:off + w]).then_inc(h_loaded[k // 2], 16)
                        did(h_loaded[k // 2], ("lr", n, part, k // 2), by=16)
                    if n == 1:
                        act.wait_ge(products_done, upto("pv", "c", 31))
                    else:
                        act.wait_ge(products_done, upto("pv", "f", 15))
                    for k in range(KT):
                        act.wait_ge(h_loaded[k // 2], upto("lr", n, part, k // 2))
                        A(hs(part, k, 0), LR[b][:, k, :], ACT.Copy).then_inc(scalar_done, 1)
                        did(scalar_done, ("lh", n, part, k))
                elif kind == "spat":
                    pass
                elif kind == "flog":
                    act.wait_ge(products_done, upto("job", name))
                    act.wait_ge(vector_done, upto("fmin"))
                    FA, FB, FC = (x[0:8, :] for x in FL)
                    A(FB, FA, ACT.Abs).then_inc(scalar_done, 1)
                    did(scalar_done, "fabs")
                    act.wait_ge(scalar_done, so_far(scalar_done))
                    A(FB, FB, ACT.Exp, scale=-1.0).then_inc(scalar_done, 1)
                    did(scalar_done, "fexp")
                    act.wait_ge(scalar_done, so_far(scalar_done))
                    A(FB, FB, ACT.Ln, bias=ONF[0:8, 0:1]).then_inc(scalar_done, 1)
                    did(scalar_done, "fln")
                    act.wait_ge(vector_done, upto("cum"))
                    act.dma_start(CUM, FB).then_inc(cum_stored, 16)
                    did(cum_stored, "cumst", by=16)
                elif kind == "conv":
                    if e["i"] == 0:
                        act.wait_ge(vector_done, upto("ug2", "h1"))
                        act.wait_ge(vector_done, upto("cum"))
                        act.wait_ge(cum_stored, upto("cumst"))
                        act.wait_ge(spilled, upto("spill", 2))
                    for t_ in CONV_SHARES.get(e["i"], ()):
                        wc = PC[:, 256 + 4 * t_ + 3:257 + 4 * t_ + 3]
                        src = U[:, 3, t_:t_ + T]
                        if t_ == 0:
                            A(CA[:, 3, :], src, ACT.Identity, scale=wc, bias=col("conv_b_2", 3)).then_inc(scalar_done, 1)
                        else:
                            if t_ > 3:
                                act.wait_ge(gpsimd_done, upto("conv", 3, t_ - 3, 1))
                            A(CTMP[t_ % 3][:, :], src, ACT.Identity, scale=wc).then_inc(scalar_done, 1)
                        did(scalar_done, ("tap", t_))
                elif kind == "mask2":
                    act.dma_start(MKF2[:, :], a["t_mask"][:, 1, :]).then_inc(late_loaded, 16)
                    did(late_loaded, "mask2l", by=16)
                    act.wait_ge(late_loaded, upto("mask2l"))
                    A(MKR2[:, :], MKF2[:, :], ACT.Copy).then_inc(scalar_done, 1)
                    did(scalar_done, "masks2")
                elif kind == "cmean":
                    act.wait_ge(products_done, upto("job", name))
                    A(CRST[:, :].rearrange("p (b n) -> p b n", n=HALF), PS[:, 4 * setof[name]:4 * setof[name] + 2, :],
                      ACT.Copy, scale=1.0 / 512).then_inc(scalar_done, 1)
                    did(scalar_done, "cmu", ("free", name))
                    for j in range(4):
                        act.wait_ge(vector_done, upto("cc", j))
                        if j >= 2:
                            act.wait_ge(vector_done, upto("csqr", 1))
                        A(CSQ[j % 2][:, :], CA[:, j, :], ACT.Square).then_inc(scalar_done, 1)
                        did(scalar_done, ("csq", j))
                elif kind == "cvar":
                    act.wait_ge(products_done, upto("job", name))
                    A(CRST[:, :].rearrange("p (b n) -> p b n", n=HALF), PS[:, 4 * setof[name]:4 * setof[name] + 2, :],
                      ACT.Sqrt, scale=1.0 / 512, bias=EPT[:, :]).then_inc(scalar_done, 1)
                    did(scalar_done, "csd", ("free", name))
                    for j in range(4):
                        act.wait_ge(vector_done, upto("cn", j))
                        x = CA[:, j, :]
                        A(x, x, ACT.Silu, scale=col("conv_ln_g_2", j), bias=col("conv_ln_b_2", j)).then_inc(scalar_done, 1)
                        did(scalar_done, "cu")
                    act.wait_ge(scalar_done, so_far(scalar_done))
                    act.dma_start(OD[:, 4:8, :], CA[:, :, :]).then_inc(spilled, 16)
                    did(spilled, "ust", by=16)
                elif kind == "out":
                    act.wait_ge(products_done, upto("job", name))
                    off = PARTS[part][0] + e["half"] * 256
                    b = len(outn) % 2
                    if len(outn) >= 2:
                        act.wait_ge(ot_stored[(len(outn) - 2) % 2], upto("outst", len(outn) - 2))
                    dst = OUTS[b][:, :]
                    A(dst, PS[:, 4 * setof[name]:4 * setof[name] + 4, :].rearrange("p b n -> p (b n)"), ACT.Copy).then_inc(scalar_done, 1)
                    did(scalar_done, ("free", name))
                    act.wait_ge(scalar_done, so_far(scalar_done))
                    act.dma_start(a["out"][0][off:off + 256, :].rearrange("(t p) d -> p t d", p=P),
                                  dst.rearrange("p (t d) -> p t d", d=D)).then_inc(ot_stored[b], 16)
                    did(ot_stored[b], ("outst", len(outn)), by=16)
                    outn.append(1)
                elif kind == "attc_pre":
                    act.dma_start(SINK[:, :],
                                  a["sink_logit"].rearrange("l h -> (l h)").partition_broadcast(P)).then_inc(late_loaded, 16)
                    did(late_loaded, "sinkm", by=16)
                    act.dma_start(MKF[:, :, :], a["t_mask"]).then_inc(late_loaded, 16)
                    did(late_loaded, "sinkm", by=16)
                    for j in range(1, 4):
                        act.wait_ge(*of("tm", (("q", 1, "h1"), 2 * j)))
                    load_q(act, 0)
                    act.wait_ge(late_loaded, upto("sinkm"))
                    A(MKR[:, :, :], MKF[:, :, :], ACT.Copy).then_inc(scalar_done, 1)
                    did(scalar_done, "masks")
                elif kind == "attc":
                    for job_before in prev[name]:
                        act.wait_ge(*of("free", job_before))
                    act.wait_ge(products_done, upto("job", ("g", 1, "h1")))
                    for j in range(1, 4):
                        act.wait_ge(*of("tm", (("g", 1, "h1"), j)))
                    prep_q_act(0, 0)
                    prep_q_act(0, 1)
                    tiles = spread("c")
                    for u in range(4 * 33 + 3):
                        s, h = u // 4, u % 4
                        if h == 0 and s % 4 == 0 and s < 32:
                            b = s // 4
                            if b + 1 < 8:
                                load_q(act, b + 1)
                            if b >= 2:
                                act.wait_ge(vector_done, upto("og", b - 2))
                            kv, hf = b // 2, b % 2
                            act.dma_start(GT[b % 2][:, :, :],
                                          GD[:, 2 * kv:2 * kv + 2, hf * HALF:(hf + 1) * HALF]).then_inc(g_loaded[b % 2], 16)
                            did(g_loaded[b % 2], ("gl", b), by=16)
                        if h == 0 and s >= 3 and (s - 3) % 4 == 3:
                            store_o(act, (s - 3) // 4)
                        for z, ti in tiles.get(u, [])[:2]:
                            weights_high(z, ti)
                        if s < 32:
                            i = s % 8
                            lo = 256 if i in (0, 7) else 128
                            src = PS[:, 2 * (u % 2):2 * (u % 2) + 2, :].rearrange("p b n -> p (b n)")[:, lo:769]
                            act.wait_ge(vector_done, upto("mx", "c", u))
                            if s >= 2:
                                act.wait_ge(products_done, upto("tr", "c", tcount(s - 1, "c") - 1))
                            A(PB[s % 2][:, h, lo - 128:641], src, ACT.Exp, scale=-1.0, bias=MX[s % 2][:, h:h + 1],
                              accum_out=SU[s % 2][:, h:h + 1]).then_inc(scalar_done, 1)
                            did(scalar_done, ("exp", "c", u))
                        for z, ti in tiles.get(u, [])[2:]:
                            weights_high(z, ti)
                        if h == 2 and s >= 2:
                            pv_act(s - 2)
                        if h == 3 and s < 32 and s % 4 in (1, 2) and s // 4 + 1 < 8:
                            prep_q_act(s // 4 + 1, s % 4 - 1)
                    store_o(act, 7)
                elif kind == "attf_pre":
                    act.wait_ge(products_done, upto("job", "flog"))
                    act.wait_ge(cum_stored, upto("cumst"))
                    for j in range(1, 4):
                        act.wait_ge(*of("tm", (("v2", "h1"), j)))
                    load_pair(act, 0)
                    load_nb(act, 0)
                    prep2_act(0)
                    prep2v_act(0)
                    load_nb(act, 1)
                elif kind == "attf":
                    for job_before in prev[name]:
                        act.wait_ge(*of("free", job_before))
                    tiles = spread("f")
                    for u in range(4 * 17 + 3):
                        s, i4 = u // 4, u % 4
                        if i4 == 0 and s >= 3 and (s - 3) % 4 == 3:
                            store_o2(act, (s - 3) // 4)
                        if i4 == 0 and s < 16 and s % 2 == 0 and s > 0 and s // 2 + 1 < 8:
                            load_nb(act, s // 2 + 1)
                        for z, j in tiles.get(u, [])[:2]:
                            weights_high2(z, j)
                        if s < 16:
                            n = (4 * (s % 2) + i4 + 1) * P
                            x = PB2[s % 2][:, i4, 0:n]
                            act.wait_ge(vector_done, upto("mx", "f", u))
                            A(x, x, ACT.Exp, scale=-1.0, bias=MX[s % 2][:, i4:i4 + 1],
                              accum_out=SU[s % 2][:, i4:i4 + 1]).then_inc(scalar_done, 1)
                            did(scalar_done, ("exp", "f", u))
                        for z, j in tiles.get(u, [])[2:]:
                            weights_high2(z, j)
                        if i4 == 2 and s >= 2:
                            pv2_act(s - 2)
                        if i4 == 3 and s < 14 and s % 2 == 0:
                            hd = s // 2 + 1
                            if hd % 2 == 0:
                                load_pair(act, hd // 2)
                            prep2_act(hd)
                        if i4 == 3 and s < 14 and s % 2 == 1:
                            prep2v_act(s // 2 + 1)
                    store_o2(act, 3)
            act.wait_ge(ot_stored[(len(outn) - 2) % 2], upto("outst", len(outn) - 2))
            act.wait_ge(ot_stored[(len(outn) - 1) % 2], upto("outst", len(outn) - 1))

        @block.vector
        def _(dve):
            v = nc.vector



            def rope(name, j, off, w):
                dve.wait_ge(scalar_done, upto("kf", name, j))
                dve.wait_ge(tables_loaded, upto("rope"))
                for use_before in tm_before(name, 2 * j + 1):
                    dve.wait_ge(*of("tm", use_before))
                x, y = tm(name, 2 * j, w), tm(name, 2 * j + 1, w)
                v.stream_shuffle(y, x, [(i + 16) % 32 for i in range(32)]).then_inc(vector_done, 1)
                did(vector_done, ("shuf", name, j))
                dve.wait_ge(vector_done, so_far(vector_done))
                v.tensor_tensor(x, x, ROPE[:, 0, off:off + w], ALU.mult).then_inc(vector_done, 1)
                did(vector_done, ("rc1", name, j))
                v.tensor_tensor(y, y, ROPE[:, 1, off:off + w], ALU.mult).then_inc(vector_done, 1)
                did(vector_done, ("rs1", name, j))
                dve.wait_ge(vector_done, so_far(vector_done))
                v.tensor_tensor(x, x, y, ALU.add).then_inc(vector_done, 1)
                did(vector_done, ("kr", name, j), ("tm", (name, 2 * j + 1)))

            def prep_q_dve(b, t):
                dve.wait_ge(scalar_done, upto("qh", b, t))
                x, q, ql = RQ[b % 2][:, t, :], QS[b % 2][0], QS[b % 2][1]
                for half in range(2):
                    own_ = slice(64 * half, 64 * half + 64)
                    for o_ in (slice(0, 64), slice(64, P)):
                        v.tensor_tensor(ql[o_, 2 * t + half, :], x[own_, :], q[own_, 2 * t + half, :].bitcast(F32),
                                            ALU.subtract).then_inc(vector_done, 1)
                        did(vector_done, ("qs", b, t))

            def pv_dve(z):
                b, i = z // 4, z % 4
                dve.wait_ge(scalar_done, upto("ott", z))
                if i == 0 and b >= 2:
                    dve.wait_ge(ot_stored[(b - 2) % 2], upto("ost", "c", b - 2))
                src = PS[:, 6 + z % 2, :].rearrange("p (r e q) -> p e r q", e=2, q=P)
                o_ = OT[b % 2][:, :, i * P:(i + 1) * P]
                v.tensor_tensor(o_[0:64], src[0:64, 0, :, :], OTT[0:64, :, :], ALU.add).then_inc(vector_done, 1)
                did(vector_done, ("ota", z))
                v.tensor_tensor(o_[64:P], src[64:P, 1, :, :], OTT[64:P, :, :], ALU.add).then_inc(vector_done, 1)
                did(vector_done, ("ota", z), ("pvfree", "c", z), ("free", "attc"))
                if i == 3:
                    dve.wait_ge(vector_done, so_far(vector_done))
                    dve.wait_ge(g_loaded[b % 2], upto("gl", b))
                    v.tensor_tensor(OT[b % 2][:, :, :], OT[b % 2][:, :, :], GT[b % 2][:, :, :], ALU.mult).then_inc(vector_done, 1)
                    did(vector_done, ("og", b))

            def prep2_dve(hd):
                b, half = hd % 2, hd % 2
                dve.wait_ge(scalar_done, upto("qh2", hd))
                own_ = slice(64 * half, 64 * half + 64)
                oth = slice(64 - 64 * half, P - 64 * half)
                for o_ in (slice(0, 64), slice(64, P)):
                    v.tensor_tensor(QL2[b][o_, :], RQ2[own_, :], QH2[b][own_, :].bitcast(F32), ALU.subtract).then_inc(vector_done, 1)
                    did(vector_done, ("ql2", hd))
                v.tensor_tensor(KS2[b][oth, :], RK2[own_, :], KS2[b][own_, :].bitcast(F32), ALU.subtract).then_inc(vector_done, 1)
                did(vector_done, ("ql2", hd))

            def prep2v_dve(hd):
                b, half = hd % 2, hd % 2
                dve.wait_ge(scalar_done, upto("vh2", hd))
                v.tensor_tensor(VS2[b][:, :, 64:P], RV2[:, :, 64 * half:64 * half + 64],
                                    VS2[b][:, :, 0:64].bitcast(F32), ALU.subtract).then_inc(vector_done, 1)
                did(vector_done, ("vs2", hd))

            def pv2_dve(z):
                hd, G = z // 2, z % 2
                dve.wait_ge(scalar_done, upto("ott2", z))
                if z % 4 == 0 and hd // 2 >= 2:
                    dve.wait_ge(ot_stored[(hd // 2 - 2) % 2], upto("ost", "f", hd // 2 - 2))
                a_ = slice(0, 64) if hd % 2 == 0 else slice(64, P)
                v.tensor_tensor(OT2[(hd // 2) % 2][a_, G * HALF:(G + 1) * HALF], PS[a_, 6 + z % 2, :], OTT2[a_, :], ALU.add).then_inc(vector_done, 1)
                did(vector_done, ("ota2", z), ("pvfree", "f", z), ("free", "attf"))

            for e in TL:
                kind, name = e["kind"], e["name"]
                part = e.get("part")
                if "vector_done" in counts:
                    dve.wait_ge(vector_done, so_far(vector_done))
                if kind == "small":
                    dve.wait_ge(scalar_done, upto("swh"))
                    dve.wait_ge(scalar_done, upto("smallh"))
                    v.tensor_tensor(SWL[:, :, :].rearrange("p h q -> p (h q)"), bank(name, 0),
                                        SWH[:, :, :].rearrange("p h q -> p (h q)").bitcast(F32), ALU.subtract).then_inc(vector_done, 1)
                    did(vector_done, ("free", name))
                    v.tensor_tensor(CHL[:, :], CHRAW[:, :], CHH[:, :].bitcast(F32), ALU.subtract).then_inc(vector_done, 1)
                    did(vector_done, "small_split")
                elif kind == "adav":
                    vv, n = e["v"], e["n"]
                    for k in range(KT):
                        for x in range(2):
                            w_ = e["ws"][k]
                            dve.wait_ge(raw_loaded[w_ % RSLOTS], upto("raw", w_))
                            c_, acc, raw = CS[:, k, x:x + 1], ada_acc(vv, n, x)[:, :], RAW[:, w_ % RSLOTS, :]
                            if k == 0:
                                v.tensor_scalar(acc, raw, c_, None, ALU.mult).then_inc(vector_done, 1)
                            else:
                                dve.wait_ge(vector_done, upto("ada_acc", vv, n, k - 1, x))
                                v.scalar_tensor_tensor(acc, raw, c_, acc, ALU.mult, ALU.add).then_inc(vector_done, 1)
                            did(vector_done, ("ada_acc", vv, n, k, x), ("rawfree", w_))
                elif kind in ("adac", "adapost"):
                    vv, n = e["v"], e.get("n")
                    if kind == "adapost":
                        name = ("adac", vv, n)
                    dve.wait_ge(products_done, upto("job", name))
                    dve.wait_ge(scalar_done, upto("pc"))
                    ab = cols("ada_b", vv * 8, 8) if vv < 6 else cols("ada_b_2", (vv - 6) * 8, 8)
                    src = bank(name, 0)[:, 0:16].rearrange("p (k c) -> p c k", c=2)
                    ks = slice(0, KT) if n is None else slice(4 * n, 4 * n + 4)
                    for c_ in range(2 if kind == "adac" or n is not None else 1):
                        v.tensor_tensor(MOD[:, vv, c_, ks], src[:, c_, ks], ab[:, ks], ALU.add).then_inc(vector_done, 1)
                        did(vector_done, ("mod", vv), ("free", name))
                    if n == 0:
                        continue
                    dve.wait_ge(vector_done, so_far(vector_done))
                    if vv in (1, 4):
                        l = vv // 3
                        for c_ in range(2):
                            v.scalar_tensor_tensor(CO[:, 2 * l + c_, :], MOD[:, vv, c_, :], 1.0,
                                                       cols("norm_g", l * 8, 8), ALU.add, ALU.mult).then_inc(vector_done, 1)
                            did(vector_done, ("coef", l))
                    if vv == 7:
                        v.scalar_tensor_tensor(CO[:, 4, :], MOD[:, vv, 0, :], 1.0, cols("mix_pre_g_2"),
                                                   ALU.add, ALU.mult).then_inc(vector_done, 1)
                        did(vector_done, ("coefa", 2))
                        dve.wait_ge(vector_done, so_far(vector_done))
                        v.tensor_tensor(CO[:, 4, :], CO[:, 4, :], cols("final_g"), ALU.mult).then_inc(vector_done, 1)
                        did(vector_done, ("coef", 2))
                    if vv == 10:
                        v.scalar_tensor_tensor(CO[:, 5, :], MOD[:, vv, 0, :], 1.0, cols("ffn_pre_g_2"),
                                                   ALU.add, ALU.mult).then_inc(vector_done, 1)
                        did(vector_done, ("coef", 4))
                    if vv == 8:
                        v.tensor_tensor(CO[:, 6, :], MOD[:, 8, 0, :], cols("mix_post_g_2"), ALU.mult).then_inc(vector_done, 1)
                        did(vector_done, ("gate", 3))
                    if vv == 11:
                        v.tensor_tensor(CO[:, 7, :], MOD[:, 11, 0, :], cols("ffn_post_g_2"), ALU.mult).then_inc(vector_done, 1)
                        did(vector_done, ("gate", 5))
                elif kind == "sum":
                    n = e["n"]
                    w = PARTS[part][1]
                    for k in range(1, KT):
                        dve.wait_ge(scalar_done, upto("sq", n, part, k))
                        in1 = tm(name, 0, w) if k == 1 else SUM[:, 0:w]
                        v.tensor_tensor(SUM[:, 0:w], tm(name, k, w), in1, ALU.add).then_inc(vector_done, 1)
                        did(vector_done, ("sum", n, part),
                            ("tm", (name, k)), *([("tm", (name, 0))] if k == 1 else []))
                        dve.wait_ge(vector_done, so_far(vector_done))
                    if n == 2:
                        for k in range(1, KT):
                            dve.wait_ge(scalar_done, upto("sqg", n, part, k))
                            in1 = tm(name, 8, w) if k == 1 else RST[:, 0:w]
                            v.tensor_tensor(RST[:, 0:w], tm(name, 8 + k, w), in1, ALU.add).then_inc(vector_done, 1)
                            did(vector_done, ("sumg", n, part),
                                ("tm", (name, 8 + k)), *([("tm", (name, 8))] if k == 1 else []))
                            dve.wait_ge(vector_done, so_far(vector_done))
                elif kind in ("stat", "statpost"):
                    n = e["n"]
                    w = PARTS[part][1]
                    if n == 2:
                        dve.wait_ge(scalar_done, upto("sq1", n, part))
                        v.reciprocal(SUM[:, 0:w], SUM[:, 0:w]).then_inc(vector_done, 1)
                        did(vector_done, ("r1", n, part))
                        dve.wait_ge(vector_done, so_far(vector_done))
                        for use_before in tm_before(name, 0):
                            dve.wait_ge(*of("tm", use_before))
                        t_ = tm(name, 0, w)
                        v.tensor_tensor(t_, bank(("stat", n, part), 1, w), SUM[:, 0:w], ALU.mult).then_inc(vector_done, 1)
                        did(vector_done, ("free", ("stat", n, part)))
                        dve.wait_ge(vector_done, so_far(vector_done))
                        v.tensor_tensor(t_, t_, SUM[:, 0:w], ALU.mult).then_inc(vector_done, 1)
                        did(vector_done, ("r1sq", n, part))
                        dve.wait_ge(scalar_done, upto("sqrt", n, part))
                        v.reciprocal(RST[:, 0:w], RST[:, 0:w]).then_inc(vector_done, 1)
                        did(vector_done, ("r2", n, part))
                        dve.wait_ge(vector_done, so_far(vector_done))
                        v.tensor_tensor(RST[:, 0:w], RST[:, 0:w], SUM[:, 0:w], ALU.mult).then_inc(vector_done, 1)
                        did(vector_done, ("rstd", n, part))
                    else:
                        dve.wait_ge(scalar_done, upto("sqrt", n, part))
                        r_ = RST0[part] if n == 0 else RST
                        v.reciprocal(r_[:, 0:w], r_[:, 0:w]).then_inc(vector_done, 1)
                        did(vector_done, ("rstd", n, part))
                    dve.wait_ge(vector_done, so_far(vector_done))
                elif kind == "apply":
                    n = e["n"]
                    w = PARTS[part][1]

                    def lo(k):
                        dve.wait_ge(scalar_done, upto("hi", n, part, k))
                        v.tensor_tensor(hs(part, k, 1), tm(name, k, w), hs(part, k, 0).bitcast(F32), ALU.subtract).then_inc(vector_done, 1)
                        did(vector_done, ("H", "apply", n, part, k), ("tm", (name, k)))

                    for k in range(KT):
                        for use_before in tm_before(name, k):
                            dve.wait_ge(*of("tm", use_before))
                        v.tensor_tensor(tm(name, k, w), xs(part, k), (RST0[part] if n == 0 else RST)[:, 0:w], ALU.mult).then_inc(vector_done, 1)
                        did(vector_done, ("t", n, part, k))
                        if k >= 2:
                            lo(k - 2)
                    lo(KT - 2)
                    lo(KT - 1)
                    if n == 2:
                        for k in range(KT):
                            v.scalar_tensor_tensor(xs(part, k), xs(part, k), col("final_g", k), SUM[:, 0:w],
                                                       ALU.mult, ALU.mult).then_inc(vector_done, 1)
                            did(vector_done, ("XW", 2))
                        if part == "h0":
                            v.memset(U[:, :, 0:TAPS - 1], 0.0).then_inc(vector_done, 1)
                            did(vector_done, "upad")
                elif kind in ("lin", "tok", "kv"):
                    layer, group = e["layer"], e["group"]
                    off, w = PARTS[part]
                    if layer == "ab" and group == "xb":
                        dve.wait_ge(products_done, upto("job", name))
                        for g in range(4):
                            dve.wait_ge(scalar_done, upto("vbh", part, g))
                            v.tensor_tensor(VBL[:, g, 0:w], bank(name, g, w), VBH[:, g, 0:w].bitcast(F32), ALU.subtract).then_inc(vector_done, 1)
                            did(vector_done, ("xbs", part), ("free", name))
                    elif layer == "ab" and group == "ga":
                        for j in range(4):
                            dve.wait_ge(scalar_done, upto("gasilu", part, j))
                            dve.wait_ge(scalar_done, upto("u", part))
                            x = xs(part, j)
                            v.tensor_tensor(x, x, tm(name, j, w), ALU.mult).then_inc(vector_done, 1)
                            did(vector_done, ("ug", part), ("tm", (name, j)))
                    elif layer == "ab" and group == "v":
                        dve.wait_ge(products_done, upto("job", name))
                        nt = w // P
                        for tb in range(nt):
                            v.bn_stats(BST[:, tb, :], bank(name, tb)).then_inc(vector_done, 1)
                            did(vector_done, ("bs", part, tb))
                        for tb in range(nt):
                            dve.wait_ge(vector_done, upto("bs", part, tb))
                            v.bn_aggr(MV[:, tb, :], BST[:, tb, :]).then_inc(vector_done, 1)
                            did(vector_done, ("mv", part))
                        dve.wait_ge(scalar_done, upto("vsd", part))
                        v.reciprocal(SM[:, 8:8 + nt], SM[:, 0:nt]).then_inc(vector_done, 1)
                        did(vector_done, ("vr", part))
                        dve.wait_ge(vector_done, so_far(vector_done))
                        for tb in range(nt):
                            for use_before in tm_before(name, tb):
                                dve.wait_ge(*of("tm", use_before))
                            if tb == 0 and part != "h0":
                                dve.wait_ge(products_done, upto("job", ("spat", {"h1": "h0", "c": "h1"}[part])))
                            if tb == 0 and part == "h0":
                                dve.wait_ge(products_done, upto("job", ("chan", "c", 0)))
                            v.tensor_scalar(tm(name, tb), bank(name, tb), MV[:, tb, 0:1], SM[:, 8 + tb:9 + tb],
                                                ALU.subtract, ALU.mult).then_inc(vector_done, 1)
                            did(vector_done, ("vf", part, tb), ("free", name))
                            dve.wait_ge(scalar_done, upto("vh", part, tb))
                            v.tensor_tensor(VBL[:, tb, :], tm(name, tb), VBH[:, tb, :].bitcast(F32), ALU.subtract).then_inc(vector_done, 1)
                            did(vector_done, ("vn", part, tb), ("tm", (name, tb)))
                    elif layer in ("abo", "co"):
                        dve.wait_ge(products_done, upto("job", name))
                        n = 1 if layer == "abo" else 2
                        dve.wait_ge(x_loaded, upto("reload", n - 1))
                        dve.wait_ge(vector_done, upto("mod", 2 if n == 1 else 5))
                        for j in range(4):
                            k = group * 4 + j
                            x = xs(part, k)
                            v.scalar_tensor_tensor(x, bank(name, j, w), mod(2 if n == 1 else 5, part, k), x,
                                                       ALU.mult, ALU.add).then_inc(vector_done, 1)
                            did(vector_done, ("X", n, part, k), ("free", name), ("XW", n))
                    elif layer == "c" and group == "kv":
                        dve.wait_ge(products_done, upto("job", name))
                        per = 1 if part == "c" else 2
                        c0 = T if part == "c" else off
                        for j in range(2):
                            if part != "c":
                                rope(name, j, off, w)
                            src = tm(name, per * j, w)
                            dve.wait_ge(scalar_done, upto("khi", part, j, 1))
                            v.tensor_tensor(KS[64:P, 2 * j, c0:c0 + w], src[0:64, :],
                                                KS[0:64, 2 * j, c0:c0 + w].bitcast(F32), ALU.subtract).then_inc(vector_done, 1)
                            did(vector_done, ("klo", part, j))
                            v.tensor_tensor(KS[0:64, 2 * j + 1, c0:c0 + w], src[64:P, :],
                                                KS[64:P, 2 * j + 1, c0:c0 + w].bitcast(F32), ALU.subtract).then_inc(vector_done, 1)
                            did(vector_done, ("tm", (name, per * j)))
                        for tb in range(0, w // P, 2):
                            b = (8 if part == "c" else off // P) + tb
                            dve.wait_ge(scalar_done, upto("vhi", part, tb))
                            src = bank(name, 2 + tb // 2).rearrange("p (t h d) -> p t h d", d=64, h=4)
                            v.tensor_tensor(VS[:, b:b + 2, :, 64:P], src, VS[:, b:b + 2, :, 0:64].bitcast(F32),
                                                ALU.subtract).then_inc(vector_done, 1)
                            did(vector_done, ("free", name))
                    elif layer == "c" and group[0] == "q":
                        for j in range(4):
                            rope(name, j, off, w)
                    elif layer == "b2" and group == "cg":
                        for j in range(4):
                            dve.wait_ge(scalar_done, upto("gasilu", name, j))
                            dve.wait_ge(scalar_done, upto("uv", part))
                            x = U[:, j, 30 + off:30 + off + w]
                            v.tensor_tensor(x, x, tm(name, j, w), ALU.mult).then_inc(vector_done, 1)
                            did(vector_done, ("ug2", part), ("tm", (name, j)))
                    elif layer == "fi":
                        ch = group
                        for j in range(2):
                            dve.wait_ge(scalar_done, upto("gsl", ch, part, j))
                            v.tensor_tensor(tm(name, j), bank(name, 2 + j), tm(name, j), ALU.mult).then_inc(vector_done, 1)
                            did(vector_done, ("av", ch, part, j), ("free", name))
                        for j in range(2):
                            dve.wait_ge(scalar_done, upto("ahi", ch, part, j))
                            v.tensor_tensor(AHL[:, j, off:off + w], tm(name, j), AHH[:, j, off:off + w].bitcast(F32),
                                                ALU.subtract).then_inc(vector_done, 1)
                            did(vector_done, ("A", ch, part, j), ("tm", (name, j)))
                    elif layer == "fo" and e["ch"] > 0:
                        dve.wait_ge(products_done, upto("job", name))
                        dve.wait_ge(scalar_done, upto("yacc", group, part))
                        y = Y[:, group * 4:group * 4 + 4, off:off + w]
                        if e["ch"] > 1:
                            dve.wait_ge(vector_done, upto("yadd", e["ch"] - 1, group, part))
                        v.tensor_tensor(y, PS[:, 4 * setof[name]:4 * setof[name] + 4, 0:w], y, ALU.add).then_inc(vector_done, 1)
                        did(vector_done, ("yadd", e["ch"], group, part),
                            ("free", name), *[("X", 5, part, group * 4 + j) for j in range(4)])
                elif kind == "spat":
                    dve.wait_ge(products_done, upto("job", name))
                    nt = PARTS[part][1] // P
                    w = nt * P
                    for h in range(4):
                        for use_before in tm_before(name, h):
                            dve.wait_ge(*of("tm", use_before))
                        t_ = tm(name, h, w).rearrange("p (t q) -> p t q", q=P)
                        src = bank(name, h, w).rearrange("p (t q) -> p t q", q=P)
                        sb = SBB[:, h:h + 1, :].broadcast_to([P, nt, P])
                        v.scalar_tensor_tensor(t_, src, col("v_norm_g", h), sb, ALU.mult, ALU.add).then_inc(vector_done, 1)
                        did(vector_done, ("free", name), ("sv", part, h))
                        dve.wait_ge(vector_done, so_far(vector_done))
                        x = xs(part, h)
                        v.tensor_tensor(x, x, tm(name, h, w), ALU.mult).then_inc(vector_done, 1)
                        did(vector_done, ("ya", part), ("tm", (name, h)))
                elif kind == "abload":
                    a_ = e["a"]
                    for x in range(2):
                        dve.wait_ge(ab_loaded[x], upto("abl", a_, x))
                        dve.wait_ge(products_done, upto("job", ("gb", "c" if a_ == "c" else "h1")))
                    if a_ == "c":
                        for x in range(2):
                            dve.wait_ge(scalar_done, upto("abh", a_, x))
                            hh, hl = (t_[:, :, :].rearrange("p k c -> p (k c)")[:, x * D:(x + 1) * D] for t_ in (HCH, HCL))
                            v.tensor_tensor(hl, ARAW[:, x, :], hh.bitcast(F32), ALU.subtract).then_inc(vector_done, 1)
                            did(vector_done, ("AB", "c"))
                    else:
                        for x, op in enumerate((ALU.add, ALU.subtract)):
                            if a_ == 0:
                                dve.wait_ge(products_done, upto("job", ("spat", "c")))
                            v.tensor_tensor(ASD[:, x, :], ARAW[:, 0, :], ARAW[:, 1, :], op).then_inc(vector_done, 1)
                            did(vector_done, ("abs", a_, x))
                        for x in range(2):
                            dve.wait_ge(scalar_done, upto("abh", a_, x))
                            v.tensor_tensor(HXL[:, a_ + 4 * x, :], ASD[:, x, :], HXH[:, a_ + 4 * x, :].bitcast(F32),
                                                ALU.subtract).then_inc(vector_done, 1)
                            did(vector_done, ("AB", a_ + 4 * x), ("abr", a_))
                        dve.wait_ge(vector_done, so_far(vector_done))
                elif kind == "dft":
                    dve.wait_ge(products_done, upto("job", name))
                    dve.wait_ge(scalar_done, upto("gb", "h0"))
                    dve.wait_ge(scalar_done, upto("gb", "h1"))
                    y = XX[:, 4:8, e["odd"]:T:2]
                    v.tensor_tensor(y, PS[:, 4 * setof[name]:4 * setof[name] + 4, :], y, ALU.mult).then_inc(vector_done, 1)
                    did(vector_done, ("yb", e["odd"]), ("free", name))
                elif kind == "dftc":
                    dve.wait_ge(products_done, upto("job", name))
                    dve.wait_ge(scalar_done, upto("gb", "c"))
                    y = XC[:, 4:8, :]
                    v.tensor_tensor(y, PS[:, 4 * setof[name]:4 * setof[name] + 4, 0:C], y, ALU.mult).then_inc(vector_done, 1)
                    did(vector_done, ("yb", "c"), ("free", name))
                elif kind == "ysplit":
                    for k in range(KT):
                        dve.wait_ge(scalar_done, upto("yh", part, k))
                        v.tensor_tensor(hs(part, k, 1), xs(part, k), hs(part, k, 0).bitcast(F32), ALU.subtract).then_inc(vector_done, 1)
                        did(vector_done, ("H", "ysplit", 0, part, k))
                elif kind == "hload":
                    n = e["n"]
                    b = 0 if part == "h0" else 1
                    for k in range(KT):
                        dve.wait_ge(scalar_done, upto("lh", n, part, k))
                        v.tensor_tensor(hs(part, k, 1), LR[b][:, k, :], hs(part, k, 0).bitcast(F32), ALU.subtract).then_inc(vector_done, 1)
                        did(vector_done, ("H", "hload", n, part, k))
                elif kind == "resid":
                    n = e["n"]
                    off, w = PARTS[part]
                    dve.wait_ge(vector_done, upto("gate", n))
                    dve.wait_ge(x_loaded, upto("reload", 2))
                    def scaled(k):
                        for use_before in tm_before(name, k):
                            dve.wait_ge(*of("tm", use_before))
                        v.tensor_tensor(tm(name, k), ys(part, k), RST[:, :], ALU.mult).then_inc(vector_done, 1)
                        did(vector_done, ("rt", n, part, k))

                    scaled(0)
                    for k in range(KT):
                        if k + 1 < KT:
                            scaled(k + 1)
                        x = xs(part, k)
                        dve.wait_ge(vector_done, upto("rt", n, part, k))
                        v.scalar_tensor_tensor(x, tm(name, k), CO[:, 6 if n == 3 else 7, k:k + 1], x, ALU.mult, ALU.add).then_inc(vector_done, 1)
                        did(vector_done, ("X", 4, part, k) if n == 3 else ("xfin", part, k), ("tm", (name, k)))
                elif kind == "conv":
                    i = e["i"]
                    if i == -1:
                        dve.wait_ge(vector_done, upto("ug2", "h0"))
                        dve.wait_ge(vector_done, upto("upad"))
                        dve.wait_ge(spilled, upto("spill", 2))
                        taps = [(j, t_, 0) for t_ in range(EARLY_TAPS) for j in range(2)]
                    else:
                        if i == 0:
                            dve.wait_ge(vector_done, upto("ug2", "h1"))
                        taps = [(j, t_, x) for t_ in range(EARLY_TAPS) for j, x in ((0, 1), (1, 1), (2, None))]
                        taps += [(j, t_, None) for t_ in range(EARLY_TAPS, TAPS) for j in range(3)]
                        per = -(-len(taps) // 5)
                        taps = taps[i * per:(i + 1) * per]
                    for j, t_, half in taps:
                        wc = PC[:, 256 + 4 * t_ + j:257 + 4 * t_ + j]
                        o_, w_ = (0, T) if half is None else (half * HALF, HALF)
                        src, dst = U[:, j, o_ + t_:o_ + t_ + w_], CA[:, j, o_:o_ + w_]
                        if t_ == 0:
                            v.tensor_scalar(dst, src, wc, col("conv_b_2", j), ALU.mult,
                                            ALU.add).then_inc(vector_done, 1)
                        else:
                            dve.wait_ge(*of("conv", j, t_ - 1, 0 if half == 0 else 1))
                            v.scalar_tensor_tensor(dst, src, wc, dst, ALU.mult, ALU.add).then_inc(vector_done, 1)
                        did(vector_done, *[("conv", j, t_, x) for x in ((0, 1) if half is None else (half,))])
                elif kind == "csum":
                    for j in range(1, 4):
                        dve.wait_ge(vector_done, so_far(vector_done))
                        if j == 3:
                            dve.wait_ge(gpsimd_done, upto("conv", 3, TAPS - 1, 1))
                        v.tensor_tensor(CSUM[:, :], CA[:, j, :], CA[:, 0, :] if j == 1 else CSUM[:, :],
                                        ALU.add).then_inc(vector_done, 1)
                        did(vector_done, "cmean_sum")
                elif kind == "flog":
                    dve.wait_ge(products_done, upto("job", name))
                    dve.wait_ge(vector_done, so_far(vector_done))
                    FA, FB, FC = (x[0:8, :] for x in FL)
                    dve.wait_ge(rows_loaded, upto("rows"))
                    src = PS[0:8, 4 * setof[name]:4 * setof[name] + 2, :].rearrange("p b n -> p (b n)")
                    v.tensor_scalar(FA, src, SM[0:8, 48:49], None, ALU.add).then_inc(vector_done, 1)
                    did(vector_done, "fz", ("free", name))
                    dve.wait_ge(vector_done, so_far(vector_done))
                    v.tensor_scalar(FC, FA, 0.0, None, ALU.min).then_inc(vector_done, 1)
                    did(vector_done, "fmin")
                    dve.wait_ge(scalar_done, upto("fln"))
                    v.tensor_tensor(FC, FC, FB, ALU.subtract).then_inc(vector_done, 1)
                    did(vector_done, "logf")
                    v.memset(FA, 1.0).then_inc(vector_done, 1)
                    did(vector_done, "f1")
                    dve.wait_ge(vector_done, so_far(vector_done))
                    v.tensor_tensor_scan(FB, FA, FC, 0.0, ALU.mult, ALU.add).then_inc(vector_done, 1)
                    did(vector_done, "cum")
                elif kind == "cmean":
                    dve.wait_ge(scalar_done, upto("cmu"))
                    for j in range(4):
                        v.tensor_tensor(CA[:, j, :], CA[:, j, :], CRST[:, :], ALU.subtract).then_inc(vector_done, 1)
                        did(vector_done, ("cc", j))
                    for j in range(1, 4):
                        dve.wait_ge(scalar_done, upto("csq", j))
                        if j > 1:
                            dve.wait_ge(vector_done, upto("csqr", j - 1))
                        v.tensor_tensor(CSUM[:, :], CSQ[j % 2][:, :], CSQ[0][:, :] if j == 1 else CSUM[:, :],
                                        ALU.add).then_inc(vector_done, 1)
                        did(vector_done, "cvar_sum", ("csqr", j))
                elif kind == "cvar":
                    dve.wait_ge(scalar_done, upto("csd"))
                    v.reciprocal(CRST[:, :], CRST[:, :]).then_inc(vector_done, 1)
                    did(vector_done, "crs")
                    dve.wait_ge(vector_done, so_far(vector_done))
                    for j in range(4):
                        v.tensor_tensor(CA[:, j, :], CA[:, j, :], CRST[:, :], ALU.mult).then_inc(vector_done, 1)
                        did(vector_done, ("cn", j))
                elif kind == "attc_pre":
                    dve.wait_ge(late_loaded, upto("sinkm"))
                    v.tensor_scalar(NSK[:, :], SINK[:, :], -1.0, None, ALU.mult).then_inc(vector_done, 1)
                    did(vector_done, "nsk")
                elif kind == "attc":
                    prep_q_dve(0, 0)
                    prep_q_dve(0, 1)
                    tiles = spread("c")
                    for u in range(4 * 33 + 4):
                        s, h = u // 4, u % 4
                        if 1 <= u <= 128:
                            y, b, hh = u - 1, (u - 1) // 4 % 2, (u - 1) % 4
                            dve.wait_ge(scalar_done, upto("exp", "c", y))
                            if y >= 8:
                                dve.wait_ge(gpsimd_done, upto("P", "c", y // 4 - 2, hh))
                            v.reciprocal(RC[b][:, hh:hh + 1], SU[b][:, hh:hh + 1]).then_inc(vector_done, 1)
                            did(vector_done, ("rc", "c", y))
                        if s < 32:
                            i = s % 8
                            lo_ = 256 if i in (0, 7) else 128
                            src = PS[:, 2 * (u % 2):2 * (u % 2) + 2, :].rearrange("p b n -> p (b n)")[:, lo_:769]
                            dve.wait_ge(products_done, upto("sc", "c", u))
                            v.tensor_reduce(MX[s % 2][:, h:h + 1], src, AX.X, ALU.min).then_inc(vector_done, 1)
                            did(vector_done, ("mx", "c", u))
                        for z, ti in tiles.get(u, []):
                            tb = tcount(z, "c") + ti
                            dve.wait_ge(scalar_done, upto("pth", "c", tb))
                            p_ = key_blocks(z)[ti]
                            v.tensor_tensor(PTL[:, p_, :], PS[:, 4 + tb % 2, :], PTH[:, p_, :].bitcast(F32),
                                            ALU.subtract).then_inc(vector_done, 1)
                            did(vector_done, ("ptl", "c", tb))
                        if h == 3 and s >= 2:
                            pv_dve(s - 2)
                        if h == 0 and s < 32 and (s - 1) % 4 in (1, 2) and s // 4 + 1 < 8:
                            prep_q_dve(s // 4 + 1, (s - 1) % 4 - 1)
                elif kind == "attf_pre":
                    prep2_dve(0)
                    prep2v_dve(0)
                elif kind == "attf":
                    tiles = spread("f")
                    for u in range(4 * 17 + 4):
                        s, i4 = u // 4, u % 4
                        if 1 <= u <= 64:
                            y, b, hh = u - 1, (u - 1) // 4 % 2, (u - 1) % 4
                            dve.wait_ge(scalar_done, upto("exp", "f", y))
                            if y >= 8:
                                dve.wait_ge(gpsimd_done, upto("P", "f", y // 4 - 2, hh))
                            v.reciprocal(RC[b][:, hh:hh + 1], SU[b][:, hh:hh + 1]).then_inc(vector_done, 1)
                            did(vector_done, ("rc", "f", y))
                        if s < 16:
                            hd = s // 2
                            n = (4 * (s % 2) + i4 + 1) * P
                            src = PS[:, 2 * (u % 2):2 * (u % 2) + 2, :].rearrange("p b n -> p (b n)")[:, 0:n]
                            dve.wait_ge(products_done, upto("sc", "f", u))
                            dve.wait_ge(nb_loaded[hd % 2], upto("nbl", hd))
                            if s >= 2:
                                dve.wait_ge(products_done, upto("tr", "f", tcount(s - 1, "f") - 1))
                            v.tensor_tensor_reduce(out=PB2[s % 2][:, i4, 0:n], in0=src, in1=NBC[hd % 2][:, 0:n],
                                                   scale=1.0, scalar=3e38, op0=ALU.add, op1=ALU.min,
                                                   accum_out=MX[s % 2][:, i4:i4 + 1]).then_inc(vector_done, 1)
                            did(vector_done, ("mx", "f", u))
                        for z, j in tiles.get(u, []):
                            tb = tcount(z, "f") + j
                            c0 = max(0, j - 4 * (z % 2)) * P
                            dve.wait_ge(scalar_done, upto("pth", "f", tb))
                            v.tensor_tensor(PT2L[:, j, c0:HALF], PS[:, 4 + tb % 2, c0:HALF],
                                            PT2H[:, j, c0:HALF].bitcast(F32), ALU.subtract).then_inc(vector_done, 1)
                            did(vector_done, ("ptl", "f", tb))
                        if i4 == 3 and s >= 2:
                            pv2_dve(s - 2)
                        if i4 == 0 and s < 15 and s % 2 == 1:
                            prep2_dve(s // 2 + 1)
                        if i4 == 0 and 2 <= s < 15 and s % 2 == 0:
                            prep2v_dve(s // 2)
    return nc


INPUTS = ["x", "c", "ctx", "c_ctx", "norm_g", "ada_w", "ada_b", "w_in_ab", "v_norm_g", "spatial_w", "spatial_b",
          "w_out_ab", "w_in_c", "sink_logit", "w_out_c", "final_g", "c_2", "w_in_2", "b_f_2", "conv_w_2", "conv_b_2",
          "conv_ln_g_2", "conv_ln_b_2", "w_o_2", "w_ffn_in_2", "w_ffn_out_2", "mix_pre_g_2", "mix_post_g_2",
          "ffn_pre_g_2", "ffn_post_g_2", "ada_w_2", "ada_b_2"]


def build(nc, arrays, old):
    a = {n[3:]: nc.dram_tensor(n, x.shape, mybir.dt.from_np(x.dtype), kind="ExternalInput").ap()
         for n, x in arrays.items()}
    a["out"] = nc.dram_tensor("out_y", (1, T, D), F32, kind="ExternalOutput").ap()
    marks = {}
    program(nc, a, marks, old)
    return marks


def kernel(**inputs):
    import concourse.bacc as bacc
    from concourse.bass_utils import run_bass_kernel_spmd

    arrays = {f"in_{n}": np.ascontiguousarray(inputs[n]) for n in INPUTS}
    arrays.update({f"in_{n}": x for n, x in shape_tables().items()})
    counted = build(bacc.Bacc("TRN2", target_bir_lowering=False, num_devices=1), arrays, {})
    nc = bacc.Bacc("TRN2", target_bir_lowering=False, num_devices=1)
    build(nc, arrays, counted)
    r = run_bass_kernel_spmd(nc, [arrays], core_ids=[0])
    return r.results[0]["out_y"]
```
